# Optimizing a Trainium2 kernel written in Bass

```python
import math
import jax, jax.numpy as jnp
from jax import lax
import numpy as np

D_MODEL = 1024
BATCH = 1
SEQ = 256
DEPTH = 2
DEC_BATCH = 8
DEC_SEQ = 8
PAST_LEN = 2048
PAGE_SIZE = 128

HEAD_DIM = 64
D_MIX = D_MODEL
GROUP_W = D_MIX // 4
N_GROUP_HEADS = GROUP_W // HEAD_DIM

A_HEADS = N_GROUP_HEADS
A_PATTERNS = ((128, 1), (512, 4), (2048, 16))
A_WIN_MAX = 2048
A_BLOCK = 128
ROPE_DIM = HEAD_DIM // 4
ROPE_THETA = 500000.0

B_HEADS = N_GROUP_HEADS
B_DK = HEAD_DIM // 2
B_DV = HEAD_DIM
GLA_RANK = 16
GLA_TAU = 16.0
GLA_CHUNK = 64

C_HEADS = N_GROUP_HEADS
SB_BLOCK = 128
SB_BIAS_INIT = -8.0

D_HEADS = N_GROUP_HEADS
D_HEADDIM = HEAD_DIM
D_INNER = D_HEADS * D_HEADDIM
D_GROUPS = 2
D_STATE = 64
CONV_W = 4
CONV_CH = D_INNER + 2 * D_GROUPS * D_STATE
SSD_CHUNK = 64
DT_MIN = 0.001
DT_MAX = 0.1

N_EXP_GROUPS = 4
EXP_PER_GROUP = 8
N_EXPERTS = N_EXP_GROUPS * EXP_PER_GROUP
TOP_K = 2
D_EXPERT = 512
MOE_BLOCK = 128

NORM_EPS = 1e-6

IN_SIZES = (A_HEADS * HEAD_DIM, A_HEADS * HEAD_DIM, A_HEADS * HEAD_DIM,
            B_HEADS * B_DK, B_HEADS * B_DK, B_HEADS * B_DV, GLA_RANK, B_HEADS * B_DV,
            C_HEADS * HEAD_DIM, C_HEADS * HEAD_DIM, C_HEADS * HEAD_DIM,
            D_INNER, CONV_CH, D_HEADS)
N_IN = sum(IN_SIZES)

kernel_name = 'hybrid_parallel_heads_decoder_step'

def rmsnorm(x, g):
    xf = x.astype(jnp.float32)
    y = xf * lax.rsqrt(jnp.mean(xf * xf, axis=-1, keepdims=True) + NORM_EPS)
    return (y * g.astype(jnp.float32)).astype(x.dtype)

def rope_partial(x, pos):
    half = ROPE_DIM // 2
    inv_freq = jnp.exp(-math.log(ROPE_THETA) * jnp.arange(half, dtype=jnp.float32) * (2.0 / ROPE_DIM))
    ang = pos.astype(jnp.float32)[:, None] * inv_freq[None, :]
    cos = jnp.cos(ang)[None, :, None, :].astype(x.dtype)
    sin = jnp.sin(ang)[None, :, None, :].astype(x.dtype)
    x1, x2, rest = x[..., :half], x[..., half:ROPE_DIM], x[..., ROPE_DIM:]
    return jnp.concatenate([x1 * cos - x2 * sin, x2 * cos + x1 * sin, rest], axis=-1)

def dilated_band_attn(q, k, v, dil, n_back):
    b, s, h, d = q.shape
    ls = s // dil
    lp = -(-ls // A_BLOCK) * A_BLOCK
    nb = lp // A_BLOCK

    def sub(t):
        t = t.reshape(b, ls, dil, h, d).transpose(0, 2, 1, 3, 4).reshape(b * dil, ls, h, d)
        t = jnp.pad(t, ((0, 0), (0, lp - ls), (0, 0), (0, 0)))
        return t.reshape(b * dil, nb, A_BLOCK, h, d)

    def with_prev(t):
        prev = jnp.pad(t[:, :-1], ((0, 0), (1, 0), (0, 0), (0, 0), (0, 0)))
        return jnp.concatenate([prev, t], axis=2)

    qb = sub(q)
    k2, v2 = with_prev(sub(k)), with_prev(sub(v))
    scores = jnp.einsum('bnqhd,bnkhd->bnhqk', qb, k2).astype(jnp.float32) * (d ** -0.5)
    qi = jnp.arange(A_BLOCK) + A_BLOCK
    ki = jnp.arange(2 * A_BLOCK)
    dist = qi[:, None] - ki[None, :]
    band = (dist >= 0) & (dist <= n_back)
    has_prev = (jnp.arange(nb)[:, None] > 0) | (ki[None, :] >= A_BLOCK)
    mask = band[None, :, :] & has_prev[:, None, :]
    scores = jnp.where(mask[None, :, None], scores, -jnp.inf)
    lse = jax.nn.logsumexp(scores, axis=-1)
    p = jnp.exp(scores - lse[..., None])
    o = jnp.einsum('bnhqk,bnkhd->bnqhd', p.astype(v.dtype), v2)
    o = o.reshape(b, dil, lp, h, d)[:, :, :ls].transpose(0, 2, 1, 3, 4).reshape(b, s, h, d)
    lse = lse.transpose(0, 1, 3, 2).reshape(b, dil, lp, h)[:, :, :ls].transpose(0, 2, 1, 3).reshape(b, s, h)
    return o, lse

def dilated_gather_attn(q, k_all, v_all, q_local0, dil, n_back):
    l = q.shape[1]
    qloc = q_local0 + jnp.arange(l)
    idx = qloc[:, None] - jnp.arange(n_back + 1)[None, :] * dil
    valid = idx >= 0
    idx = jnp.maximum(idx, 0)
    kg, vg = k_all[:, idx], v_all[:, idx]
    s = jnp.einsum('blhd,bljhd->blhj', q, kg).astype(jnp.float32) * (q.shape[-1] ** -0.5)
    s = jnp.where(valid[None, :, None, :], s, -jnp.inf)
    lse = jax.nn.logsumexp(s, axis=-1)
    p = jnp.exp(s - lse[..., None])
    return jnp.einsum('blhj,bljhd->blhd', p.astype(v_all.dtype), vg), lse

def merge_by_denominator(branches):
    lse = jnp.stack([l for _, l in branches])
    w = jax.nn.softmax(lse, axis=0)[..., None]
    o = jnp.stack([o.astype(jnp.float32) for o, _ in branches])
    return jnp.sum(w * o, axis=0).astype(branches[0][0].dtype)

def stick_breaking(q, k, v, q_pos0, bias):
    z = jnp.einsum('bqhd,bkhd->bhqk', q, k).astype(jnp.float32) * (q.shape[-1] ** -0.5)
    z = z + bias.astype(jnp.float32)[None, :, None, None]
    qpos = q_pos0 + jnp.arange(q.shape[1])
    strict = jnp.arange(k.shape[1])[None, :] < qpos[:, None]
    log_keep = jnp.where(strict, jax.nn.log_sigmoid(-z), 0.0)
    after = lax.cumsum(log_keep, axis=3, reverse=True) - log_keep
    a = jnp.where(strict, jnp.exp(jax.nn.log_sigmoid(z) + after), 0.0)
    return jnp.einsum('bhqk,bkhd->bqhd', a.astype(v.dtype), v)

def stick_breaking_prompt(q, k, v, bias):
    b, s, h, d = q.shape
    nb = s // SB_BLOCK
    qb = q.reshape(b, nb, SB_BLOCK, h, d).transpose(1, 0, 2, 3, 4)
    o = lax.map(lambda args: stick_breaking(args[1], k, v, args[0] * SB_BLOCK, bias), (jnp.arange(nb), qb))
    return o.transpose(1, 0, 2, 3, 4).reshape(b, s, h, d)

def _to_chunks(t, c):
    b, l = t.shape[:2]
    lp = -(-l // c) * c
    t = jnp.pad(t, [(0, 0), (0, lp - l)] + [(0, 0)] * (t.ndim - 2))
    return jnp.swapaxes(t.reshape((b, lp // c, c) + t.shape[2:]), 0, 1)

def gla_chunked(q, k, v, log_a, s0):
    b, l, h, _ = q.shape
    c = min(GLA_CHUNK, l)
    f = lambda t: _to_chunks(t.astype(jnp.float32), c)
    causal = jnp.tril(jnp.ones((c, c), bool))

    def step(s, inp):
        qc, kc, vc, lc = inp
        cum = jnp.cumsum(lc, axis=1)
        last = cum[:, -1]
        qg = qc * jnp.exp(cum)
        kg = kc * jnp.exp(-cum)
        att = jnp.where(causal[None, None], jnp.einsum('bthk,bshk->bhts', qg, kg), 0.0)
        o = jnp.einsum('bthk,bhkv->bthv', qg, s) + jnp.einsum('bhts,bshv->bthv', att, vc)
        s = jnp.exp(last)[..., None] * s + jnp.einsum('bshk,bshv->bhkv', kc * jnp.exp(last[:, None] - cum), vc)
        return s, o

    s, o = lax.scan(step, s0.astype(jnp.float32), (f(q), f(k), f(v), f(log_a)))
    o = jnp.swapaxes(o, 0, 1)
    o = o.reshape((b, -1) + o.shape[3:])[:, :l]
    return o, s

def ssd_chunked(x, dt, a, bm, cm, s0):
    b, l, h, _ = x.shape
    rep = h // bm.shape[2]
    bh = jnp.repeat(bm, rep, axis=2)
    ch = jnp.repeat(cm, rep, axis=2)
    c = min(SSD_CHUNK, l)
    f = lambda t: _to_chunks(t.astype(jnp.float32), c)
    xdt = x.astype(jnp.float32) * dt[..., None]
    da = dt * a
    causal = jnp.tril(jnp.ones((c, c), bool))

    def step(s, inp):
        xc, ac, bc, cc = inp
        cum = jnp.cumsum(ac, axis=1)
        seg = cum[:, :, None, :] - cum[:, None, :, :]
        decay = jnp.exp(jnp.where(causal[None, :, :, None], seg, -jnp.inf))
        scores = jnp.einsum('bthn,bshn->btsh', cc, bc) * decay
        y = jnp.einsum('btsh,bshp->bthp', scores, xc) + jnp.einsum('bthn,bhpn->bthp', cc, s) * jnp.exp(cum)[..., None]
        last = cum[:, -1]
        w = jnp.exp(last[:, None] - cum)
        s = jnp.exp(last)[:, :, None, None] * s + jnp.einsum('bshn,bshp->bhpn', bc * w[..., None], xc)
        return s, y

    s, y = lax.scan(step, s0.astype(jnp.float32), (f(xdt), f(da), f(bh), f(ch)))
    y = jnp.swapaxes(y, 0, 1)
    y = y.reshape((b, -1) + y.shape[3:])[:, :l]
    return y, s

def causal_dwconv(x, prev, w, bias):
    xp = jnp.concatenate([prev.astype(x.dtype), x], axis=1)
    y = lax.conv_general_dilated(xp, w[:, None, :].astype(x.dtype), window_strides=(1,), padding='VALID',
                                 dimension_numbers=('NWC', 'WIO', 'NWC'), feature_group_count=x.shape[-1])
    return y + bias, xp[:, xp.shape[1] - (CONV_W - 1):]

def hier_moe(h, w_rg, b_rg, w_re, b_re, w_gate, w_up, w_down):
    b, l, d = h.shape
    t = b * l
    xf = h.reshape(t, d)
    g_logits = (xf @ w_rg + b_rg).astype(jnp.float32)
    g_sel = jnp.argmax(g_logits, axis=-1)
    g_prob = jnp.take_along_axis(jax.nn.softmax(g_logits, axis=-1), g_sel[:, None], axis=-1)
    e_logits = (xf @ w_re + b_re).astype(jnp.float32).reshape(t, N_EXP_GROUPS, EXP_PER_GROUP)
    e_logits = jnp.take_along_axis(e_logits, g_sel[:, None, None], axis=1)[:, 0]
    top_v, top_i = lax.top_k(e_logits, TOP_K)
    gate = g_prob * jax.nn.softmax(top_v, axis=-1)
    expert = g_sel[:, None] * EXP_PER_GROUP + top_i
    n_slots = t * TOP_K
    e_flat = expert.reshape(n_slots)
    order = jnp.argsort(e_flat)
    e_s = e_flat[order]
    tok_s = order // TOP_K
    gate_s = gate.reshape(n_slots)[order]
    counts = jnp.zeros((N_EXPERTS,), jnp.int32).at[e_flat].add(1)
    starts = jnp.cumsum(counts) - counts
    padded = (counts + MOE_BLOCK - 1) // MOE_BLOCK * MOE_BLOCK
    pad_end = jnp.cumsum(padded)
    dest = (pad_end - padded)[e_s] + jnp.arange(n_slots) - starts[e_s]
    n_blocks = -(-n_slots // MOE_BLOCK) + N_EXPERTS
    rows = jnp.zeros((n_blocks * MOE_BLOCK, d), h.dtype).at[dest].set(xf[tok_s])
    block_expert = jnp.minimum(jnp.searchsorted(pad_end, jnp.arange(n_blocks) * MOE_BLOCK, side='right'), N_EXPERTS - 1)

    def expert_ffn(args):
        xb, e = args
        return (jax.nn.silu(xb @ w_gate[e]) * (xb @ w_up[e])) @ w_down[e]

    out = lax.map(expert_ffn, (rows.reshape(n_blocks, MOE_BLOCK, d), block_expert)).reshape(-1, d)
    y = jnp.zeros((t, d), jnp.float32).at[tok_s].add(out[dest].astype(jnp.float32) * gate_s[:, None])
    return y.astype(h.dtype).reshape(b, l, d)

def token_mixing(h, pos, p, cache):
    b, l, _ = h.shape
    split_at = np.cumsum(IN_SIZES)[:-1].tolist()
    (aq, ak, av, bq, bk, bv, b_lr, b_gate, cq, ck, cv, d_z, d_xbc, d_dt) = jnp.split(h @ p['w_in'], split_at, axis=-1)
    heads = lambda t, n: t.reshape(b, l, n, -1)

    aq = rope_partial(heads(aq, A_HEADS), pos)
    ak = rope_partial(heads(ak, A_HEADS), pos)
    av = heads(av, A_HEADS)
    if cache is None:
        branches = [dilated_band_attn(aq, ak, av, dil, win // dil) for win, dil in A_PATTERNS]
        keep = min(A_WIN_MAX, l)
        new_win_k, new_win_v = ak[:, l - keep:], av[:, l - keep:]
    else:
        win_k, win_v = cache[0], cache[1]
        k_all = jnp.concatenate([win_k.astype(ak.dtype), ak], axis=1)
        v_all = jnp.concatenate([win_v.astype(av.dtype), av], axis=1)
        branches = [dilated_gather_attn(aq, k_all, v_all, win_k.shape[1], dil, win // dil) for win, dil in A_PATTERNS]
        new_win_k, new_win_v = ak, av
    o_a = merge_by_denominator(branches).reshape(b, l, GROUP_W)

    log_a = jax.nn.log_sigmoid((b_lr @ p['w_gla_a2'] + p['b_gla_a']).astype(jnp.float32)) / GLA_TAU
    s0_gla = jnp.zeros((b, B_HEADS, B_DK, B_DV), jnp.float32) if cache is None else cache[4]
    o_b, gla_state = gla_chunked(heads(bq, B_HEADS) * (B_DK ** -0.5), heads(bk, B_HEADS), heads(bv, B_HEADS),
                                 heads(log_a, B_HEADS), s0_gla)
    o_b = rmsnorm(o_b, p['g_gla']).astype(h.dtype).reshape(b, l, GROUP_W) * jax.nn.silu(b_gate)

    cq, ck, cv = heads(cq, C_HEADS), heads(ck, C_HEADS), heads(cv, C_HEADS)
    if cache is None:
        o_c = stick_breaking_prompt(cq, ck, cv, p['b_sb'])
        new_sb_k = ck.reshape(b, l // PAGE_SIZE, PAGE_SIZE, C_HEADS, HEAD_DIM)
        new_sb_v = cv.reshape(b, l // PAGE_SIZE, PAGE_SIZE, C_HEADS, HEAD_DIM)
    else:
        k_all = jnp.concatenate([cache[2].astype(ck.dtype), ck], axis=1)
        v_all = jnp.concatenate([cache[3].astype(cv.dtype), cv], axis=1)
        o_c = stick_breaking(cq, k_all, v_all, cache[2].shape[1], p['b_sb'])
        new_sb_k, new_sb_v = ck, cv
    o_c = o_c.reshape(b, l, GROUP_W)

    conv_prev = jnp.zeros((b, CONV_W - 1, CONV_CH), h.dtype) if cache is None else cache[6]
    xbc, conv_state = causal_dwconv(d_xbc, conv_prev, p['w_conv'], p['b_conv'])
    xbc = jax.nn.silu(xbc)
    xs, bm, cm = jnp.split(xbc, [D_INNER, D_INNER + D_GROUPS * D_STATE], axis=-1)
    xs = heads(xs, D_HEADS)
    dt = jax.nn.softplus((d_dt + p['dt_bias']).astype(jnp.float32))
    a = -jnp.exp(p['a_log'].astype(jnp.float32))
    s0_ssm = jnp.zeros((b, D_HEADS, D_HEADDIM, D_STATE), jnp.float32) if cache is None else cache[5]
    y, ssm_state = ssd_chunked(xs, dt, a, heads(bm, D_GROUPS), heads(cm, D_GROUPS), s0_ssm)
    y = y + p['d_skip'].astype(jnp.float32)[:, None] * xs.astype(jnp.float32)
    y = y.reshape(b, l, D_INNER) * jax.nn.silu(d_z.astype(jnp.float32))
    o_d = rmsnorm(y, p['g_ssm']).astype(h.dtype)

    mixed = jnp.concatenate([o_a, o_b, o_c, o_d.astype(o_a.dtype)], axis=-1) @ p['w_out']
    new_state = (new_win_k, new_win_v, new_sb_k, new_sb_v,
                 gla_state.astype(h.dtype), ssm_state.astype(h.dtype), conv_state)
    return mixed, new_state

def block(x, c, pos, p, cache):
    mod = (jax.nn.silu(c) @ p['w_ada'] + p['b_ada'])[:, None, :]
    shift1, scale1, gate1, shift2, scale2, gate2 = jnp.split(mod, 6, axis=-1)
    h = rmsnorm(x, p['g_norm1']) * (1.0 + scale1) + shift1
    mixed, new_state = token_mixing(h, pos, p, cache)
    x = x + gate1 * mixed
    h = rmsnorm(x, p['g_norm2']) * (1.0 + scale2) + shift2
    x = x + gate2 * hier_moe(h, p['w_router_grp'], p['b_router_grp'], p['w_router_exp'], p['b_router_exp'],
                             p['w_exp_gate'], p['w_exp_up'], p['w_exp_down'])
    return x, new_state

def setup_inputs(seed: int = 0) -> dict:
    key = jax.random.key(seed)
    ks = iter(list(jax.random.split(key, 48)))
    nrm = lambda shape, scale=1.0: scale * jax.random.normal(next(ks), shape, jnp.float32)
    n_pages = PAST_LEN // PAGE_SIZE
    n_pool = (DEC_BATCH * n_pages * 5) // 4
    win_len = min(A_WIN_MAX, PAST_LEN)
    page_table = jax.random.permutation(next(ks), n_pool)[: DEC_BATCH * n_pages].reshape(DEC_BATCH, n_pages).astype(jnp.int32)
    dt0 = jnp.exp(jax.random.uniform(next(ks), (DEPTH, D_HEADS), jnp.float32, math.log(DT_MIN), math.log(DT_MAX)))
    dt_bias = dt0 + jnp.log(-jnp.expm1(-dt0))
    a_log = jnp.log(jax.random.uniform(next(ks), (DEPTH, D_HEADS), jnp.float32, 1.0, 16.0))
    return {
        'x_prompt': nrm((BATCH, SEQ, D_MODEL)),
        'x_sample': nrm((DEC_BATCH, DEC_SEQ, D_MODEL)),
        'cache_win_k': nrm((DEPTH, DEC_BATCH, win_len, A_HEADS, HEAD_DIM)),
        'cache_win_v': nrm((DEPTH, DEC_BATCH, win_len, A_HEADS, HEAD_DIM)),
        'cache_sb_k': nrm((DEPTH, n_pool, PAGE_SIZE, C_HEADS, HEAD_DIM)),
        'cache_sb_v': nrm((DEPTH, n_pool, PAGE_SIZE, C_HEADS, HEAD_DIM)),
        'state_gla': nrm((DEPTH, DEC_BATCH, B_HEADS, B_DK, B_DV)),
        'state_ssm': nrm((DEPTH, DEC_BATCH, D_HEADS, D_HEADDIM, D_STATE)),
        'state_conv': nrm((DEPTH, DEC_BATCH, CONV_W - 1, CONV_CH)),
        'page_table': page_table,
        'c_prompt': nrm((BATCH, D_MODEL)),
        'c_sample': nrm((DEC_BATCH, D_MODEL)),
        'w_ada': nrm((DEPTH, D_MODEL, 6 * D_MODEL), 0.5 * D_MODEL ** -0.5),
        'b_ada': nrm((DEPTH, 6 * D_MODEL), 0.02),
        'g_norm1': 1.0 + nrm((DEPTH, D_MODEL), 0.02),
        'g_norm2': 1.0 + nrm((DEPTH, D_MODEL), 0.02),
        'w_in': nrm((DEPTH, D_MODEL, N_IN), D_MODEL ** -0.5),
        'w_gla_a2': nrm((DEPTH, GLA_RANK, B_HEADS * B_DK), GLA_RANK ** -0.5),
        'b_gla_a': nrm((DEPTH, B_HEADS * B_DK), 0.1),
        'g_gla': 1.0 + nrm((DEPTH, B_DV), 0.02),
        'b_sb': SB_BIAS_INIT + nrm((DEPTH, C_HEADS), 0.1),
        'w_conv': nrm((DEPTH, CONV_W, CONV_CH), CONV_W ** -0.5),
        'b_conv': nrm((DEPTH, CONV_CH), 0.02),
        'dt_bias': dt_bias,
        'a_log': a_log,
        'd_skip': 1.0 + nrm((DEPTH, D_HEADS), 0.02),
        'g_ssm': 1.0 + nrm((DEPTH, D_INNER), 0.02),
        'w_out': nrm((DEPTH, D_MIX, D_MODEL), D_MIX ** -0.5),
        'w_router_grp': nrm((DEPTH, D_MODEL, N_EXP_GROUPS), D_MODEL ** -0.5),
        'b_router_grp': nrm((DEPTH, N_EXP_GROUPS), 0.01),
        'w_router_exp': nrm((DEPTH, D_MODEL, N_EXPERTS), D_MODEL ** -0.5),
        'b_router_exp': nrm((DEPTH, N_EXPERTS), 0.01),
        'w_exp_gate': nrm((DEPTH, N_EXPERTS, D_MODEL, D_EXPERT), D_MODEL ** -0.5),
        'w_exp_up': nrm((DEPTH, N_EXPERTS, D_MODEL, D_EXPERT), D_MODEL ** -0.5),
        'w_exp_down': nrm((DEPTH, N_EXPERTS, D_EXPERT, D_MODEL), D_EXPERT ** -0.5),
        'g_final': 1.0 + nrm((D_MODEL,), 0.02),
    }

def reference(x_prompt, x_sample, cache_win_k, cache_win_v, cache_sb_k, cache_sb_v, state_gla, state_ssm,
              state_conv, page_table, c_prompt, c_sample, w_ada, b_ada, g_norm1, g_norm2, w_in, w_gla_a2,
              b_gla_a, g_gla, b_sb, w_conv, b_conv, dt_bias, a_log, d_skip, g_ssm, w_out, w_router_grp,
              b_router_grp, w_router_exp, b_router_exp, w_exp_gate, w_exp_up, w_exp_down, g_final):
    db = x_sample.shape[0]
    past_len = page_table.shape[1] * cache_sb_k.shape[2]
    pos_p = jnp.arange(x_prompt.shape[1])
    pos_s = past_len + jnp.arange(x_sample.shape[1])
    xp, xs = x_prompt, x_sample
    states_p, states_s = [], []
    for l in range(DEPTH):
        p = {'w_ada': w_ada[l], 'b_ada': b_ada[l], 'g_norm1': g_norm1[l], 'g_norm2': g_norm2[l],
             'w_in': w_in[l], 'w_gla_a2': w_gla_a2[l], 'b_gla_a': b_gla_a[l], 'g_gla': g_gla[l],
             'b_sb': b_sb[l], 'w_conv': w_conv[l], 'b_conv': b_conv[l], 'dt_bias': dt_bias[l],
             'a_log': a_log[l], 'd_skip': d_skip[l], 'g_ssm': g_ssm[l], 'w_out': w_out[l],
             'w_router_grp': w_router_grp[l], 'b_router_grp': b_router_grp[l],
             'w_router_exp': w_router_exp[l], 'b_router_exp': b_router_exp[l],
             'w_exp_gate': w_exp_gate[l], 'w_exp_up': w_exp_up[l], 'w_exp_down': w_exp_down[l]}
        xp, st_p = block(xp, c_prompt, pos_p, p, None)
        k_past = cache_sb_k[l][page_table].reshape(db, past_len, C_HEADS, HEAD_DIM)
        v_past = cache_sb_v[l][page_table].reshape(db, past_len, C_HEADS, HEAD_DIM)
        cache = (cache_win_k[l], cache_win_v[l], k_past, v_past, state_gla[l], state_ssm[l], state_conv[l])
        xs, st_s = block(xs, c_sample, pos_s, p, cache)
        states_p.append(st_p)
        states_s.append(st_s)
    y_prompt = rmsnorm(xp, g_final)
    y_sample = rmsnorm(xs, g_final)
    win_k_p, win_v_p, sb_k_p, sb_v_p, gla_p, ssm_p, conv_p = [jnp.stack(t) for t in zip(*states_p)]
    win_k_s, win_v_s, sb_k_s, sb_v_s, gla_s, ssm_s, conv_s = [jnp.stack(t) for t in zip(*states_s)]
    return (y_prompt, y_sample, win_k_p, win_v_p, win_k_s, win_v_s, sb_k_p, sb_v_p, sb_k_s, sb_v_s,
            gla_p, gla_s, ssm_p, ssm_s, conv_p, conv_s)


_drawn_inputs = setup_inputs


def setup_inputs(seed=0):
    import zlib

    import numpy as np

    out = dict(_drawn_inputs(seed))
    spreads = {}
    factors = {'cache_win_k': 2.736,
     'cache_sb_k': 64.0,
     'cache_sb_v': 64.0,
     'g_norm2': 3.278,
     'g_gla': 8.0,
     'b_sb': 64.0,
     'd_skip': 8.0,
     'g_ssm': 8.0,
     'b_router_grp': 7.317,
     'b_router_exp': 6.379,
     'g_final': 8.661}
    for name, (base, spread) in spreads.items():
        noise = np.random.default_rng([zlib.crc32(name.encode()), seed]).standard_normal(out[name].shape)
        drawn = base * np.exp(spread * noise) if base else spread * noise
        out[name] = __import__('jax').numpy.asarray(drawn.astype(out[name].dtype))
    for name, factor in factors.items():
        out[name] = (out[name] * factor).astype(out[name].dtype)
    return out
```

```python
from contextlib import ExitStack

import numpy as np

import concourse.bass as bass
from concourse import mybir

F32, I32, U32 = mybir.dt.float32, mybir.dt.int32, mybir.dt.uint32
ALU, ACT, AX = mybir.AluOpType, mybir.ActivationFunctionType, mybir.AxisListType

DM, SEQ, DEPTH, DB, DS, PAST, PAGE = 1024, 256, 2, 8, 8, 2048, 128
KT8 = DM // 128
NS = DB * DS
T = SEQ + NS
SPANS = ((0, 128), (128, 128), (256, 64))
NH, HD = 4, 64
N_POOL = DB * (PAST // PAGE) * 5 // 4
NE, FE = 32, 512
CONV_CH = 512
EPS = 1e-6
BIG_F = float(2.0 ** 100)
NEG = -1e30
ROPE_DIM, THETA = 16, 500000.0
AQ, AK, AV, BQ, BK, BV, CQ, CK, CV, GATE, Z, XBC = 0, 2, 4, 6, 7, 8, 10, 12, 14, 16, 18, 20
RING = 4
CHUNKS = 12 + 6 + 2 + 3 * NE
PER_SLOT = CHUNKS // RING
NA1, NA = 768, 1280
NVEC = 88


def constants():
    out = {}
    p = np.arange(128)
    out["ident"] = np.eye(128)
    half = ROPE_DIM // 2
    freq = np.exp(-np.log(THETA) * np.arange(half, dtype=np.float32) * np.float32(2.0 / ROPE_DIM)).astype(np.float32)
    pos = np.concatenate([np.arange(SEQ), np.tile(PAST + np.arange(DS), DB)]).astype(np.float32)
    ang = (pos[None, :] * freq[:, None]).astype(np.float32)
    cos, sin = np.ones((128, T)), np.zeros((128, T))
    turn = np.zeros((128, 128))
    for base in (0, 64):
        for d in range(half):
            cos[base + d] = cos[base + half + d] = np.cos(ang[d].astype(np.float64))
            sin[base + d] = sin[base + half + d] = np.sin(ang[d].astype(np.float64))
            turn[base + half + d, base + d] = -1
            turn[base + d, base + half + d] = 1
    out["cos"], out["sin"], out["turn"] = cos, sin, turn

    def mult(dist):
        return sum(((dist >= 0) & (dist <= w) & (dist % d == 0)).astype(int) for w, d in ((128, 1), (512, 4), (2048, 16)))

    def cap(m):
        return np.where(m == 0, NEG, m * BIG_F)

    q = np.stack([p, p + 128], 1)[:, :, None]
    k = np.arange(SEQ)[None, None, :]
    out["cap_a"] = cap(mult(q - k)).reshape(128, -1)
    out["cap_c"] = cap((k < q).astype(int)).reshape(128, -1)
    qs = (PAST + np.arange(32) % DS)[:, None]
    far = np.concatenate([16 * np.arange(96) + r for r in range(8)])
    near = np.concatenate([1536 + 4 * p + j for j in range(4)])
    rows = np.zeros((128, NA))
    rows[:32] = cap(mult(qs - np.concatenate([far, near])[None, :]))
    out["cap_sa"] = rows
    b = np.arange(DB)[None, :, None, None]
    bb, j = np.arange(DB)[None, None, :, None], np.arange(DS)[None, None, None, :]
    i = (np.arange(32) % DS)[:, None, None, None]
    for name, ok in (("cap_na", mult(i - j) * (b == bb)), ("cap_nc", (j < i) * (b == bb) * 1)):
        rows = np.zeros((128, DB * NS))
        rows[:32] = cap(ok).reshape(32, -1)
        out[name] = rows
    s, t = p[:, None], p[None, :]
    for name, c in (("tri64", 64), ("tri8", 8)):
        out[name] = ((s // c == t // c) & (s <= t)).astype(int)
        out[name + "c"] = np.where(out[name] == 0, NEG, BIG_F)
    out["blk64"] = s // 64 == t // 64
    out["blk8"] = s // 8 == t // 8
    out["diag_gla"] = (s // 32) == (np.arange(256)[None, :] // 64)
    out["ones"] = np.ones((128, 128))
    out["seq_of"] = (p[:, None] // 8) == np.arange(8)[None, :]
    out["ones256"] = np.ones((128, 256))
    out["ones1"] = np.ones((128, 1))
    out["rev"] = np.tile(np.arange(8, 0, -1), (128, 1))
    reset = np.ones((128, T))
    reset[:, 0:SEQ:64] = 0
    reset[:, SEQ::8] = 0
    out["reset"] = reset
    out["sub"] = (p % 16)[:, None]
    return {n: np.ascontiguousarray(v, np.float32) for n, v in out.items()}


CONST = constants()
COFF, at = {}, 0
for _n, _v in CONST.items():
    COFF[_n] = (at, _v.shape[1])
    at += _v.shape[1]
NCONST = at


def trunk(nc, x_rows, c_rows, win_k, win_v, sb_k, sb_v, st_gla, st_ssm, st_conv, pages, w_ada, vecs, w_in,
          w_tail, w_a2, bcs, b_sb, w_out, w_router, w_gate, w_up, w_down, g_final, consts,
          y_p, y_s, wk_p, wv_p, wk_s, wv_s, sk_p, sv_p, sk_s, sv_s, gla_p, gla_s, ssm_p, ssm_s, cv_p, cv_s):
    with ExitStack() as ctx:
        def sb(name, n, dt=F32):
            return ctx.enter_context(nc.sbuf_tensor(name, [128, n], dt))

        cst = sb("cst", NCONST)

        def K(name, parts=128):
            o, n = COFF[name]
            return cst[0:parts, o:o + n]

        ring = [sb(f"ring{i}", 4096) for i in range(RING)]
        xT_ = sb("xT", KT8 * T)
        mT_ = sb("mT", KT8 * T)
        modT_ = sb("modT", 48 * 9)
        scaleT_ = sb("scaleT", 8 * 9)
        cT_ = sb("cT", 8 * 9)
        cT2_ = sb("cT2", 8 * 9)
        vec = sb("vec", NVEC)
        vrow = sb("vrow", 128)
        bc = sb("bc", 52)
        gfin = sb("gfin", 8)
        wtail_ = sb("wtail", 8 * 20)
        wr_ = sb("wr", 8 * 36)
        wa2 = sb("wa2", 128)
        bsb = sb("bsb", 1)
        qzA_ = sb("qzA", 4 * T)
        qzC_ = sb("qzC", 4 * T)
        vA_ = sb("vA", 3 * 256)
        vC_ = sb("vC", 3 * 256)
        kS_ = sb("kS", 4 * NS)
        qb_ = sb("qb", 2 * 32)
        pS_ = sb("pS", 17 * 32)
        idxf = sb("idxf", 16)
        idxi = sb("idxi", 16, I32)
        idxu = sb("idxu", 16, U32)
        rr = sb("rr", T)
        rv, rt = sb("rv", 2 * T), sb("rt", 2 * T)
        sm = sb("sm", 64)
        big = sb("big", 16896)
        PS = ctx.enter_context(nc.psum_tensor("PS", [128, 8, 512], F32))
        PSF = PS[:, :, :].rearrange("p b n -> p (b n)")

        def v3(t, off, a, b, parts=128):
            return t[0:parts, off:off + a * b].rearrange("p (a b) -> p a b", a=a)

        def v4(t, off, a, b, c, parts=128):
            return t[0:parts, off:off + a * b * c].rearrange("p (a b c) -> p a b c", a=a, b=b)

        def spread(ap, axis, n):
            u = ap.unsqueeze(axis)
            shape = list(u.shape)
            shape[axis] = n
            return u.to_broadcast(shape)

        xT, mT = v3(xT_, 0, KT8, T), v3(mT_, 0, KT8, T)
        modT = v3(modT_, 0, 48, 9)
        wtail, wr = v3(wtail_, 0, 8, 20), v3(wr_, 0, 8, 36)
        qzA, qzC = v3(qzA_, 0, 4, T), v3(qzC_, 0, 4, T)
        vA, vC = v3(vA_, 0, 3, 256), v3(vC_, 0, 3, 256)
        kS = v3(kS_, 0, 4, NS)
        ident, ones = K("ident"), K("ones")
        SCR = 10412
        PT = v3(big, 0, 20, T)
        lrT = big[0:16, 6400:6720]
        XP = v3(big, 6720, 4, 347)
        XPs = XP[:, :, 259:347].rearrange("p c (b k) -> p c b k", b=DB)
        kA, kC, vB = v3(big, 8108, 3, 256), v3(big, 8876, 3, 256), v3(big, 9644, 3, 256)

        def ring3(s, a):
            return v3(ring[s], 0, a, 4096 // a)

        cvo = sb("cvo", 512)
        idxb = sb("idxb", 2, U32)
        L3 = lambda off, a, b: v3(big, off, a, b)
        class gla:
            cum = big[:, 0:320]
            ec = big[:, 320:640]
            en = big[:, 640:960]
            el = big[:, 960:1280]
            kg = big[:, 1280:1600]
            kdT = big[:, 1600:1920]
            qg = big[:, 2560:2880]
            la = big[:, 2880:3200]
            qgz = L3(3200, 4, T)
            kdt = L3(4480, 3, 128)
            kdm = L3(8108, 8, 128)
            att = L3(SCR, 3, 512)
            st0 = L3(11948, 8, 256)
            stp = L3(13996, 4, 256)
            raw = L3(16044, 8, 64)
            o = L3(15020, 2, T)
            sq = L3(15660, 2, T)
            last = sm[:, 32:44]

        class ssd:
            xc = L3(0, 4, T)
            tok = L3(1280, 3, 384)
            cz = L3(2432, 2, T)
            ce = L3(3072, 4, T)
            ex = L3(3072, 4, T)
            dab = v4(big, 3072, 3, 4, 128)
            ec = L3(8108, 4, T)
            dec = v4(big, 9388, 3, 4, 128)
            xdt = L3(10924, 3, 256)
            xw = L3(11692, 3, 256)
            bm = L3(12460, 8, 128)
            raw = L3(13484, 8, 128)
            st0 = L3(14508, 8, 128)
            stp = L3(15532, 4, 128)
            y = L3(3072, 2, T)
            sq = L3(3712, 2, T)
            outb = big[:, 9388:10540]
            v = L3(16044, 3, 4)
            tt = L3(16056, 3, 4)
            u = L3(16068, 3, 4)
            w1 = L3(16080, 3, 4)
            l = L3(16092, 3, 4)
            d = L3(16104, 3, 4)
            eq = L3(16116, 3, 4)
            dt = L3(16128, 3, 4)
            da = L3(16140, 3, 4)
            cum = L3(16152, 3, 4)
            w = L3(16164, 3, 4)
            alog = big[:, 16176:16180]
            last = L3(16180, 12, 2)
            dsk = big[:, 16204:16206]

        ssd.fin = lambda j: ssd.stp[:, 3, :] if j == 0 else ssd.st0[:, j - 1, :]
        class seq:
            kT = L3(8192, 2, 2112)
            s = big[0:32, 12416:14528]
            t = big[0:32, 14528:16640]

        seq.kt8 = lambda k, g, jh: seq.kT[:, k, g * 1024:(g + 1) * 1024].rearrange("p (q e) -> p e q", e=8)[:, jh * 4:jh * 4 + 4, :]
        class moe:
            y = L3(0, 8, T)
            a = L3(2560, 4, T)
            gt = L3(3840, 3, 32)
            gt4 = v4(big, 3840, 3, 4, 8)
            gT = big[:, 3936:4256]
            gm = big[:, 4256:4576]
            gb = big[:, 4576:4896]
            e = L3(4896, 2, T)
            L = L3(5536, 3, 36)
            tmp = L3(5644, 3, 8)
            km = big[:, 5668:5671]
            gmax = big[:, 5671:5674]
            ghot = L3(5674, 3, 4)
            gx = L3(5686, 3, 4)
            e8 = L3(5698, 3, 8)
            m1 = big[:, 5722:5725]
            m2 = big[:, 5725:5728]
            h1 = L3(5728, 3, 8)
            h2 = L3(5752, 3, 8)
            dx = big[:, 5776:5779]
            gp = big[:, 5779:5782]


        ring_full = [ctx.enter_context(nc.semaphore(f"ring_full{i}")) for i in range(RING)]
        ring_free = [ctx.enter_context(nc.semaphore(f"ring_free{i}")) for i in range(RING)]
        a_k_full = ctx.enter_context(nc.semaphore("a_k_full"))
        a_v_full = ctx.enter_context(nc.semaphore("a_v_full"))
        loads = ctx.enter_context(nc.semaphore("loads"))
        outputs = ctx.enter_context(nc.semaphore("outputs"))
        gathered_k = ctx.enter_context(nc.semaphore("gathered_k"))
        gathered_v = ctx.enter_context(nc.semaphore("gathered_v"))
        k_free = ctx.enter_context(nc.semaphore("k_free"))
        v_free = ctx.enter_context(nc.semaphore("v_free"))
        arrived = ctx.enter_context(nc.semaphore("arrived"))
        cleared = ctx.enter_context(nc.semaphore("cleared"))
        seen = ctx.enter_context(nc.semaphore("seen"))
        go = ctx.enter_context(nc.semaphore("go"))

        LOADS_PRE, LOADS_A, LOADS_B = 16 * 13, 16 * 10, 16
        LOADS = LOADS_A + LOADS_B + 32
        OUTS_B, OUTS_G = 160, 128
        OUTS = OUTS_B + OUTS_G + 64
        sem = {}
        for n in ("dve_step act_step pool_step variance rstd rows_in rows_T c_T silu_e vec_T mod_mm mod_done sq rms_mm h_done "
                  "proj_mm proj_ev tail_mm convT_mm xp_done pre_T "
                  "turn_mm rope_done qz_done tok_mm tok_ev tail27_mm tail27_ev "
                  "sA_mm sA_cap eA pA_done tA_mm tA_ev oA_mm oA_ev "
                  "zC_mm zC_ev zC_t zC_l zC_r zC_a tC_mm tC_ev oC_mm "
                  "lr_mm gla_operands gla_scores_mm gla_scores_masked gla_kv_mm gla_states gla_out_mm gla_squares "
                  "gla_norm_mm conv_silu xb_turned ssm_in_turned log_decays cum_mm cb_mm decays_spread cum_rows_mm "
                  "cb_sample_mm ssd_operands bx_mm ssm_states ssd_out_mm ssm_final ssm_turned ssd_squares ssd_norm_mm "
                  "a_keys_turned a_keys_copied_dve a_keys_copied_act a_queries a_scores_mm a_probs a_probs_turned "
                  "a_probs_copied a_out_mm c_keys_copied_dve c_keys_copied_act c_keys_turned c_queries c_logits_mm "
                  "c_weights c_weights_turned c_weights_copied a_out_copied c_out_mm router_mm gates_done gates_turned "
                  "gate_row down_added gate_mm hidden up_mm gate_copied down_mm rows_turned gate_logits gate_abs "
                  "gate_log gla_cum gla_exps silu_exp conv_done conv_exp dt_exp dt_plus1 dt_log ssm_in_copied "
                  "decay_left decay_left_exp cum_exps decay_args decay_exps ssm_out_copied a_max a_exp c_logits c_abs "
                  "c_log c_exponents c_out_copied group_args group_exps pair_args pair_exps expert_exp rows_copied "
                  "gla_final_states ").split():
            sem[n] = ctx.enter_context(nc.semaphore(n))

        own = {}

        def step(eng, ins):
            own[eng][1] += 1
            ins.then_inc(own[eng][0], 1)
            eng.wait_ge(own[eng][0], own[eng][1])

        def barrier(eng):
            eng.drain().then_inc(arrived, 1)
            eng.wait_ge(cleared, 1)
            eng.sem_inc(seen, 1)
            eng.wait_ge(go, 1)
            own[eng][1] = 0

        def barrier_lead(pool):
            pool.sem_inc(arrived, 1)
            pool.wait_ge(arrived, 4)
            nums = sorted(s.num for s in sem.values())
            assert nums[-1] - nums[0] == len(nums) - 1
            pool.sem_clear(range(nums[0], nums[-1] + 1))
            pool.sem_clear(arrived)
            pool.sem_clear(go)
            pool.sem_inc(cleared, 1)
            pool.wait_ge(seen, 3)
            pool.sem_clear(seen)
            pool.sem_clear(cleared)
            pool.sem_inc(go, 1)
            own[pool][1] = 0

        STAGES_BEFORE, STAGES_AFTER = 0, 0
        block = ctx.enter_context(nc.Block())

        @block.sync
        def _(sp):
            def load(l, src, slot, idx):
                sp.wait_ge(ring_free[slot], l * PER_SLOT + idx + 1)
                a = src.shape[1]
                sp.dma_start(ring3(slot, a), src).then_inc(ring_full[slot], 16)

            with sp.Fori(0, DEPTH) as l:
                with sp.Fori(0, 3) as it:
                    for s in range(4):
                        src = w_ada[l, :, bass.ds(it * 2048 + s * 512, 512)]
                        load(l, src.rearrange("(k p) n -> p k n", p=128), s, it)
                for j in range(6):
                    load(l, w_in[l, :, j * 512:(j + 1) * 512].rearrange("(k p) n -> p k n", p=128), j % 4, 3 + j // 4)
                with sp.Fori(0, DB) as b:
                    sp.wait_ge(k_free, l * (DB + 1) + b + 1)
                    kb, vb = v3(big, 0, 8, 256), v3(big, 4096, 8, 256)
                    kn, vn = v3(big, 2048, 4, 256), v3(big, 6144, 4, 256)
                    for cache, far, near, full, free in ((win_k, kb, kn, a_k_full, None), (win_v, vb, vn, a_v_full, v_free)):
                        if free is not None:
                            sp.wait_ge(free, l * (DB + 1) + b + 1)
                        sp.dma_start(far[0:96], cache[l, b, 0:1536].rearrange("(a r) c -> a r c", r=16)[:, 0:8, :]).then_inc(full, 16)
                        sp.dma_start(near, cache[l, b, 1536:2048].rearrange("(p r) c -> p r c", r=4)).then_inc(full, 16)
                for j in range(2):
                    load(l, w_out[l, :, j * 512:(j + 1) * 512].rearrange("(k p) n -> p k n", p=128), 2 + j, 4)
                with sp.Fori(0, NE // 4) as it:
                    for q in range(12):
                        e = it * 4 + q // 3
                        w = (w_gate, w_up, w_down)[q % 3]
                        load(l, w[l, e].rearrange("(k p) n -> p k n", p=128), q % 4, it * 3 + 5 + q // 4)

        @block.tensor
        def _(pe):
            own[pe] = [None, 0]
            mm = nc.tensor.matmul

            def tr(out, in_):
                return nc.tensor.transpose(out, in_, ident[0:in_.shape[0], 0:in_.shape[0]])

            def full(l, slot, idx):
                pe.wait_ge(ring_full[slot], (l * PER_SLOT + idx + 1) * 16)

            def pre():
                pe.wait_ge(loads, LOADS_PRE)
                rows = v3(big, 0, 3, 1024)
                for k in range(KT8):
                    for t, (t0, n) in enumerate(SPANS):
                        i = tr(PS[:, k, t0:t0 + n], rows[0:n, t, k * 128:(k + 1) * 128])
                i.then_inc(sem["rows_T"], 1)
                pe.wait_ge(sem["rows_in"], 1)
                pe.wait_ge(sem["xp_done"], 1)
                for k in range(KT8):
                    i = tr(PS[:, 0, k * 9:(k + 1) * 9], big[0:9, 4096 + k * 128:4096 + (k + 1) * 128])
                i = tr(PS[:, 1, 0:8], big[0:8, 5120:5248])
                i.then_inc(sem["c_T"], 1)

            def rms():
                pe.wait_ge(sem["sq"], 1)
                sq = v3(big, SCR, KT8, T)
                for k in range(KT8):
                    i = mm(PS[:, 1, 0:T], ones, sq[:, k, :], start=(k == 0), stop=(k == KT8 - 1))
                i.then_inc(sem["rms_mm"], 1)

            def stage_a(l):
                pe.wait_ge(loads, l * LOADS + LOADS_PRE + LOADS_A)
                i = tr(PS[:, 1, 0:NVEC], vrow[0:NVEC, :])
                i.then_inc(sem["vec_T"], 1)
                crow = big[0:24, SCR + 2560:SCR + 3072]
                for c in range(4):
                    i = tr(PS[:, 2, 24 * c:24 * c + 24], crow[:, c * 128:(c + 1) * 128])
                i.then_inc(sem["convT_mm"], 1)
                with pe.Fori(0, 3) as it:
                    for s in range(4):
                        full(l, s, it)
                        for m in range(4):
                            for k in range(KT8):
                                i = mm(PS[:, 0, bass.ds(it * 144 + s * 36 + m * 9, 9)], ring3(s, 8)[:, k, m * 128:(m + 1) * 128],
                                       v3(cT_, 0, 8, 9)[:, k, :], start=(k == 0), stop=(k == 7))
                        i.then_inc(ring_free[s], 1)
                pe.drain().then_inc(sem["mod_mm"], 1)
                pe.wait_ge(sem["vec_T"], 1)
                pe.wait_ge(sem["mod_done"], 1)
                rms()
                pe.wait_ge(sem["h_done"], 1)
                pe.wait_ge(sem["xp_done"], 1)
                for c in range(24):
                    j, m = divmod(c, 4)
                    if m == 0:
                        full(l, j % 4, 3 + j // 4)
                    if c >= 4:
                        pe.wait_ge(sem["proj_ev"], c - 3)
                    for k in range(KT8):
                        i = mm(PS[:, c % 4, 0:T], ring3(j % 4, 8)[:, k, m * 128:(m + 1) * 128], mT[:, k, :],
                               start=(k == 0), stop=(k == 7))
                    i.then_inc(sem["proj_mm"], 1)
                    if m == 3:
                        pe.wait_ge(sem["proj_mm"], c + 1)
                        pe.sem_inc(ring_free[j % 4], 1)
                for k in range(KT8):
                    mm(PS[0:16, 4, 0:T], wtail[:, k, 0:16], mT[:, k, :], start=(k == 0), stop=(k == 7))
                for t, (t0, n) in enumerate(SPANS):
                    for k in range(KT8):
                        i = mm(PS[0:n, 5, 4 * t:4 * t + 4], mT[:, k, t0:t0 + n], wtail[:, k, 16:20], start=(k == 0), stop=(k == 7))
                i.then_inc(sem["tail_mm"], 1)

            def tok(chunks, bank, n_free):
                for t, (t0, n) in enumerate(SPANS):
                    for c in range(2):
                        o = PS[0:n, bank + t // 2, (t % 2) * 256 + c * 128:(t % 2) * 256 + c * 128 + 128]
                        i = tr(o, PT[:, chunks + c, t0:t0 + n])
                return i

            def stage_b():
                for c in range(4):
                    i = mm(PS[:, c, 0:T], K("turn"), PT[:, AQ + c, :], start=True, stop=True)
                i.then_inc(sem["turn_mm"], 1)
                tail = v3(big, SCR, 4, 27)
                pe.wait_ge(sem["pre_T"], 1)
                for c in range(4):
                    i = tr(PS[0:27, 4, c * 128:(c + 1) * 128], tail[:, c, :])
                i.then_inc(sem["tail27_mm"], 1)
                pe.wait_ge(sem["rope_done"], 1)
                tok(AK, 0, 0).then_inc(sem["tok_mm"], 1)
                tok(AV, 2, 0).then_inc(sem["tok_mm"], 1)
                tok(BV, 6, 0).then_inc(sem["tok_mm"], 1)
                pe.wait_ge(sem["tail27_ev"], 1)
                tok(CK, 4, 0).then_inc(sem["tok_mm"], 1)
                pe.wait_ge(sem["tok_ev"], 1)
                tok(CV, 0, 0).then_inc(sem["tok_mm"], 1)
                pe.wait_ge(sem["tok_ev"], 5)
                s, pt = v3(big, SCR, 4, 512), v4(big, SCR + 4096, 2, 4, 256)
                for qz, kc, v, oc, names in ((qzA, AK, vA, 0, ("sA_mm", "pA_done", "tA_mm", "tA_ev", "oA_mm", "sA_cap", "oA_ev")),
                                             (qzC, CK, vC, 4, ("zC_mm", "zC_a", "tC_mm", "tC_ev", "oC_mm", "zC_ev", "oC_ev"))):
                    if oc == 0:
                        pe.wait_ge(sem["qz_done"], 1)
                    else:
                        pe.wait_ge(sem["oA_ev"], 1)
                    for h in range(4):
                        for qb in range(2):
                            i = mm(PS[:, h, qb * 256:qb * 256 + 256], qz[:, h, qb * 128:qb * 128 + 128],
                                   PT[:, kc + h // 2, 0:256], start=True, stop=True)
                    i.then_inc(sem[names[0]], 1)
                    pe.wait_ge(sem[names[1]], 1)
                    for kb in range(2):
                        for h in range(4):
                            for qb in range(2):
                                i = tr(PSF[:, kb * 1024 + h * 256 + qb * 128:kb * 1024 + h * 256 + qb * 128 + 128],
                                       s[:, h, qb * 256 + kb * 128:qb * 256 + kb * 128 + 128])
                    i.then_inc(sem[names[2]], 1)
                    pe.wait_ge(sem[names[3]], 1)
                    for h in range(4):
                        for kb in range(2):
                            i = mm(PS[64 * (h % 2):64 * (h % 2) + 64, 4 + h // 2, 0:256], v[:, kb, h * 64:h * 64 + 64],
                                   pt[:, kb, h, :], start=(kb == 0), stop=(kb == 1))
                    i.then_inc(sem[names[4]], 1)

            def stage_gla():
                i = mm(PS[:, 7, 0:T], wa2[0:16, :], lrT, start=True, stop=True)
                i.then_inc(sem["lr_mm"], 1)
                G = gla
                pe.wait_ge(sem["gla_operands"], 1)
                for t, (t0, n) in enumerate(SPANS):
                    mm(PS[0:n, t, 0:4 * n].rearrange("p (h t) -> p h t", h=4), G.kg[:, t0:t0 + n], G.qgz[:, :, t0:t0 + n], start=True, stop=True)
                for t, (t0, n) in enumerate(SPANS):
                    i = tr(PS[0:n, 3, t * 128:(t + 1) * 128], G.kdT[:, t0:t0 + n])
                i.then_inc(sem["gla_scores_mm"], 1)
                pe.wait_ge(sem["gla_scores_masked"], 1)
                for c in range(4):
                    r = 64 * (c % 2)
                    mm(PS[:, 4 + c % 2, (c // 2) * 256:(c // 2) * 256 + 256], G.kdt[r:r + 64, c // 2, :], vB[r:r + 64, c // 2, :],
                       start=True, stop=True)
                for b in range(DB):
                    i = mm(PSF[:, b * 256:b * 256 + 256], G.kdm[0:64, b, :], vB[0:64, 2, :], start=True, stop=True)
                i.then_inc(sem["gla_kv_mm"], 1)
                pe.wait_ge(sem["gla_states"], 1)
                for c in range(2):
                    o = PS[:, 6 + c, 0:T]
                    cs = slice(c * 128, c * 128 + 128)
                    for b in range(DB):
                        mm(o[:, 256 + 8 * b:264 + 8 * b], G.st0[:, b, cs], G.qg[:, 256 + 8 * b:264 + 8 * b],
                           start=(b == 0), stop=False, skip_group_check=True)
                    for j in range(1, 4):
                        mm(o[:, 64 * j:64 * j + 64], G.stp[:, j - 1, cs], G.qg[:, 64 * j:64 * j + 64],
                           start=False, stop=False, skip_group_check=True)
                    for hh in range(2):
                        h = 2 * c + hh
                        for t, (t0, n) in enumerate(SPANS):
                            att = G.att[0:n, t, 0:4 * n].rearrange("p (h t) -> p h t", h=4)
                            i = mm(o[64 * hh:64 * hh + 64, t0:t0 + n], vB[0:n, t, h * 64:h * 64 + 64], att[:, h, :],
                                   start=False, stop=(t == 2), skip_group_check=True)
                i.then_inc(sem["gla_out_mm"], 1)
                pe.wait_ge(sem["gla_squares"], 1)
                for c in range(2):
                    i = mm(PS[:, c, 0:T], K("blk64"), G.sq[:, c, :], start=True, stop=True)
                i.then_inc(sem["gla_norm_mm"], 1)

            def stage_ssd(l):
                D = ssd
                pe.wait_ge(sem["conv_silu"], 1)
                for c in range(3):
                    for t, (t0, n) in enumerate(SPANS):
                        i = tr(PS[0:n, t, c * 128:(c + 1) * 128], D.xc[:, c, t0:t0 + n])
                i.then_inc(sem["xb_turned"], 1)
                pe.wait_ge(loads, l * LOADS + LOADS_PRE + LOADS)
                for b in range(DB):
                    i = tr(PSF[:, 1536 + b * 128:1536 + b * 128 + 128], D.raw[:, b, :])
                i.then_inc(sem["ssm_in_turned"], 1)
                pe.wait_ge(sem["log_decays"], 1)
                for t, (t0, n) in enumerate(SPANS):
                    tri, blk = (K("tri8"), K("blk8")) if t == 2 else (K("tri64"), K("blk64"))
                    mm(PS[0:n, 5, 4 * t:4 * t + 4], tri[0:n, 0:n], D.da[0:n, t, :], start=True, stop=True)
                    i = mm(PS[0:n, 5, 16 + 4 * t:20 + 4 * t], blk[0:n, 0:n], D.da[0:n, t, :], start=True, stop=True)
                i.then_inc(sem["cum_mm"], 1)
                for t, (t0, n) in enumerate(SPANS):
                    i = mm(PS[0:n, 6, 0:2 * n].rearrange("p (g t) -> p g t", g=2) if t == 2 else PS[0:n, 6 + t, 0:256].rearrange("p (g t) -> p g t", g=2),
                           D.xc[:, 2, t0:t0 + n], D.cz[:, :, t0:t0 + n], start=True, stop=True) if t < 2 else i
                i.then_inc(sem["cb_mm"], 1)
                pe.wait_ge(sem["decays_spread"], 1)
                for h in range(4):
                    for t, (t0, n) in enumerate(SPANS):
                        tri = K("tri8") if t == 2 else K("tri64")
                        i = mm(PS[:, h, t0:t0 + n], D.dab[0:n, t, h, :], tri[0:n, 0:n], start=True, stop=True)
                i.then_inc(sem["cum_rows_mm"], 1)
                t0, n = SPANS[2]
                i = mm(PS[0:n, 4, 0:2 * n].rearrange("p (g t) -> p g t", g=2), D.xc[:, 2, t0:t0 + n], D.cz[:, :, t0:t0 + n], start=True, stop=True)
                i.then_inc(sem["cb_sample_mm"], 1)
                pe.wait_ge(sem["ssd_operands"], 1)
                for c in range(4):
                    r = 64 * (c % 2)
                    for g in range(2):
                        mm(PS[64 * g:64 * g + 64, c % 2, (c // 2) * 128:(c // 2) * 128 + 128],
                           D.tok[r:r + 64, c // 2, 256 + 64 * g:320 + 64 * g], D.xw[r:r + 64, c // 2, 128 * g:128 * g + 128],
                           start=True, stop=True)
                for b in range(DB):
                    for g in range(2):
                        i = mm(PSF[64 * g:64 * g + 64, 1024 + b * 128:1152 + b * 128], D.bm[0:64, b, 64 * g:64 * g + 64],
                               D.xw[0:64, 2, 128 * g:128 * g + 128], start=True, stop=True)
                i.then_inc(sem["bx_mm"], 1)
                pe.wait_ge(sem["ssm_states"], 1)
                for c in range(2):
                    for hh in range(2):
                        h = 2 * c + hh
                        o = PS[64 * hh:64 * hh + 64, 6 + c, 0:T]
                        for b in range(DB):
                            mm(o[:, 256 + 8 * b:264 + 8 * b], D.st0[:, b, 64 * hh:64 * hh + 64], D.ce[:, h, 256 + 8 * b:264 + 8 * b],
                               start=(b == 0), stop=False, skip_group_check=True)
                        for j in range(1, 4):
                            mm(o[:, 64 * j:64 * j + 64], D.stp[:, j - 1, 64 * hh:64 * hh + 64], D.ce[:, h, 64 * j:64 * j + 64],
                               start=False, stop=False, skip_group_check=True)
                        for t, (t0, n) in enumerate(SPANS):
                            i = mm(o[:, t0:t0 + n], D.xdt[0:n, t, 64 * h:64 * h + 64], D.dec[0:n, t, h, 0:n],
                                   start=False, stop=(t == 2), skip_group_check=True)
                i.then_inc(sem["ssd_out_mm"], 1)
                pe.wait_ge(sem["ssm_final"], 1)
                for j in range(9):
                    i = tr(PSF[:, j * 128:(j + 1) * 128], D.fin(j))
                i.then_inc(sem["ssm_turned"], 1)
                pe.wait_ge(sem["ssd_squares"], 1)
                for c in range(2):
                    i = mm(PS[:, 3, 0:T], ones, D.sq[:, c, :], start=(c == 0), stop=(c == 1))
                i.then_inc(sem["ssd_norm_mm"], 1)

            def seq_a(l, b):
                Q = seq
                pe.wait_ge(a_k_full, (l * DB + b + 1) * 32)
                kb, kn = v3(big, 0, 8, 256), v3(big, 2048, 4, 256)
                for c in range(2):
                    for r in range(8):
                        tr(PS[:, 3 * c + r // 4, (r % 4) * 96:(r % 4) * 96 + 96], kb[0:96, r, c * 128:(c + 1) * 128])
                    for j in range(4):
                        i = tr(PS[:, 3 * c + 2, j * 128:(j + 1) * 128], kn[:, j, c * 128:(c + 1) * 128])
                    i.then_inc(sem["a_keys_turned"], 1)
                pe.wait_ge(sem["a_keys_copied_dve"], 2)
                pe.wait_ge(sem["a_keys_copied_act"], 2)
                pe.wait_ge(sem["a_queries"], 1)
                for n0, n in ((0, 512), (512, 512), (1024, 256)):
                    for c in range(2):
                        mm(PS[0:32, n0 // 512, 0:n], v3(qb_, 0, 2, 32)[:, c, :], Q.kT[:, c, n0:n0 + n], start=(c == 0), stop=(c == 1))
                for c in range(2):
                    i = mm(PS[0:32, 2, 256:320], v3(qb_, 0, 2, 32)[:, c, :], kS[:, c, :], start=(c == 0), stop=(c == 1))
                i.then_inc(sem["a_scores_mm"], 1)
                pe.wait_ge(sem["a_probs"], 1)
                for r in range(8):
                    tr(PS[0:96, 6, r * 32:r * 32 + 32], Q.s[:, r * 96:(r + 1) * 96])
                for j in range(4):
                    tr(PS[:, 6, (8 + j) * 32:(9 + j) * 32], Q.s[:, NA1 + j * 128:NA1 + (j + 1) * 128])
                i = tr(PS[0:64, 6, 384:416], Q.s[:, NA:NA + 64])
                i.then_inc(sem["a_probs_turned"], 1)
                pe.wait_ge(a_v_full, (l * DB + b + 1) * 32)
                pe.wait_ge(sem["a_probs_copied"], 1)
                vb, vn = v3(big, 4096, 8, 256), v3(big, 6144, 4, 256)
                pS = v3(pS_, 0, 17, 32)
                for c in range(2):
                    for r in range(8):
                        mm(PS[:, 7, c * 32:c * 32 + 32], vb[0:96, r, c * 128:(c + 1) * 128], pS[0:96, r, :], start=(r == 0), stop=False)
                    for j in range(4):
                        mm(PS[:, 7, c * 32:c * 32 + 32], vn[:, j, c * 128:(c + 1) * 128], pS[:, 8 + j, :], start=False, stop=False)
                    i = mm(PS[:, 7, c * 32:c * 32 + 32], vA[0:64, 2, c * 128:(c + 1) * 128], pS[0:64, 12, :], start=False, stop=True)
                i.then_inc(sem["a_out_mm"], 1)

            def seq_c(l, b):
                Q = seq
                pe.wait_ge(gathered_k, (l * DB + b + 1) * 32)
                pe.wait_ge(sem["a_scores_mm"], 1)
                kb = v4(big, 0, 2, 8, 256)
                for n in range(8):
                    c, g, jh = n // 4, (n // 2) % 2, n % 2
                    if n >= 3:
                        pe.wait_ge(sem["c_keys_copied_dve" if n % 2 == 0 else "c_keys_copied_act"], (n - 3) // 2 + 1)
                    for j in range(4):
                        i = tr(PS[:, 3 + n % 3, j * 128:(j + 1) * 128], kb[:, g, jh * 4 + j, c * 128:(c + 1) * 128])
                    i.then_inc(sem["c_keys_turned"], 1)
                pe.wait_ge(sem["c_keys_turned"], 8)
                pe.sem_inc(k_free, 1)
                pe.wait_ge(sem["c_keys_copied_act"], 4)
                pe.wait_ge(sem["c_keys_copied_dve"], 4)
                pe.wait_ge(sem["c_queries"], 1)
                for n0 in range(0, 2048, 512):
                    for c in range(2):
                        mm(PS[0:32, n0 // 512, 0:512], v3(qb_, 0, 2, 32)[:, c, :], Q.kT[:, c, n0:n0 + 512], start=(c == 0), stop=(c == 1))
                for c in range(2):
                    i = mm(PS[0:32, 4, 0:64], v3(qb_, 0, 2, 32)[:, c, :], kS[:, 2 + c, :], start=(c == 0), stop=(c == 1))
                i.then_inc(sem["c_logits_mm"], 1)
                pe.wait_ge(sem["c_weights"], 1)
                for g in range(2):
                    for j in range(8):
                        tr(PS[:, 5 + g, j * 32:(j + 1) * 32], Q.s[:, g * 1024 + j:(g + 1) * 1024:8])
                i = tr(PS[0:64, 5, 256:288], Q.s[:, 2048:2112])
                i.then_inc(sem["c_weights_turned"], 1)
                pe.wait_ge(sem["c_weights_copied"], 1)
                pe.wait_ge(sem["a_out_copied"], 2)
                pe.wait_ge(gathered_v, (l * DB + b + 1) * 32)
                vb = v4(big, 4096, 2, 8, 256)
                pS = v3(pS_, 0, 17, 32)
                for c in range(2):
                    for g in range(2):
                        for j in range(8):
                            mm(PS[:, 7, c * 32:c * 32 + 32], vb[:, g, j, c * 128:(c + 1) * 128], pS[:, g * 8 + j, :],
                               start=(g + j == 0), stop=False)
                    i = mm(PS[:, 7, c * 32:c * 32 + 32], vC[0:64, 2, c * 128:(c + 1) * 128], pS[0:64, 16, :], start=False, stop=True)
                i.then_inc(sem["c_out_mm"], 1)
                pe.wait_ge(sem["c_out_mm"], 1)
                pe.sem_inc(v_free, 1)

            def stage_out(l):
                for c in range(8):
                    j, m = divmod(c, 4)
                    if m == 0:
                        full(l, 2 + j, 4)
                    if c >= 4:
                        pe.wait_ge(sem["proj_ev"], c - 3)
                    for k in range(KT8):
                        i = mm(PS[:, 4 + c % 4, 0:T], ring3(2 + j, 8)[:, k, m * 128:(m + 1) * 128], mT[:, k, :], start=(k == 0), stop=(k == 7))
                    i.then_inc(sem["proj_mm"], 1)
                    if m == 3:
                        pe.wait_ge(sem["proj_mm"], c + 1)
                        pe.sem_inc(ring_free[2 + j], 1)
                rms()
                pe.wait_ge(sem["h_done"], 1)
                for t, (t0, n) in enumerate(SPANS):
                    for k in range(KT8):
                        i = mm(PS[0:n, 2, t * 36:(t + 1) * 36], mT[:, k, t0:t0 + n], wr[:, k, :], start=(k == 0), stop=(k == 7))
                i.then_inc(sem["router_mm"], 1)
                pe.wait_ge(sem["gates_done"], 1)
                for t, (t0, n) in enumerate(SPANS):
                    i = tr(PS[0:32, 3, t0:t0 + n], moe.gt[0:n, t, :])
                i.then_inc(sem["gates_turned"], 1)

            def expert(l, it, u):
                M = moe
                q = 3 * u
                sg, su, sd = q % 4, (q + 1) % 4, (q + 2) % 4
                ig, iu, id_ = (it * 3 + 5 + (q + x) // 4 for x in range(3))
                pe.wait_ge(sem["gate_row"], u + 1)
                if u:
                    pe.wait_ge(sem["down_added"], 8 * u)
                i = mm(PS[:, 4, 0:T], ones[0:32, :], M.gm[0:32, :], start=True, stop=True)
                i.then_inc(sem["gate_mm"], 1)
                full(l, sg, ig)
                full(l, su, iu)
                for f in range(4):
                    if u * 4 + f >= 2:
                        pe.wait_ge(sem["hidden"], u * 4 + f - 1)
                    for w, o in ((sg, 0), (su, 2)):
                        for k in range(KT8):
                            i = mm(PS[:, o + f % 2, 0:T], ring3(w, 8)[:, k, f * 128:(f + 1) * 128], mT[:, k, :], start=(k == 0), stop=(k == 7))
                    i.then_inc(sem["up_mm"], 1)
                pe.wait_ge(sem["up_mm"], 4 * u + 4)
                pe.sem_inc(ring_free[sg], 1)
                pe.sem_inc(ring_free[su], 1)
                pe.wait_ge(sem["hidden"], 4 * u + 4)
                pe.wait_ge(sem["gate_copied"], u + 1)
                full(l, sd, id_)
                for d in range(8):
                    if d >= 4:
                        pe.wait_ge(sem["down_added"], 8 * u + d - 3)
                    for f in range(4):
                        i = mm(PS[:, 4 + d % 4, 0:T], ring3(sd, 4)[:, f, d * 128:(d + 1) * 128], M.a[:, f, :], start=(f == 0), stop=(f == 3))
                    i.then_inc(sem["down_mm"], 1)
                pe.wait_ge(sem["down_mm"], 8 * u + 8)
                pe.sem_inc(ring_free[sd], 1)

            def final():
                rms()
                pe.wait_ge(sem["h_done"], 1)
                for t, (t0, n) in enumerate(SPANS):
                    for half in range(2):
                        for k in range(4):
                            i = tr(PS[0:n, 2 * t + half, k * 128:(k + 1) * 128], mT[:, 4 * half + k, t0:t0 + n])
                i.then_inc(sem["rows_turned"], 1)

            for s in range(RING):
                pe.sem_inc(ring_free[s], 1)
            pre()
            barrier(pe)
            with pe.Fori(0, DEPTH) as l:
                stage_a(l)
                barrier(pe)
                stage_b()
                barrier(pe)
                stage_gla()
                barrier(pe)
                stage_ssd(l)
                barrier(pe)
                pe.sem_inc(k_free, 1)
                pe.sem_inc(v_free, 1)
                with pe.Fori(0, DB) as b:
                    seq_a(l, b)
                    seq_c(l, b)
                    barrier(pe)
                stage_out(l)
                barrier(pe)
                with pe.Fori(0, NE // 4) as it:
                    for u in range(4):
                        expert(l, it, u)
                    barrier(pe)
                barrier(pe)
            final()
            barrier(pe)

        @block.scalar
        def _(act):
            own[act] = [sem["act_step"], 0]
            def f(out, in_, func, scale=1.0, bias=None):
                if bias is None:
                    return nc.scalar.activation(out, in_, func, scale=scale)
                return nc.scalar.activation(out, in_, func, scale=scale, bias=bias)

            def copy(out, in_):
                return nc.scalar.activation(out, in_, ACT.Copy)

            def squares():
                f(v3(big, SCR, KT8, T), xT, ACT.Square).then_inc(sem["sq"], 1)

            def rsqrt(out):
                v = rv[:, :].rearrange("p (a b) -> p a b", a=2) if len(out.shape) == 3 else rv[:, 0:T]
                act.wait_ge(sem["variance"], 1)
                step(act, f(out, v, ACT.Ln))
                f(out, out, ACT.Exp, scale=-0.5).then_inc(sem["rstd"], 1)

            def pre():
                act.wait_ge(loads, LOADS_PRE)
                f(big[0:9, 5248:6272], big[0:9, 4096:5120], ACT.Exp, scale=-1.0).then_inc(sem["silu_e"], 1)

            def stage_a():
                squares()
                rsqrt(rr[:, :])
                for c in range(24):
                    act.wait_ge(sem["proj_mm"], c + 1)
                    if c < 20:
                        copy(PT[:, c, :], PS[:, c % 4, 0:T]).then_inc(sem["proj_ev"], 1)
                    else:
                        if c == 20:
                            act.wait_ge(sem["xp_done"], 1)
                        step(act, copy(XP[:, c - 20, 3:259], PS[:, c % 4, 0:256]))
                        copy(XPs[:, c - 20, :, 3:11], PS[:, c % 4, 256:T].rearrange("p (b i) -> p b i", b=DB)).then_inc(sem["proj_ev"], 1)
                act.wait_ge(sem["tail_mm"], 1)
                copy(lrT, PS[0:16, 4, 0:T])
                copy(sm[:, 0:8], PS[:, 5, 0:8])
                copy(sm[0:64, 8:12], PS[0:64, 5, 8:12])

            def stage_b():
                act.wait_ge(sem["tail27_mm"], 1)
                copy(cvo[0:27, :], PS[0:27, 4, :]).then_inc(sem["tail27_ev"], 1)
                for n, (buf, bank) in enumerate(((kA, 0), (vA, 2), (vB, 6), (kC, 4), (vC, 0))):
                    act.wait_ge(sem["tok_mm"], n + 1)
                    step(act, copy(buf[:, 0:2, :], PS[:, bank, :].rearrange("p (t c) -> p t c", t=2)))
                    copy(buf[0:64, 2, :], PS[0:64, bank + 1, 0:256]).then_inc(sem["tok_ev"], 1)
                s, t = v3(big, SCR, 4, 512), v3(big, SCR + 2048, 4, 512)
                act.wait_ge(sem["sA_cap"], 1)
                for j in range(8):
                    x = s[:, j // 2, (j % 2) * 256:(j % 2) * 256 + 256]
                    i = f(x, x, ACT.Exp, scale=HD ** -0.5, bias=sm[:, 24 + j:25 + j])
                i.then_inc(sem["eA"], 1)
                act.wait_ge(sem["tA_mm"], 1)
                copy(big[:, SCR + 4096:SCR + 6144], PSF[:, 0:2048]).then_inc(sem["tA_ev"], 1)
                act.wait_ge(sem["tA_ev"], 1)
                act.wait_ge(sem["oA_mm"], 1)
                copy(mT[:, 0:2, 0:256], PS[:, 4:6, 0:256]).then_inc(sem["oA_ev"], 1)
                act.wait_ge(sem["zC_mm"], 1)
                for h in range(4):
                    i = f(s[:, h, :], PS[:, h, :], ACT.Identity, scale=HD ** -0.5, bias=bc[:, h:h + 1])
                i.then_inc(sem["zC_ev"], 1)
                act.wait_ge(sem["zC_t"], 1)
                step(act, f(t, t, ACT.Exp, scale=-1.0))
                f(t, t, ACT.Ln, bias=1.0).then_inc(sem["zC_l"], 1)
                act.wait_ge(sem["zC_r"], 1)
                f(s, s, ACT.Exp).then_inc(sem["zC_a"], 1)
                act.wait_ge(sem["tC_mm"], 1)
                copy(big[:, SCR + 4096:SCR + 6144], PSF[:, 0:2048]).then_inc(sem["tC_ev"], 1)
                act.wait_ge(sem["oC_mm"], 1)
                copy(mT[:, 4:6, 0:256], PS[:, 4:6, 0:256])

            def stage_gla():
                G = gla
                act.wait_ge(sem["lr_mm"], 1)
                f(G.la, PS[:, 7, 0:T], ACT.Identity, bias=vec[:, 86:87]).then_inc(sem["gate_logits"], 1)
                act.wait_ge(sem["gate_abs"], 1)
                step(act, f(G.cum, G.cum, ACT.Exp, scale=-1.0))
                f(G.cum, G.cum, ACT.Ln, bias=1.0).then_inc(sem["gate_log"], 1)
                act.wait_ge(sem["gla_cum"], 1)
                f(G.ec, G.cum, ACT.Exp)
                f(G.en, G.cum, ACT.Exp, scale=-1.0)
                f(G.el, G.el, ACT.Exp).then_inc(sem["gla_exps"], 1)
                act.wait_ge(sem["gla_scores_mm"], 1)
                f(G.qgz, PT[:, GATE:GATE + 4, :], ACT.Exp, scale=-1.0).then_inc(sem["silu_exp"], 1)
                rsqrt(G.sq)

            def stage_ssd():
                D = ssd
                act.wait_ge(sem["conv_done"], 1)
                f(D.ex, D.xc, ACT.Exp, scale=-1.0).then_inc(sem["conv_exp"], 1)
                f(D.alog, bc[:, 8:12], ACT.Exp)
                f(D.u, D.tt, ACT.Exp, scale=-1.0).then_inc(sem["dt_exp"], 1)
                act.wait_ge(sem["dt_plus1"], 1)
                f(D.l, D.w1, ACT.Ln).then_inc(sem["dt_log"], 1)
                act.wait_ge(sem["ssm_in_turned"], 1)
                copy(D.st0, PSF[:, 1536:2560].rearrange("p (b n) -> p b n", b=DB)).then_inc(sem["ssm_in_copied"], 1)
                act.wait_ge(sem["decay_left"], 1)
                f(D.w, D.w, ACT.Exp).then_inc(sem["decay_left_exp"], 1)
                act.wait_ge(sem["cum_rows_mm"], 1)
                f(D.ec, PS[:, 0:4, 0:T], ACT.Exp).then_inc(sem["cum_exps"], 1)
                act.wait_ge(sem["decay_args"], 1)
                f(D.dec[:, 0:2], D.dec[:, 0:2], ACT.Exp)
                f(D.dec[0:64, 2, :, 0:64], D.dec[0:64, 2, :, 0:64], ACT.Exp).then_inc(sem["decay_exps"], 1)
                act.wait_ge(sem["ssm_turned"], 1)
                copy(D.outb, PSF[:, 0:1152]).then_inc(sem["ssm_out_copied"], 1)
                rsqrt(rr[:, :])

            def seq_a(b):
                Q = seq
                act.wait_ge(sem["a_keys_turned"], 2)
                kt = Q.kT[:, 1, 0:768].rearrange("p (a n) -> p a n", a=2)
                copy(kt, PS[:, 3:5, 0:384]).then_inc(sem["a_keys_copied_act"], 1)
                copy(Q.kT[:, 1, 768:1280], PS[:, 5, :]).then_inc(sem["a_keys_copied_act"], 1)
                act.wait_ge(sem["a_max"], 1)
                f(Q.s[:, 0:1344], Q.s[:, 0:1344], ACT.Exp, scale=HD ** -0.5, bias=sm[0:32, 24:25]).then_inc(sem["a_exp"], 1)
                act.wait_ge(sem["a_probs_turned"], 1)
                pS = v3(pS_, 0, 17, 32)
                copy(pS[0:96, 0:8, :], PS[0:96, 6, 0:256].rearrange("p (a n) -> p a n", a=8))
                copy(pS[:, 8:12, :], PS[:, 6, 256:384].rearrange("p (a n) -> p a n", a=4))
                copy(pS[0:64, 12, :], PS[0:64, 6, 384:416]).then_inc(sem["a_probs_copied"], 1)
                act.wait_ge(sem["a_out_mm"], 1)
                out(b, 0, "a_out_copied")

            def out(b, c0, name):
                for hh in range(2):
                    src = PS[64 * hh:64 * hh + 64, 7, 0:96].rearrange("p (c n) -> p c n", c=2)[:, :, 8 * hh:8 * hh + 8]
                    copy(mT[64 * hh:64 * hh + 64, c0:c0 + 2, bass.ds(SEQ + b * 8, 8)], src).then_inc(sem[name], 1)
                    act.wait_ge(sem[name], hh + 1)

            def seq_c(b):
                Q = seq
                act.wait_ge(sem["a_scores_mm"], 1)
                for n in range(0, 8, 2):
                    act.wait_ge(sem["c_keys_turned"], n + 1)
                    c, g, jh = n // 4, (n // 2) % 2, n % 2
                    copy(Q.kt8(c, g, jh), PS[:, 3 + n % 3, :].rearrange("p (j q) -> p j q", j=4)).then_inc(sem["c_keys_copied_act"], 1)
                act.wait_ge(sem["c_logits_mm"], 1)
                f(Q.s, PSF[0:32, 0:2112], ACT.Identity, scale=HD ** -0.5, bias=bsb[0:32, 0:1]).then_inc(sem["c_logits"], 1)
                act.wait_ge(sem["c_abs"], 1)
                step(act, f(Q.t, Q.t, ACT.Exp, scale=-1.0))
                f(Q.t, Q.t, ACT.Ln, bias=1.0).then_inc(sem["c_log"], 1)
                act.wait_ge(sem["c_exponents"], 1)
                f(Q.s, Q.s, ACT.Exp).then_inc(sem["c_weights"], 1)
                act.wait_ge(sem["c_weights_turned"], 1)
                pS = v3(pS_, 0, 17, 32)
                for g in range(2):
                    copy(pS[:, 8 * g:8 * g + 8, :], PS[:, 5 + g, 0:256].rearrange("p (a n) -> p a n", a=8))
                copy(pS[0:64, 16, :], PS[0:64, 5, 256:288]).then_inc(sem["c_weights_copied"], 1)
                act.wait_ge(sem["c_out_mm"], 1)
                out(b, 4, "c_out_copied")

            def stage_out():
                act.wait_ge(sem["proj_ev"], 8)
                squares()
                rsqrt(rr[:, :])
                act.wait_ge(sem["group_args"], 1)
                f(moe.gx, moe.gx, ACT.Exp).then_inc(sem["group_exps"], 1)
                act.wait_ge(sem["pair_args"], 1)
                f(moe.dx, moe.dx, ACT.Exp).then_inc(sem["pair_exps"], 1)

            def expert(u):
                M = moe
                act.wait_ge(sem["gate_mm"], u + 1)
                if u:
                    act.wait_ge(sem["hidden"], 4 * u)
                copy(M.gb, PS[:, 4, 0:T]).then_inc(sem["gate_copied"], 1)
                for ff in range(4):
                    act.wait_ge(sem["up_mm"], 4 * u + ff + 1)
                    if 4 * u + ff >= 2:
                        act.wait_ge(sem["hidden"], 4 * u + ff - 1)
                    f(M.e[:, ff % 2, :], PS[:, ff % 2, 0:T], ACT.Exp, scale=-1.0).then_inc(sem["expert_exp"], 1)

            def final():
                squares()
                rsqrt(rr[:, :])
                act.wait_ge(sem["rows_turned"], 1)
                rows = v3(big, 0, 3, 1024)
                for t, (t0, n) in enumerate(SPANS):
                    i = copy(rows[0:n, t, :].rearrange("p (a n) -> p a n", a=2), PS[0:n, 2 * t:2 * t + 2, :])
                i.then_inc(sem["rows_copied"], 1)

            pre()
            barrier(act)
            with act.Fori(0, DEPTH):
                stage_a()
                barrier(act)
                stage_b()
                barrier(act)
                stage_gla()
                barrier(act)
                stage_ssd()
                barrier(act)
                with act.Fori(0, DB) as b:
                    seq_a(b)
                    seq_c(b)
                    barrier(act)
                stage_out()
                barrier(act)
                with act.Fori(0, NE // 4):
                    for u in range(4):
                        expert(u)
                    barrier(act)
                barrier(act)
            final()
            barrier(act)

        @block.vector
        def _(dve):
            own[dve] = [sem["dve_step"], 0]
            V = nc.vector

            def c(ins):
                step(dve, ins)

            def tt(out, a, b, op):
                return V.tensor_tensor(out, a, b, op)

            def ts(out, a, s1, s2, op0, op1=None):
                return V.tensor_scalar(out, a, s1, s2, op0, op1) if op1 is not None else V.tensor_scalar(out, a, s1, None, op0)

            def stt(out, a, s, b, op0, op1):
                return V.scalar_tensor_tensor(out=out, in0=a, scalar=s, in1=b, op0=op0, op1=op1)

            M_, A_, S_ = ALU.mult, ALU.add, ALU.subtract

            def pre():
                c(V.memset(qzA_[:, :], 0.0))
                c(V.memset(qzC_[:, :], 0.0))
                c(V.memset(qb_[:, :], 0.0))
                c(V.memset(sm[:, :], 0.0))
                dve.wait_ge(loads, LOADS_PRE)
                c(V.tensor_copy(idxf[:, :], idxi[:, :]))
                c(stt(idxf[:, :], idxf[:, :], 16.0, K("sub").to_broadcast([128, 16]), M_, A_))
                dve.wait_ge(sem["silu_e"], 1)
                e, x = big[0:9, 5248:6272], big[0:9, 4096:5120]
                c(ts(e, e, 1.0, None, A_))
                c(V.reciprocal(e, e))
                tt(x, x, e, M_).then_inc(sem["rows_in"], 1)
                dve.wait_ge(sem["rows_T"], 1)
                V.tensor_copy(xT, PS[:, :, 0:T]).then_inc(sem["xp_done"], 1)
                dve.wait_ge(sem["c_T"], 1)
                V.tensor_copy(cT_[:, :], PS[:, 0, 0:72])
                V.tensor_copy(gfin[:, :], PS[:, 1, 0:8])

            def rsqrt(out, in_, n):
                v, t = (x[:, :] if len(out.shape) == 3 else x[:, 0:T] for x in (rv, rt))
                if len(out.shape) == 3:
                    v, t = (x.rearrange("p (a b) -> p a b", a=2) for x in (v, t))
                ts(v, in_, 1.0 / n, EPS, M_, A_).then_inc(sem["variance"], 1)
                dve.wait_ge(sem["variance"], 1)
                dve.wait_ge(sem["rstd"], 1)
                c(tt(t, out, out, M_))
                c(tt(t, t, v, M_))
                c(ts(t, t, -0.5, 1.5, M_, A_))
                c(tt(out, out, t, M_))

            def norm(g, shift):
                sc = v3(scaleT_, 0, 8, 9)
                c(tt(sc, modT[:, shift + 8:shift + 16, :], spread(vec[:, g:g + 8], 2, 9), M_))
                dve.wait_ge(sem["rms_mm"], 1)
                rsqrt(rr[:, :], PS[:, 1, 0:T], DM)
                c(tt(mT, xT, spread(rr[:, :], 1, KT8), M_))
                hp = mT[:, :, 0:SEQ]
                c(tt(hp, hp, sc[:, :, 0:1].to_broadcast([128, 8, SEQ]), M_))
                c(tt(hp, hp, modT[:, shift:shift + 8, 0:1].to_broadcast([128, 8, SEQ]), A_))
                hs = mT[:, :, SEQ:T].rearrange("p k (b i) -> p k b i", b=DB)
                c(tt(hs, hs, spread(sc[:, :, 1:9], 3, 8), M_))
                tt(hs, hs, spread(modT[:, shift:shift + 8, 1:9], 3, 8), A_).then_inc(sem["h_done"], 1)
                dve.wait_ge(sem["h_done"], 1)

            def stage_a():
                c(V.memset(XP[:, :, 0:3], 0.0))
                c(V.tensor_copy(idxu[:, :], idxf[:, :]))
                c(ts(idxf[:, :], idxf[:, :], float(N_POOL * 16), None, A_))
                dve.wait_ge(sem["vec_T"], 1)
                c(V.tensor_copy(vec[:, :], PS[:, 1, 0:NVEC]))
                dve.wait_ge(sem["convT_mm"], 1)
                V.tensor_copy(XPs[:, :, :, 0:3], PS[:, 2, 0:96].rearrange("p (c b k) -> p c b k", c=4, b=DB)).then_inc(sem["xp_done"], 1)
                dve.wait_ge(sem["xp_done"], 1)
                dve.wait_ge(sem["mod_mm"], 1)
                c(tt(modT, PS[:, 0, 0:432].rearrange("p (m s) -> p m s", s=9), spread(vec[:, 0:48], 2, 9), A_))
                c(ts(modT[:, 8:16, :], modT[:, 8:16, :], 1.0, None, A_))
                ts(modT[:, 32:40, :], modT[:, 32:40, :], 1.0, None, A_).then_inc(sem["mod_done"], 1)
                dve.wait_ge(sem["mod_done"], 1)
                norm(48, 0)

            def stage_b():
                tail = v3(big, SCR, 4, 27)
                c(V.tensor_copy(tail[:, :, 0:3], XP[:, :, 256:259]))
                for k in range(4):
                    i = V.tensor_copy(tail[:, k, 3:27].rearrange("p (b k) -> p b k", b=DB), XPs[:, k, :, 8:11])
                    if k < 3:
                        c(i)
                    else:
                        i.then_inc(sem["pre_T"], 1)
                        dve.wait_ge(sem["pre_T"], 1)
                dve.wait_ge(sem["turn_mm"], 1)
                t1 = v3(big, SCR + 512, 4, T)
                c(tt(t1, PS[:, 0:4, 0:T], spread(K("sin"), 1, 4), M_))
                c(tt(PT[:, 0:4, :], PT[:, 0:4, :], spread(K("cos"), 1, 4), M_))
                tt(PT[:, 0:4, :], PT[:, 0:4, :], t1, A_).then_inc(sem["rope_done"], 1)
                dve.wait_ge(sem["rope_done"], 1)
                for qz, q in ((qzA, AQ), (qzC, CQ)):
                    c(V.tensor_copy(qz[0:64, 0:4:2, :], PT[0:64, q:q + 2, :]))
                    c(V.tensor_copy(qz[64:128, 1:4:2, :], PT[64:128, q:q + 2, :]))
                c(V.tensor_copy(kS[:, 0:2, :], PT[:, AK:AK + 2, SEQ:T]))
                V.tensor_copy(kS[:, 2:4, :], PT[:, CK:CK + 2, SEQ:T]).then_inc(sem["qz_done"], 1)
                dve.wait_ge(sem["qz_done"], 1)
                s, t = v3(big, SCR, 4, 512), v3(big, SCR + 2048, 4, 512)
                s8, t8 = v3(big, SCR, 8, 256), v3(big, SCR + 2048, 8, 256)
                dve.wait_ge(sem["sA_mm"], 1)
                dve.wait_ge(sem["tail27_mm"], 1)
                c(tt(s, PS[:, 0:4, :], spread(K("cap_a"), 1, 4), ALU.min))
                c(V.tensor_reduce(sm[:, 24:32], s8, AX.X, ALU.max))
                ts(sm[:, 24:32], sm[:, 24:32], -HD ** -0.5, None, M_).then_inc(sem["sA_cap"], 1)
                dve.wait_ge(sem["sA_cap"], 1)
                dve.wait_ge(sem["eA"], 1)
                c(stt(s, spread(K("cap_a"), 1, 4), 1.0 / BIG_F, s, M_, M_))
                c(V.tensor_reduce(sm[:, 24:32], s8, AX.X, ALU.add))
                c(V.reciprocal(sm[:, 24:32], sm[:, 24:32]))
                tt(s8, s8, spread(sm[:, 24:32], 2, 256), M_).then_inc(sem["pA_done"], 1)
                dve.wait_ge(sem["pA_done"], 1)
                dve.wait_ge(sem["zC_ev"], 1)
                c(tt(s, s, spread(K("cap_c"), 1, 4), ALU.min))
                stt(t, s, -1.0, s, M_, ALU.max).then_inc(sem["zC_t"], 1)
                dve.wait_ge(sem["zC_t"], 1)
                dve.wait_ge(sem["zC_l"], 1)
                c(stt(t, s, 0.0, t, ALU.max, A_))
                for j in range(8):
                    x = t8[:, j, ::-1]
                    i = V.tensor_tensor_scan(x, K("ones256"), x, 0.0, M_, A_)
                c(i)
                tt(s, s, t, S_).then_inc(sem["zC_r"], 1)
                dve.wait_ge(sem["zC_r"], 1)

            def stage_gla(l):
                G = gla
                c(V.memset(G.qgz, 0.0))
                dve.wait_ge(sem["gate_logits"], 1)
                stt(G.cum, G.la, -1.0, G.la, M_, ALU.max).then_inc(sem["gate_abs"], 1)
                dve.wait_ge(sem["gate_abs"], 1)
                dve.wait_ge(loads, l * LOADS + LOADS_PRE + LOADS_A + LOADS_B)
                c(tt(G.st0.rearrange("p b (h v) -> p b h v", h=4), spread(G.raw, 2, 4),
                     spread(K("diag_gla").rearrange("p (h v) -> p h v", h=4), 1, DB), M_))
                dve.wait_ge(sem["gate_log"], 1)
                c(stt(G.la, G.la, 0.0, G.cum, ALU.min, S_))
                c(ts(G.la, G.la, 1.0 / 16.0, None, M_))
                c(V.tensor_tensor_scan(G.cum, K("reset"), G.la, 0.0, M_, A_))
                for a, b_, n, w in ((0, SEQ, 4, 64), (SEQ, T, 8, 8)):
                    x = G.cum[:, a:b_].rearrange("p (n w) -> p n w", w=w)
                    y = G.el[:, a:b_].rearrange("p (n w) -> p n w", w=w)
                    i = tt(y, x[:, :, w - 1:w].to_broadcast([128, n, w]), x, S_)
                    if a == 0:
                        c(i)
                    else:
                        i.then_inc(sem["gla_cum"], 1)
                        dve.wait_ge(sem["gla_cum"], 1)
                dve.wait_ge(sem["gla_exps"], 1)
                c(stt(G.qg, PT[:, BQ, :], 32 ** -0.5, G.ec, M_, M_))
                for h in range(4):
                    c(V.tensor_copy(G.qgz[32 * h:32 * h + 32, h, :], G.qg[32 * h:32 * h + 32, :]))
                c(V.tensor_copy(G.last[:, 0:4], G.ec[:, 63:SEQ:64]))
                c(V.tensor_copy(G.last[:, 4:12], G.ec[:, SEQ + 7:T:8]))
                c(tt(G.kg, PT[:, BK, :], G.en, M_))
                tt(G.kdT, PT[:, BK, :], G.el, M_).then_inc(sem["gla_operands"], 1)
                dve.wait_ge(sem["gla_operands"], 1)
                dve.wait_ge(sem["gla_scores_mm"], 1)
                for t, (t0, n) in enumerate(SPANS):
                    tri = K("tri8") if t == 2 else K("tri64")
                    c(tt(G.att[0:n, t, 0:4 * n].rearrange("p (h t) -> p h t", h=4), PS[0:n, t, 0:4 * n].rearrange("p (h t) -> p h t", h=4),
                         spread(tri[0:n, 0:n], 1, 4), M_))
                c(V.tensor_copy(G.kdt[:, 0:2, :], PS[:, 3, 0:256].rearrange("p (t n) -> p t n", t=2)))
                c(V.tensor_copy(G.kdt[0:64, 2, :], PS[0:64, 3, 256:384]))
                tt(G.kdm[0:64], spread(G.kdt[0:64, 2, :], 1, DB), spread(K("seq_of")[0:64], 2, 128), M_).then_inc(sem["gla_scores_masked"], 1)
                dve.wait_ge(sem["gla_scores_masked"], 1)
                dve.wait_ge(sem["gla_kv_mm"], 1)
                d4 = spread(K("diag_gla"), 1, 2)
                for k in range(2):
                    x = PS[:, 4 + k, :].rearrange("p (j n) -> p j n", j=2)
                    c(tt(x, x, d4, M_))
                c(V.tensor_copy(G.stp[:, 0, :], PS[:, 4, 0:256]))
                for j in range(1, 4):
                    i = stt(G.stp[:, j, :], G.stp[:, j - 1, :], G.last[:, j:j + 1], PS[:, 4 + j % 2, (j // 2) * 256:(j // 2) * 256 + 256], M_, A_)
                    if j < 3:
                        c(i)
                    else:
                        i.then_inc(sem["gla_states"], 1)
                        dve.wait_ge(sem["gla_states"], 1)
                x = PSF[:, 0:2048].rearrange("p (b n) -> p b n", b=DB)
                c(tt(x, x, spread(K("diag_gla"), 1, DB), M_))
                dve.wait_ge(sem["gla_out_mm"], 1)
                c(tt(G.st0, G.st0, spread(G.last[:, 4:12], 2, 256), M_))
                tt(G.st0, G.st0, x, A_).then_inc(sem["gla_final_states"], 1)
                dve.wait_ge(sem["gla_final_states"], 1)
                c(V.tensor_copy(G.o, PS[:, 6:8, 0:T]))
                tt(G.sq, G.o, G.o, M_).then_inc(sem["gla_squares"], 1)
                dve.wait_ge(sem["gla_squares"], 1)
                dve.wait_ge(sem["silu_exp"], 1)
                c(ts(G.qgz, G.qgz, 1.0, None, A_))
                c(V.reciprocal(G.qgz, G.qgz))
                c(tt(PT[:, GATE:GATE + 4, :], PT[:, GATE:GATE + 4, :], G.qgz, M_))
                dve.wait_ge(sem["gla_norm_mm"], 1)
                rsqrt(G.sq, PS[:, 0:2, 0:T], HD)
                c(stt(G.o, G.o, vec[:, 87:88], G.sq, M_, M_))
                c(tt(mT[:, 2:4, :], G.o, PT[:, GATE:GATE + 2, :], M_))

            def stage_ssd():
                D = ssd
                c(tt(D.v, v3(sm, 0, 3, 4), spread(bc[:, 4:8], 1, 3), A_))
                c(stt(D.tt, D.v, -1.0, D.v, M_, ALU.max))
                for k in range(4):
                    w = lambda j: vec[:, 64 + 4 * j + k:65 + 4 * j + k]
                    xp, xs = D.xc[:, k, 0:SEQ], D.xc[:, k, SEQ:T].rearrange("p (b i) -> p b i", b=DB)
                    c(ts(xp, XP[:, k, 0:256], w(0), vec[:, 80 + k:81 + k], M_, A_))
                    c(ts(xs, XPs[:, k, :, 0:8], w(0), vec[:, 80 + k:81 + k], M_, A_))
                    for j in range(1, 4):
                        c(stt(xp, XP[:, k, j:j + 256], w(j), xp, M_, A_))
                        i = stt(xs, XPs[:, k, :, j:j + 8], w(j), xs, M_, A_)
                        if (k, j) != (3, 3):
                            c(i)
                        else:
                            i.then_inc(sem["conv_done"], 1)
                            dve.wait_ge(sem["conv_done"], 1)
                c(V.memset(D.cz, 0.0))
                dve.wait_ge(sem["conv_exp"], 1)
                c(ts(D.ex, D.ex, 1.0, None, A_))
                c(V.reciprocal(D.ex, D.ex))
                c(tt(D.xc, D.xc, D.ex, M_))
                c(V.tensor_copy(D.cz[0:64, 0, :], D.xc[0:64, 3, :]))
                V.tensor_copy(D.cz[64:128, 1, :], D.xc[64:128, 3, :]).then_inc(sem["conv_silu"], 1)
                dve.wait_ge(sem["conv_silu"], 1)
                dve.wait_ge(sem["dt_exp"], 1)
                ts(D.w1, D.u, 1.0, None, A_).then_inc(sem["dt_plus1"], 1)
                dve.wait_ge(sem["dt_plus1"], 1)
                c(ts(D.d, D.w1, -1.0, None, A_))
                c(ts(D.eq, D.d, 0.0, None, ALU.is_equal))
                c(tt(D.d, D.d, D.eq, A_))
                c(V.reciprocal(D.d, D.d))
                c(tt(D.u, D.u, D.d, M_))
                dve.wait_ge(sem["dt_log"], 1)
                c(tt(D.l, D.l, D.eq, A_))
                c(tt(D.u, D.u, D.l, M_))
                c(stt(D.dt, D.v, 0.0, D.u, ALU.max, A_))
                stt(D.da, D.dt, -1.0, spread(D.alog, 1, 3), M_, M_).then_inc(sem["log_decays"], 1)
                dve.wait_ge(sem["log_decays"], 1)
                dve.wait_ge(sem["xb_turned"], 1)
                c(V.tensor_copy(D.tok[:, 0:2, :], PS[:, 0:2, 0:384]))
                c(V.tensor_copy(D.tok[0:64, 2, :], PS[0:64, 2, 0:384]))
                dve.wait_ge(sem["ssm_in_copied"], 1)
                V.tensor_copy(D.dab, spread(D.da, 3, 128)).then_inc(sem["decays_spread"], 1)
                dve.wait_ge(sem["decays_spread"], 1)
                c(V.memset(D.cum, 0.0))
                c(V.memset(D.w, 0.0))
                dve.wait_ge(sem["cum_mm"], 1)
                for n, t in ((128, slice(0, 2)), (64, slice(2, 3))):
                    cs = slice(4 * t.start, 4 * t.stop)
                    c(V.tensor_copy(D.cum[0:n, t, :].rearrange("p a b -> p (a b)"), PS[0:n, 5, cs]))
                    i = tt(D.w[0:n, t, :].rearrange("p a b -> p (a b)"), PS[0:n, 5, 16 + cs.start:16 + cs.stop], D.cum[0:n, t, :].rearrange("p a b -> p (a b)"), S_)
                    if n == 128:
                        c(i)
                    else:
                        i.then_inc(sem["decay_left"], 1)
                        dve.wait_ge(sem["decay_left"], 1)
                dve.wait_ge(sem["cum_exps"], 1)
                for t, (t0, n) in enumerate(SPANS):
                    d = D.dec[0:n, t, :, 0:n]
                    tri = K("tri8c") if t == 2 else K("tri64c")
                    c(tt(d, PS[0:n, 0:4, t0:t0 + n], spread(D.cum[0:n, t, :], 2, n), S_))
                    i = tt(d, d, spread(tri[0:n, 0:n], 1, 4), ALU.min)
                    if t < 2:
                        c(i)
                    else:
                        i.then_inc(sem["decay_args"], 1)
                        dve.wait_ge(sem["decay_args"], 1)
                dve.wait_ge(sem["decay_left_exp"], 1)
                for n, t in ((128, slice(0, 2)), (64, slice(2, 3))):
                    k = t.stop - t.start
                    x = D.tok[0:n, t, 0:256].rearrange("p t (h q) -> p t h q", h=4)
                    xd, xw = (v[0:n, t, :].rearrange("p t (h q) -> p t h q", h=4) for v in (D.xdt, D.xw))
                    c(tt(xd, x, spread(D.dt[0:n, t, :], 3, 64), M_))
                    c(tt(xw, xd, spread(D.w[0:n, t, :], 3, 64), M_))
                c(tt(D.bm[0:64], spread(D.tok[0:64, 2, 256:384], 1, DB), spread(K("seq_of")[0:64], 2, 128), M_))
                dve.wait_ge(sem["cum_exps"], 1)
                tt(D.ce.rearrange("p (g x) t -> p g x t", g=2), spread(D.cz, 2, 2), D.ec.rearrange("p (g x) t -> p g x t", g=2), M_).then_inc(sem["ssd_operands"], 1)
                dve.wait_ge(sem["ssd_operands"], 1)
                for g in range(2):
                    r = slice(64 * g, 64 * g + 64)
                    c(V.tensor_copy(D.last[r, 0:4, :].rearrange("p j h -> p h j"), D.ec[r, 2 * g:2 * g + 2, 63:SEQ:64]))
                    c(V.tensor_copy(D.last[r, 4:12, :].rearrange("p j h -> p h j"), D.ec[r, 2 * g:2 * g + 2, SEQ + 7:T:8]))
                dve.wait_ge(sem["decay_exps"], 1)
                dve.wait_ge(sem["cb_sample_mm"], 1)
                for t, (t0, n) in enumerate(SPANS):
                    bank = (6, 7, 4)[t]
                    d = D.dec[0:n, t, :, 0:n].rearrange("p (g x) t -> p g x t", g=2)
                    c(tt(d, d, spread(PS[0:n, bank, 0:2 * n].rearrange("p (g t) -> p g t", g=2), 2, 2), M_))
                dve.wait_ge(sem["bx_mm"], 1)
                hp = lambda x: x.rearrange("p (h q) -> p h q", h=2)
                c(V.tensor_copy(D.stp[:, 0, :], PS[:, 0, 0:128]))
                for j in range(1, 4):
                    c(tt(hp(D.stp[:, j, :]), hp(D.stp[:, j - 1, :]), spread(D.last[:, j, :], 2, 64), M_))
                    i = tt(D.stp[:, j, :], D.stp[:, j, :], PS[:, j % 2, (j // 2) * 128:(j // 2) * 128 + 128], A_)
                    if j < 3:
                        c(i)
                    else:
                        i.then_inc(sem["ssm_states"], 1)
                        dve.wait_ge(sem["ssm_states"], 1)
                dve.wait_ge(sem["ssd_out_mm"], 1)
                c(tt(D.st0.rearrange("p b (h q) -> p b h q", h=2), D.st0.rearrange("p b (h q) -> p b h q", h=2),
                     spread(D.last[:, 4:12, :], 3, 64), M_))
                tt(D.st0, D.st0, PSF[:, 1024:2048].rearrange("p (b n) -> p b n", b=DB), A_).then_inc(sem["ssm_final"], 1)
                dve.wait_ge(sem["ssm_final"], 1)
                c(V.tensor_copy(D.dsk[0:64, :], bc[0:64, 12:16:2]))
                c(V.tensor_copy(D.dsk[64:128, :], bc[64:128, 13:16:2]))
                for k in range(2):
                    c(stt(D.y[:, k, :], D.xc[:, k, :], D.dsk[:, k:k + 1], PS[:, 6 + k, 0:T], M_, A_))
                c(tt(D.y, D.y, PT[:, Z:Z + 2, :], M_))
                tt(D.sq, D.y, D.y, M_).then_inc(sem["ssd_squares"], 1)
                dve.wait_ge(sem["ssd_squares"], 1)
                dve.wait_ge(sem["ssd_norm_mm"], 1)
                rsqrt(rr[:, :], PS[:, 3, 0:T], 256)
                for k in range(2):
                    c(stt(mT[:, 6 + k, :], D.y[:, k, :], vec[:, 84 + k:85 + k], rr[:, :], M_, M_))

            def queries(qz, b, name):
                qb = v3(qb_, 0, 2, 32)
                for k in range(2):
                    i = V.tensor_copy(qb[:, k, 16 * k:16 * k + 16].rearrange("p (h i) -> p h i", h=2),
                                      qz[:, 2 * k:2 * k + 2, bass.ds(SEQ + b * 8, 8)])
                    if k == 0:
                        c(i)
                    else:
                        i.then_inc(sem[name], 1)
                        dve.wait_ge(sem[name], 1)

            def seq_a(b):
                Q = seq
                queries(qzA, b, "a_queries")
                dve.wait_ge(sem["a_keys_turned"], 1)
                kt = Q.kT[:, 0, 0:768].rearrange("p (a n) -> p a n", a=2)
                V.tensor_copy(kt, PS[:, 0:2, 0:384]).then_inc(sem["a_keys_copied_dve"], 1)
                V.tensor_copy(Q.kT[:, 0, 768:1280], PS[:, 2, :]).then_inc(sem["a_keys_copied_dve"], 1)
                dve.wait_ge(sem["a_scores_mm"], 1)
                new = K("cap_na", 32)[:, bass.ds(b * NS, NS)]
                c(tt(Q.s[:, 0:NA], PSF[0:32, 0:NA], K("cap_sa", 32), ALU.min))
                c(tt(Q.s[:, NA:NA + NS], PSF[0:32, NA:NA + NS], new, ALU.min))
                c(V.tensor_reduce(sm[0:32, 24:25], Q.s[:, 0:NA + NS], AX.X, ALU.max))
                ts(sm[0:32, 24:25], sm[0:32, 24:25], -HD ** -0.5, None, M_).then_inc(sem["a_max"], 1)
                dve.wait_ge(sem["a_max"], 1)
                queries(qzC, b, "c_queries")
                dve.wait_ge(sem["a_exp"], 1)
                c(stt(Q.s[:, 0:NA], K("cap_sa", 32), 1.0 / BIG_F, Q.s[:, 0:NA], M_, M_))
                c(stt(Q.s[:, NA:NA + NS], new, 1.0 / BIG_F, Q.s[:, NA:NA + NS], M_, M_))
                c(V.tensor_reduce(sm[0:32, 25:26], Q.s[:, 0:NA + NS], AX.X, ALU.add))
                c(V.reciprocal(sm[0:32, 25:26], sm[0:32, 25:26]))
                ts(Q.s[:, 0:NA + NS], Q.s[:, 0:NA + NS], sm[0:32, 25:26], None, M_).then_inc(sem["a_probs"], 1)
                dve.wait_ge(sem["a_probs"], 1)

            def seq_c(b):
                Q = seq
                for n in range(1, 8, 2):
                    dve.wait_ge(sem["c_keys_turned"], n + 1)
                    k, g, jh = n // 4, (n // 2) % 2, n % 2
                    V.tensor_copy(Q.kt8(k, g, jh), PS[:, 3 + n % 3, :].rearrange("p (j q) -> p j q", j=4)).then_inc(sem["c_keys_copied_dve"], 1)
                dve.wait_ge(sem["c_logits"], 1)
                x = Q.s[:, 2048:2112]
                c(tt(x, x, K("cap_nc", 32)[:, bass.ds(b * NS, NS)], ALU.min))
                stt(Q.t, Q.s, -1.0, Q.s, M_, ALU.max).then_inc(sem["c_abs"], 1)
                dve.wait_ge(sem["c_abs"], 1)
                dve.wait_ge(sem["c_log"], 1)
                c(stt(Q.t, Q.s, 0.0, Q.t, ALU.max, A_))
                x = Q.t[:, ::-1]
                c(V.tensor_tensor_scan(x, K("ones1", 32).to_broadcast([32, 2112]), x, 0.0, M_, A_))
                tt(Q.s, Q.s, Q.t, S_).then_inc(sem["c_exponents"], 1)
                dve.wait_ge(sem["c_exponents"], 1)

            def stage_out():
                c(V.memset(moe.y, 0.0))
                c(V.memset(moe.L, 0.0))
                tmp = rr[:, 0:64].rearrange("p (b i) -> p b i", b=DB)
                for k in range(8):
                    dve.wait_ge(sem["proj_mm"], k + 1)
                    o = PS[:, 4 + k % 4, 0:T]
                    c(stt(xT[:, k, 0:SEQ], o[:, 0:SEQ], modT[:, 16 + k, 0:1], xT[:, k, 0:SEQ], M_, A_))
                    c(tt(tmp, o[:, SEQ:T].rearrange("p (b i) -> p b i", b=DB), spread(modT[:, 16 + k, 1:9], 2, 8), M_))
                    tt(xT[:, k, SEQ:T], xT[:, k, SEQ:T], rr[:, 0:64], A_).then_inc(sem["proj_ev"], 1)
                    dve.wait_ge(sem["proj_ev"], k + 1)
                norm(56, 24)
                Mo = moe
                dve.wait_ge(sem["router_mm"], 1)
                for n, t in ((128, slice(0, 2)), (64, slice(2, 3))):
                    k = t.stop - t.start
                    c(tt(Mo.L[0:n, t, :], PS[0:n, 2, 36 * t.start:36 * t.stop].rearrange("p (t n) -> p t n", n=36),
                         spread(bc[0:n, 16:52], 1, k), A_))
                gl, el = Mo.L[:, :, 0:4], Mo.L[:, :, 4:36].rearrange("p t (g e) -> p t g e", g=4)

                def first_max(values, mx, hot, n):
                    tmp = Mo.tmp[:, :, 0:n]
                    c(V.tensor_reduce(mx, values, AX.X, ALU.max))
                    c(tt(tmp, values, spread(mx, 2, n), ALU.is_equal))
                    c(tt(tmp, tmp, spread(K("rev")[:, 0:n], 1, 3), M_))
                    c(V.tensor_reduce(Mo.km, tmp, AX.X, ALU.max))
                    c(tt(hot, tmp, spread(Mo.km, 2, n), ALU.is_equal))

                first_max(gl, Mo.gmax, Mo.ghot, 4)
                tt(Mo.gx, gl, spread(Mo.gmax, 2, 4), S_).then_inc(sem["group_args"], 1)
                dve.wait_ge(sem["group_args"], 1)
                c(tt(Mo.gt4, el, spread(Mo.ghot, 3, 8), M_))
                c(V.tensor_reduce(Mo.e8, Mo.gt4.rearrange("p t g e -> p t e g"), AX.X, ALU.add))
                first_max(Mo.e8, Mo.m1, Mo.h1, 8)
                c(stt(Mo.e8, Mo.h1, NEG, Mo.e8, M_, A_))
                first_max(Mo.e8, Mo.m2, Mo.h2, 8)
                tt(Mo.dx, Mo.m2, Mo.m1, S_).then_inc(sem["pair_args"], 1)
                dve.wait_ge(sem["pair_args"], 1)
                dve.wait_ge(sem["group_exps"], 1)
                c(V.tensor_reduce(Mo.gp, Mo.gx, AX.X, ALU.add))
                dve.wait_ge(sem["pair_exps"], 1)
                c(ts(Mo.m1, Mo.dx, 1.0, None, A_))
                c(tt(Mo.m1, Mo.m1, Mo.gp, M_))
                c(V.reciprocal(Mo.m1, Mo.m1))
                c(tt(Mo.m2, Mo.m1, Mo.dx, M_))
                c(tt(Mo.h1, Mo.h1, spread(Mo.m1, 2, 8), M_))
                c(tt(Mo.h2, Mo.h2, spread(Mo.m2, 2, 8), M_))
                c(tt(Mo.h1, Mo.h1, Mo.h2, A_))
                tt(Mo.gt4, spread(Mo.ghot, 3, 8), spread(Mo.h1, 2, 4), M_).then_inc(sem["gates_done"], 1)
                dve.wait_ge(sem["gates_done"], 1)
                dve.wait_ge(sem["gates_turned"], 1)
                c(V.tensor_copy(Mo.gT[0:32, :], PS[0:32, 3, 0:T]))

            def expert(it, u):
                Mo = moe
                if u:
                    dve.wait_ge(sem["gate_mm"], u)
                ts(Mo.gm[0:32, :], Mo.gT[0:32, :], ident[0:32, bass.ds(it * 4 + u, 1)], None, M_).then_inc(sem["gate_row"], 1)
                dve.wait_ge(sem["gate_copied"], u + 1)
                for ff in range(4):
                    e = Mo.e[:, ff % 2, :]
                    dve.wait_ge(sem["expert_exp"], 4 * u + ff + 1)
                    if u:
                        dve.wait_ge(sem["down_mm"], 8 * u)
                    c(ts(e, e, 1.0, None, A_))
                    c(V.reciprocal(e, e))
                    c(tt(e, e, PS[:, ff % 2, 0:T], M_))
                    c(tt(e, e, PS[:, 2 + ff % 2, 0:T], M_))
                    tt(Mo.a[:, ff, :], e, Mo.gb, M_).then_inc(sem["hidden"], 1)
                    dve.wait_ge(sem["hidden"], 4 * u + ff + 1)
                for d in range(8):
                    dve.wait_ge(sem["down_mm"], 8 * u + d + 1)
                    tt(Mo.y[:, d, :], Mo.y[:, d, :], PS[:, 4 + d % 4, 0:T], A_).then_inc(sem["down_added"], 1)

            def add_moe():
                y = moe.y
                c(tt(y[:, :, 0:SEQ], y[:, :, 0:SEQ], modT[:, 40:48, 0:1].to_broadcast([128, 8, SEQ]), M_))
                ys = y[:, :, SEQ:T].rearrange("p k (b i) -> p k b i", b=DB)
                c(tt(ys, ys, spread(modT[:, 40:48, 1:9], 3, 8), M_))
                c(tt(xT, xT, y, A_))

            def final():
                dve.wait_ge(sem["rms_mm"], 1)
                rsqrt(rr[:, :], PS[:, 1, 0:T], DM)
                c(tt(mT, xT, spread(rr[:, :], 1, KT8), M_))
                tt(mT, mT, spread(gfin[:, :], 2, T), M_).then_inc(sem["h_done"], 1)
                dve.wait_ge(sem["h_done"], 1)

            pre()
            barrier(dve)
            with dve.Fori(0, DEPTH) as l:
                stage_a()
                barrier(dve)
                stage_b()
                barrier(dve)
                stage_gla(l)
                barrier(dve)
                stage_ssd()
                barrier(dve)
                with dve.Fori(0, DB) as b:
                    seq_a(b)
                    seq_c(b)
                    barrier(dve)
                stage_out()
                barrier(dve)
                with dve.Fori(0, NE // 4) as it:
                    for u in range(4):
                        expert(it, u)
                    barrier(dve)
                add_moe()
                barrier(dve)
            final()
            barrier(dve)

        @block.gpsimd
        def _(pool):
            own[pool] = [sem["pool_step"], 0]
            def dma(out, in_, sem):
                pool.dma_start(out, in_).then_inc(sem, 16)

            def pre():
                dma(cst[:, :], consts, loads)
                rows = v3(big, 0, 3, 1024)
                dma(rows[:, 0:2, :], x_rows[0:256].rearrange("(t p) c -> p t c", p=128), loads)
                dma(rows[0:64, 2, :], x_rows[256:T], loads)
                dma(big[0:9, 4096:5120], c_rows, loads)
                dma(big[0:8, 5120:5248], g_final.rearrange("(k p) -> k p", p=128), loads)
                for t in range(8):
                    src = pages.rearrange("b (g t) -> t (b g)", t=8)[t:t + 1, :]
                    pool.dma_start(idxi[16 * t:16 * t + 16, :], src.to_broadcast([16, 16]), allow_slow_non_contiguous=True).then_inc(loads, 16)
                pool.wait_ge(loads, LOADS_PRE)

            def stage_a(l):
                dma(vrow[0:NVEC, :], vecs[l], loads)
                dma(bc[:, :], bcs[bass.ds(l, 1), :].to_broadcast([128, 52]), loads)
                for h in range(4):
                    dma(bsb[8 * h:8 * h + 8, :], b_sb[bass.ds(l, 1), h:h + 1].to_broadcast([8, 1]), loads)
                dma(wtail, w_tail[l].rearrange("(k p) n -> p k n", p=128), loads)
                dma(wr, w_router[l].rearrange("(k p) n -> p k n", p=128), loads)
                dma(wa2[0:16, :], w_a2[l], loads)
                dma(big[0:24, SCR + 2560:SCR + 3072], st_conv[l].rearrange("b k c -> (b k) c"), loads)
                pool.wait_ge(loads, l * LOADS + LOADS_PRE + LOADS_A)

            def stage_b(l):
                pool.wait_ge(sem["tail27_ev"], 1)
                dma(cv_p[l, 0], cvo[0:3, :], outputs)
                dma(cv_s[l].rearrange("b k c -> (b k) c"), cvo[3:27, :], outputs)
                for n, (buf, op, os) in enumerate(((kA, wk_p, wk_s), (vA, wv_p, wv_s), (None, None, None), (kC, sk_p, sk_s), (vC, sv_p, sv_s))):
                    if buf is None:
                        continue
                    pool.wait_ge(sem["tok_ev"], n + 1)
                    dma(op[l].rearrange("(t p) c -> p t c", p=128), buf[:, 0:2, :], outputs)
                    dma(os[l], buf[0:64, 2, :], outputs)
                pool.wait_ge(outputs, l * OUTS + OUTS_B)

            def stage_gla(l):
                G = gla
                dma(G.raw, st_gla[l].rearrange("b h k v -> (h k) b v"), loads)
                pool.wait_ge(sem["gla_final_states"], 1)
                for h in range(4):
                    dma(gla_p[l, 0, h], G.stp[32 * h:32 * h + 32, 3, 64 * h:64 * h + 64], outputs)
                    dma(gla_s[l, :, h].rearrange("b k v -> k b v"), G.st0[32 * h:32 * h + 32, :, 64 * h:64 * h + 64], outputs)
                pool.wait_ge(outputs, l * OUTS + OUTS_B + OUTS_G)

            def stage_ssd(l):
                D = ssd
                for g in range(2):
                    dma(D.raw[:, :, 64 * g:64 * g + 64], st_ssm[l, :, 2 * g:2 * g + 2].rearrange("b h p n -> (h p) b n"), loads)
                pool.wait_ge(sem["ssm_out_copied"], 1)
                ob = D.outb.rearrange("p (j n) -> p j n", j=9)
                for g in range(2):
                    dma(ssm_p[l, 0, 2 * g:2 * g + 2].rearrange("h p n -> (h p) n"), ob[:, 0, 64 * g:64 * g + 64], outputs)
                    dma(ssm_s[l, :, 2 * g:2 * g + 2].rearrange("b h p n -> (h p) b n"), ob[:, 1:9, 64 * g:64 * g + 64], outputs)
                pool.wait_ge(outputs, l * OUTS + OUTS)

            def gather(cache, off, sem):
                for g in range(2):
                    i = pool.indirect_dma_start(
                        out=big[:, off + 2048 * g:off + 2048 * g + 2048], out_offset=None, in_=cache,
                        in_offset=bass.IndirectOffsetOnAxis(ap=idxb[:, g:g + 1], axis=0))
                    i.then_inc(sem, 16)

            def seq_step(l, b):
                step(pool, nc.gpsimd.tensor_copy(idxb[:, :], idxu[:, bass.ds(b * 2, 2)]))
                pool.wait_ge(sem["a_keys_turned"], 2)
                gather(sb_k, 0, gathered_k)
                pool.wait_ge(sem["a_out_mm"], 1)
                gather(sb_v, 4096, gathered_v)
                pool.wait_ge(gathered_k, (l * DB + b + 1) * 32)
                pool.wait_ge(gathered_v, (l * DB + b + 1) * 32)

            def final():
                pool.wait_ge(sem["rows_copied"], 1)
                rows = v3(big, 0, 3, 1024)
                dma(y_p.rearrange("(t p) c -> p t c", p=128), rows[:, 0:2, :], outputs)
                dma(y_s, rows[0:64, 2, :], outputs)
                pool.wait_ge(outputs, DEPTH * OUTS + 32)

            pre()
            barrier_lead(pool)
            with pool.Fori(0, DEPTH) as l:
                for stage in (stage_a, stage_b, stage_gla, stage_ssd):
                    stage(l)
                    barrier_lead(pool)
                with pool.Fori(0, DB) as b:
                    seq_step(l, b)
                    barrier_lead(pool)
                barrier_lead(pool)
                with pool.Fori(0, NE // 4):
                    barrier_lead(pool)
                barrier_lead(pool)
            final()
            barrier_lead(pool)


def kernel(x_prompt, x_sample, cache_win_k, cache_win_v, cache_sb_k, cache_sb_v, state_gla, state_ssm, state_conv,
           page_table, c_prompt, c_sample, w_ada, b_ada, g_norm1, g_norm2, w_in, w_gla_a2, b_gla_a, g_gla, b_sb,
           w_conv, b_conv, dt_bias, a_log, d_skip, g_ssm, w_out, w_router_grp, b_router_grp, w_router_exp,
           b_router_exp, w_exp_gate, w_exp_up, w_exp_down, g_final):
    import concourse.bacc as bacc
    from concourse.bass_utils import run_bass_kernel_spmd

    a = {k: np.asarray(v) for k, v in locals().items() if k not in ("bacc", "run_bass_kernel_spmd")}
    L = DEPTH
    cols = np.split(a["w_in"], np.cumsum([256, 256, 256, 128, 128, 256, 16, 256, 256, 256, 256, 256, 512])[:13].tolist(), axis=-1)
    aq, ak, av, bq, bk, bv, lr, gate, cq, ck, cv, z, xbc, dt = cols
    vec = np.concatenate([a["b_ada"], a["g_norm1"], a["g_norm2"], a["w_conv"].reshape(L, -1), a["b_conv"], a["g_ssm"],
                          a["b_gla_a"], a["g_gla"], a["g_gla"]], axis=-1).reshape(L, NVEC, 128)
    ins = {
        "x_rows": np.concatenate([a["x_prompt"].reshape(-1, DM), a["x_sample"].reshape(-1, DM)]),
        "c_rows": np.concatenate([a["c_prompt"], a["c_sample"]]),
        "win_k": a["cache_win_k"].reshape(L, DB, PAST, 256), "win_v": a["cache_win_v"].reshape(L, DB, PAST, 256),
        "sb_k": a["cache_sb_k"].reshape(L * N_POOL * 16, 2048), "sb_v": a["cache_sb_v"].reshape(L * N_POOL * 16, 2048),
        "st_gla": a["state_gla"], "st_ssm": a["state_ssm"], "st_conv": a["state_conv"], "pages": a["page_table"],
        "w_ada": a["w_ada"], "vecs": vec,
        "w_in": np.concatenate([aq, ak, av, bq, bk, bv, cq, ck, cv, gate, z, xbc], axis=-1),
        "w_tail": np.concatenate([lr, dt], axis=-1), "w_a2": a["w_gla_a2"],
        "bcs": np.concatenate([a["b_sb"], a["dt_bias"], a["a_log"], a["d_skip"], a["b_router_grp"], a["b_router_exp"]], axis=-1),
        "b_sb": a["b_sb"], "w_out": a["w_out"],
        "w_router": np.concatenate([a["w_router_grp"], a["w_router_exp"]], axis=-1),
        "w_gate": a["w_exp_gate"], "w_up": a["w_exp_up"], "w_down": a["w_exp_down"], "g_final": a["g_final"],
        "consts": np.concatenate(list(CONST.values()), axis=1),
    }
    outs = [("y_p", (SEQ, DM)), ("y_s", (NS, DM)), ("wk_p", (L, SEQ, 256)), ("wv_p", (L, SEQ, 256)), ("wk_s", (L, NS, 256)),
            ("wv_s", (L, NS, 256)), ("sk_p", (L, SEQ, 256)), ("sv_p", (L, SEQ, 256)), ("sk_s", (L, NS, 256)),
            ("sv_s", (L, NS, 256)), ("gla_p", (L, 1, NH, 32, 64)), ("gla_s", (L, DB, NH, 32, 64)),
            ("ssm_p", (L, 1, NH, 64, 64)), ("ssm_s", (L, DB, NH, 64, 64)), ("cv_p", (L, 1, 3, CONV_CH)), ("cv_s", (L, DB, 3, CONV_CH))]
    nc = bacc.Bacc("TRN2", target_bir_lowering=False, num_devices=1)
    args, arrays = [], {}
    for name, x in ins.items():
        arrays["in_" + name] = np.ascontiguousarray(x)
        args.append(nc.dram_tensor("in_" + name, x.shape, mybir.dt.from_np(x.dtype), kind="ExternalInput").ap())
    for name, shape in outs:
        args.append(nc.dram_tensor("out_" + name, shape, F32, kind="ExternalOutput").ap())
    trunk(nc, *args)
    r = run_bass_kernel_spmd(nc, [arrays], core_ids=[0]).results[0]
    g = {n: r["out_" + n] for n, _ in outs}
    heads = (NH, HD)
    return (g["y_p"].reshape(1, SEQ, DM), g["y_s"].reshape(DB, DS, DM),
            g["wk_p"].reshape(L, 1, SEQ, *heads), g["wv_p"].reshape(L, 1, SEQ, *heads),
            g["wk_s"].reshape(L, DB, DS, *heads), g["wv_s"].reshape(L, DB, DS, *heads),
            g["sk_p"].reshape(L, 1, SEQ // PAGE, PAGE, *heads), g["sv_p"].reshape(L, 1, SEQ // PAGE, PAGE, *heads),
            g["sk_s"].reshape(L, DB, DS, *heads), g["sv_s"].reshape(L, DB, DS, *heads),
            g["gla_p"], g["gla_s"], g["ssm_p"], g["ssm_s"], g["cv_p"], g["cv_s"])
```

```python
from contextlib import ExitStack

import numpy as np

import concourse.bass as bass
from concourse import mybir

F32, I32, U32 = mybir.dt.float32, mybir.dt.int32, mybir.dt.uint32
ALU, ACT, AX = mybir.AluOpType, mybir.ActivationFunctionType, mybir.AxisListType

DM, SEQ, DEPTH, DB, DS, PAST, PAGE = 1024, 256, 2, 8, 8, 2048, 128
KT8 = DM // 128
NS = DB * DS
T = SEQ + NS
SPANS = ((0, 128), (128, 128), (256, 64))
NH, HD = 4, 64
N_POOL = DB * (PAST // PAGE) * 5 // 4
NE, FE = 32, 512
CONV_CH = 512
EPS = 1e-6
BIG_F = float(2.0 ** 100)
NEG = -1e30
ROPE_DIM, THETA = 16, 500000.0
AQ, AK, AV, BQ, BK, BV, CQ, CK, CV, GATE, Z, XBC = 0, 2, 4, 6, 7, 8, 10, 12, 14, 16, 18, 20
RING = 4
CHUNKS = 12 + 6 + 2 + 3 * NE
PER_SLOT = CHUNKS // RING
NA1, NA = 768, 1280
SLOTS, GE = 64, 4
GATE_AT, UP_AT, DOWN_AT = (0, 1, 4, 5), (2, 3, 6, 7), (8, 9, 10, 11)
NVEC = 88


def constants():
    out = {}
    p = np.arange(128)
    out["ident"] = np.eye(128)
    half = ROPE_DIM // 2
    freq = np.exp(-np.log(THETA) * np.arange(half, dtype=np.float32) * np.float32(2.0 / ROPE_DIM)).astype(np.float32)
    pos = np.concatenate([np.arange(SEQ), np.tile(PAST + np.arange(DS), DB)]).astype(np.float32)
    ang = (pos[None, :] * freq[:, None]).astype(np.float32)
    cos, sin = np.ones((128, T)), np.zeros((128, T))
    turn = np.zeros((128, 128))
    for base in (0, 64):
        for d in range(half):
            cos[base + d] = cos[base + half + d] = np.cos(ang[d].astype(np.float64))
            sin[base + d] = sin[base + half + d] = np.sin(ang[d].astype(np.float64))
            turn[base + half + d, base + d] = -1
            turn[base + d, base + half + d] = 1
    out["cos"], out["sin"], out["turn"] = cos, sin, turn

    def mult(dist):
        return sum(((dist >= 0) & (dist <= w) & (dist % d == 0)).astype(int) for w, d in ((128, 1), (512, 4), (2048, 16)))

    def cap(m):
        return np.where(m == 0, NEG, m * BIG_F)

    q = np.stack([p, p + 128], 1)[:, :, None]
    k = np.arange(SEQ)[None, None, :]
    out["cap_a"] = cap(mult(q - k)).reshape(128, -1)
    out["cap_c"] = cap((k < q).astype(int)).reshape(128, -1)
    qs = (PAST + np.arange(32) % DS)[:, None]
    far = np.concatenate([16 * np.arange(96) + r for r in range(8)])
    near = np.concatenate([1536 + 4 * p + j for j in range(4)])
    rows = np.zeros((128, NA))
    rows[:32] = cap(mult(qs - np.concatenate([far, near])[None, :]))
    out["cap_sa"] = rows
    b = np.arange(DB)[None, :, None, None]
    bb, j = np.arange(DB)[None, None, :, None], np.arange(DS)[None, None, None, :]
    i = (np.arange(32) % DS)[:, None, None, None]
    for name, ok in (("cap_na", mult(i - j) * (b == bb)), ("cap_nc", (j < i) * (b == bb) * 1)):
        rows = np.zeros((128, DB * NS))
        rows[:32] = cap(ok).reshape(32, -1)
        out[name] = rows
    s, t = p[:, None], p[None, :]
    for name, c in (("tri64", 64), ("tri8", 8)):
        out[name] = ((s // c == t // c) & (s <= t)).astype(int)
        out[name + "c"] = np.where(out[name] == 0, NEG, BIG_F)
    out["blk64"] = s // 64 == t // 64
    out["blk8"] = s // 8 == t // 8
    out["diag_gla"] = (s // 32) == (np.arange(256)[None, :] // 64)
    out["ones"] = np.ones((128, 128))
    out["seq_of"] = (p[:, None] // 8) == np.arange(8)[None, :]
    out["before"] = s < t
    out["iota"] = np.tile(np.arange(SLOTS), (128, 1))
    out["ones1"] = np.ones((128, 1))
    out["rev"] = np.tile(np.arange(8, 0, -1), (128, 1))
    reset = np.ones((128, T))
    reset[:, 0:SEQ:64] = 0
    reset[:, SEQ::8] = 0
    out["reset"] = reset
    out["sub"] = (p % 16)[:, None]
    return {n: np.ascontiguousarray(v, np.float32) for n, v in out.items()}


CONST = constants()
COFF, at = {}, 0
for _n, _v in CONST.items():
    COFF[_n] = (at, _v.shape[1])
    at += _v.shape[1]
NCONST = at


def trunk(nc, x_rows, c_rows, win_k, win_v, sb_k, sb_v, st_gla, st_ssm, st_conv, pages, w_ada, vecs, w_in,
          w_tail, w_a2, bcs, b_sb, w_out, w_router, w_gate, w_up, w_down, g_final, consts,
          y_p, y_s, wk_p, wv_p, wk_s, wv_s, sk_p, sv_p, sk_s, sv_s, gla_p, gla_s, ssm_p, ssm_s, cv_p, cv_s):
    with ExitStack() as ctx:
        def sb(name, n, dt=F32):
            return ctx.enter_context(nc.sbuf_tensor(name, [128, n], dt))

        cst = sb("cst", NCONST)

        def K(name, parts=128):
            o, n = COFF[name]
            return cst[0:parts, o:o + n]

        ring = [sb(f"ring{i}", 4096) for i in range(RING)]
        xT_ = sb("xT", KT8 * T)
        mT_ = sb("mT", KT8 * T)
        modT_ = sb("modT", 48 * 9)
        scaleT_ = sb("scaleT", 8 * 9)
        cT_ = sb("cT", 8 * 9)
        vec = sb("vec", NVEC)
        vrow = sb("vrow", 128)
        bc = sb("bc", 52)
        gfin = sb("gfin", 8)
        wtail_ = sb("wtail", 8 * 20)
        wr_ = sb("wr", 8 * 36)
        wa2 = sb("wa2", 128)
        bsb = sb("bsb", 1)
        qzA_ = sb("qzA", 4 * T)
        qzC_ = sb("qzC", 4 * T)
        vA_ = sb("vA", 3 * 256)
        vC_ = sb("vC", 3 * 256)
        kS_ = sb("kS", 4 * NS)
        qb_ = sb("qb", 2 * 32)
        pS_ = sb("pS", 17 * 32)
        idxf = sb("idxf", 16)
        idxi = sb("idxi", 16, I32)
        idxu = sb("idxu", 16, U32)
        rr = sb("rr", T)
        rv, rt = sb("rv", 2 * T), sb("rt", 2 * T)
        sm = sb("sm", 64)
        big = sb("big", 16896)
        PS = ctx.enter_context(nc.psum_tensor("PS", [128, 8, 512], F32))
        PSF = PS[:, :, :].rearrange("p b n -> p (b n)")

        def v3(t, off, a, b, parts=128):
            return t[0:parts, off:off + a * b].rearrange("p (a b) -> p a b", a=a)

        def v4(t, off, a, b, c, parts=128):
            return t[0:parts, off:off + a * b * c].rearrange("p (a b c) -> p a b c", a=a, b=b)

        def spread(ap, axis, n):
            u = ap.unsqueeze(axis)
            shape = list(u.shape)
            shape[axis] = n
            return u.to_broadcast(shape)

        xT, mT = v3(xT_, 0, KT8, T), v3(mT_, 0, KT8, T)
        modT = v3(modT_, 0, 48, 9)
        wtail, wr = v3(wtail_, 0, 8, 20), v3(wr_, 0, 8, 36)
        qzA, qzC = v3(qzA_, 0, 4, T), v3(qzC_, 0, 4, T)
        vA, vC = v3(vA_, 0, 3, 256), v3(vC_, 0, 3, 256)
        kS = v3(kS_, 0, 4, NS)
        ident, ones = K("ident"), K("ones")
        SCR = 10412
        PT = v3(big, 0, 20, T)
        lrT = big[0:16, 6400:6720]
        XP = v3(big, 6720, 4, 347)
        XPs = XP[:, :, 259:347].rearrange("p c (b k) -> p c b k", b=DB)
        kA, kC, vB = v3(big, 8108, 3, 256), v3(big, 8876, 3, 256), v3(big, 9644, 3, 256)

        def ring3(s, a):
            return v3(ring[s], 0, a, 4096 // a)

        cvo = rv[:, 0:512]
        idxb = sb("idxb", 2, U32)
        crowded = sb("crowded", 1, I32)
        L3 = lambda off, a, b: v3(big, off, a, b)
        class gla:
            cum = big[:, 0:320]
            ec = big[:, 320:640]
            en = big[:, 640:960]
            el = big[:, 960:1280]
            kg = big[:, 1280:1600]
            kdT = big[:, 1600:1920]
            qg = big[:, 2560:2880]
            la = big[:, 2880:3200]
            qgz = L3(3200, 4, T)
            kdt = L3(4480, 3, 128)
            kdm = L3(8108, 8, 128)
            att = L3(SCR, 3, 512)
            st0 = L3(11948, 8, 256)
            stp = L3(13996, 4, 256)
            raw = L3(16044, 8, 64)
            o = L3(15020, 2, T)
            sq = L3(15660, 2, T)
            last = sm[:, 32:44]

        class ssd:
            xc = L3(0, 4, T)
            tok = L3(1280, 3, 384)
            cz = L3(2432, 2, T)
            ce = L3(3072, 4, T)
            ex = L3(3072, 4, T)
            dab = v4(big, 3072, 3, 4, 128)
            ec = L3(8108, 4, T)
            dec = v4(big, 9388, 3, 4, 128)
            xdt = L3(10924, 3, 256)
            xw = L3(11692, 3, 256)
            bm = L3(12460, 8, 128)
            raw = L3(13484, 8, 128)
            st0 = L3(14508, 8, 128)
            stp = L3(15532, 4, 128)
            y = L3(3072, 2, T)
            sq = L3(3712, 2, T)
            outb = big[:, 9388:10540]
            v = L3(16044, 3, 4)
            tt = L3(16056, 3, 4)
            u = L3(16068, 3, 4)
            w1 = L3(16080, 3, 4)
            l = L3(16092, 3, 4)
            d = L3(16104, 3, 4)
            eq = L3(16116, 3, 4)
            dt = L3(16128, 3, 4)
            da = L3(16140, 3, 4)
            cum = L3(16152, 3, 4)
            w = L3(16164, 3, 4)
            alog = big[:, 16176:16180]
            last = L3(16180, 12, 2)
            dsk = big[:, 16204:16206]

        ssd.fin = lambda j: ssd.stp[:, 3, :] if j == 0 else ssd.st0[:, j - 1, :]
        class seq:
            kT = L3(8192, 2, 2112)
            s = big[0:32, 12416:14528]
            t = big[0:32, 14528:16640]

        seq.kt8 = lambda k, g, jh: seq.kT[:, k, g * 1024:(g + 1) * 1024].rearrange("p (q e) -> p e q", e=8)[:, jh * 4:jh * 4 + 4, :]
        class moe:
            y = L3(0, 8, T)
            a = L3(8960, 4 * GE, T)
            gt = L3(3840, 3, 32)
            gt4 = v4(big, 3840, 3, 4, 8)
            gT = big[:, 3936:4256]
            gm = big[:, 4256:4576]
            gb = big[:, 4576:4896]
            e = L3(4896, 2, T)
            L = L3(5536, 3, 36)
            tmp = L3(5644, 3, 8)
            km = big[:, 5668:5671]
            gmax = big[:, 5671:5674]
            ghot = L3(5674, 3, 4)
            gx = L3(5686, 3, 4)
            e8 = L3(5698, 3, 8)
            m1 = big[:, 5722:5725]
            m2 = big[:, 5725:5728]
            h1 = L3(5728, 3, 8)
            h2 = L3(5752, 3, 8)
            dx = big[:, 5776:5779]
            gp = big[:, 5779:5782]
            htok = L3(5888, 3, 1024)
            pick = L3(8960, 3, GE * SLOTS)
            wpick = L3(9728, 3, GE * SLOTS)
            hsel = L3(10496, 8, GE * SLOTS)
            spread = L3(12544, 2, T)
            outs = L3(13184, 2, 1024)
            hid = L3(2560, 2, FE)
            silu = L3(15232, 2, FE)
            hidT = v4(big, 4576, 2, 4, 128)
            rank = L3(16256, 3, 32)
            sel = L3(16352, 3, 32)
            selc = L3(16448, 3, 32)


        ring_full = [ctx.enter_context(nc.semaphore(f"ring_full{i}")) for i in range(RING)]
        ring_free = [ctx.enter_context(nc.semaphore(f"ring_free{i}")) for i in range(RING)]
        a_k_full = ctx.enter_context(nc.semaphore("a_k_full"))
        a_v_full = ctx.enter_context(nc.semaphore("a_v_full"))
        loads = ctx.enter_context(nc.semaphore("loads"))
        outputs = ctx.enter_context(nc.semaphore("outputs"))
        gathered_k = ctx.enter_context(nc.semaphore("gathered_k"))
        gathered_v = ctx.enter_context(nc.semaphore("gathered_v"))
        k_free = ctx.enter_context(nc.semaphore("k_free"))
        v_free = ctx.enter_context(nc.semaphore("v_free"))
        arrived = ctx.enter_context(nc.semaphore("arrived"))
        cleared = ctx.enter_context(nc.semaphore("cleared"))
        seen = ctx.enter_context(nc.semaphore("seen"))
        go = ctx.enter_context(nc.semaphore("go"))

        LOADS_PRE, LOADS_A, LOADS_B = 16 * 13, 16 * 10, 16
        LOADS = LOADS_A + LOADS_B + 32
        OUTS_B, OUTS_G = 160, 128
        OUTS = OUTS_B + OUTS_G + 64
        sem = {}
        for n in ("dve_step act_step pool_step variance rstd rows_in rows_T c_T silu_e vec_T mod_mm mod_done sq rms_mm "
                  "h_done proj_mm proj_ev tail_mm convT_mm xp_done pre_T turn_mm rope_done qz_done tok_mm tok_ev "
                  "tail27_mm tail27_ev a_scores_mm a_max a_exp a_probs a_probs_turned a_probs_copied a_out_mm "
                  "a_out_copied c_logits_mm c_logits c_abs c_log c_exponents c_weights c_weights_turned "
                  "c_weights_copied c_out_mm lr_mm gla_operands gla_scores_mm gla_scores_masked gla_kv_mm gla_states "
                  "gla_out_mm mixer_squares mixer_norm_mm conv_silu xb_turned ssm_in_turned log_decays cum_mm cb_mm "
                  "decays_spread cum_rows_mm cb_sample_mm ssd_operands bx_mm ssm_states ssd_out_mm ssm_final ssm_turned "
                  "a_keys_turned a_keys_copied_dve a_keys_copied_act a_queries c_keys_copied_dve c_keys_copied_act "
                  "c_keys_turned c_queries router_mm gates_done gates_turned gate_row down_added gate_mm hidden up_mm "
                  "gate_copied down_mm rows_turned gate_logits gate_abs gate_log gla_cum gla_exps silu_exp conv_done "
                  "conv_exp dt_exp dt_plus1 dt_log ssm_in_copied decay_left decay_left_exp cum_exps decay_args "
                  "decay_exps ssm_out_copied c_out_copied group_args group_exps pair_args pair_exps gate_act "
                  "rows_copied gla_final_states ranks_mm rows_kept spread_copied slot_out_copied picks gather_mm "
                  "weighted_picks spread_turned gathered slot_sum_mm selected pair_mm hidden_turned hidden_kept").split():
            sem[n] = ctx.enter_context(nc.semaphore(n))

        own = {}

        def step(eng, ins):
            own[eng][1] += 1
            ins.then_inc(own[eng][0], 1)
            eng.wait_ge(own[eng][0], own[eng][1])

        def barrier(eng):
            eng.drain().then_inc(arrived, 1)
            eng.wait_ge(cleared, 1)
            eng.sem_inc(seen, 1)
            eng.wait_ge(go, 1)
            own[eng][1] = 0

        def barrier_lead(pool):
            pool.sem_inc(arrived, 1)
            pool.wait_ge(arrived, 4)
            nums = sorted(s.num for s in sem.values())
            assert nums[-1] - nums[0] == len(nums) - 1
            pool.sem_clear(range(nums[0], nums[-1] + 1))
            pool.sem_clear(arrived)
            pool.sem_clear(go)
            pool.sem_inc(cleared, 1)
            pool.wait_ge(seen, 3)
            pool.sem_clear(seen)
            pool.sem_clear(cleared)
            pool.sem_inc(go, 1)
            own[pool][1] = 0

        STAGES_BEFORE, STAGES_AFTER = 0, 0
        block = ctx.enter_context(nc.Block())

        @block.sync
        def _(sp):
            def load(l, src, slot, idx):
                sp.wait_ge(ring_free[slot], l * PER_SLOT + idx + 1)
                a = src.shape[1]
                sp.dma_start(ring3(slot, a), src).then_inc(ring_full[slot], 16)

            with sp.Fori(0, DEPTH) as l:
                with sp.Fori(0, 3) as it:
                    for s in range(4):
                        src = w_ada[l, :, bass.ds(it * 2048 + s * 512, 512)]
                        load(l, src.rearrange("(k p) n -> p k n", p=128), s, it)
                for j in range(6):
                    load(l, w_in[l, :, j * 512:(j + 1) * 512].rearrange("(k p) n -> p k n", p=128), j % 4, 3 + j // 4)
                with sp.Fori(0, DB) as b:
                    sp.wait_ge(k_free, l * (DB + 1) + b + 1)
                    kb, vb = v3(big, 0, 8, 256), v3(big, 4096, 8, 256)
                    kn, vn = v3(big, 2048, 4, 256), v3(big, 6144, 4, 256)
                    for cache, far, near, full, free in ((win_k, kb, kn, a_k_full, None), (win_v, vb, vn, a_v_full, v_free)):
                        if free is not None:
                            sp.wait_ge(free, l * (DB + 1) + b + 1)
                        sp.dma_start(far[0:96], cache[l, b, 0:1536].rearrange("(a r) c -> a r c", r=16)[:, 0:8, :]).then_inc(full, 16)
                        sp.dma_start(near, cache[l, b, 1536:2048].rearrange("(p r) c -> p r c", r=4)).then_inc(full, 16)
                for j in range(2):
                    load(l, w_out[l, :, j * 512:(j + 1) * 512].rearrange("(k p) n -> p k n", p=128), 2 + j, 4)
                with sp.Fori(0, NE // 4) as it:
                    for q in range(3 * GE):
                        u, w = next((u, w) for u in range(GE) for w, at in ((w_gate, GATE_AT), (w_up, UP_AT), (w_down, DOWN_AT)) if at[u] == q)
                        load(l, w[l, it * GE + u].rearrange("(k p) n -> p k n", p=128), q % RING, it * 3 + 5 + q // RING)

        @block.tensor
        def _(pe):
            own[pe] = [None, 0]
            mm = nc.tensor.matmul

            def tr(out, in_):
                return nc.tensor.transpose(out, in_, ident[0:in_.shape[0], 0:in_.shape[0]])

            def full(l, slot, idx):
                pe.wait_ge(ring_full[slot], (l * PER_SLOT + idx + 1) * 16)

            def pre():
                pe.wait_ge(loads, LOADS_PRE)
                rows = v3(big, 0, 3, 1024)
                for k in range(KT8):
                    for t, (t0, n) in enumerate(SPANS):
                        i = tr(PS[:, k, t0:t0 + n], rows[0:n, t, k * 128:(k + 1) * 128])
                i.then_inc(sem["rows_T"], 1)
                pe.wait_ge(sem["rows_in"], 1)
                pe.wait_ge(sem["xp_done"], 1)
                for k in range(KT8):
                    i = tr(PS[:, 0, k * 9:(k + 1) * 9], big[0:9, 4096 + k * 128:4096 + (k + 1) * 128])
                i = tr(PS[:, 1, 0:8], big[0:8, 5120:5248])
                i.then_inc(sem["c_T"], 1)

            def rms():
                pe.wait_ge(sem["sq"], 1)
                sq = v3(big, SCR, KT8, T)
                for k in range(KT8):
                    i = mm(PS[:, 1, 0:T], ones, sq[:, k, :], start=(k == 0), stop=(k == KT8 - 1))
                i.then_inc(sem["rms_mm"], 1)

            def stage_a(l):
                pe.wait_ge(loads, l * LOADS + LOADS_PRE + LOADS_A)
                i = tr(PS[:, 1, 0:NVEC], vrow[0:NVEC, :])
                i.then_inc(sem["vec_T"], 1)
                crow = big[0:24, SCR + 2560:SCR + 3072]
                for c in range(4):
                    i = tr(PS[:, 2, 24 * c:24 * c + 24], crow[:, c * 128:(c + 1) * 128])
                i.then_inc(sem["convT_mm"], 1)
                with pe.Fori(0, 3) as it:
                    for s in range(4):
                        full(l, s, it)
                        for m in range(4):
                            for k in range(KT8):
                                i = mm(PS[:, 0, bass.ds(it * 144 + s * 36 + m * 9, 9)], ring3(s, 8)[:, k, m * 128:(m + 1) * 128],
                                       v3(cT_, 0, 8, 9)[:, k, :], start=(k == 0), stop=(k == 7))
                        i.then_inc(ring_free[s], 1)
                pe.drain().then_inc(sem["mod_mm"], 1)
                pe.wait_ge(sem["vec_T"], 1)
                pe.wait_ge(sem["mod_done"], 1)
                rms()
                pe.wait_ge(sem["h_done"], 1)
                pe.wait_ge(sem["xp_done"], 1)
                for c in range(24):
                    j, m = divmod(c, 4)
                    if m == 0:
                        full(l, j % 4, 3 + j // 4)
                    if c >= 4:
                        pe.wait_ge(sem["proj_ev"], c - 3)
                    for k in range(KT8):
                        i = mm(PS[:, c % 4, 0:T], ring3(j % 4, 8)[:, k, m * 128:(m + 1) * 128], mT[:, k, :],
                               start=(k == 0), stop=(k == 7))
                    i.then_inc(sem["proj_mm"], 1)
                    if m == 3:
                        pe.wait_ge(sem["proj_mm"], c + 1)
                        pe.sem_inc(ring_free[j % 4], 1)
                for k in range(KT8):
                    mm(PS[0:16, 4, 0:T], wtail[:, k, 0:16], mT[:, k, :], start=(k == 0), stop=(k == 7))
                for t, (t0, n) in enumerate(SPANS):
                    for k in range(KT8):
                        i = mm(PS[0:n, 5, 4 * t:4 * t + 4], mT[:, k, t0:t0 + n], wtail[:, k, 16:20], start=(k == 0), stop=(k == 7))
                i.then_inc(sem["tail_mm"], 1)

            def tok(chunks, bank, n_free):
                for t, (t0, n) in enumerate(SPANS):
                    for c in range(2):
                        o = PS[0:n, bank + t // 2, (t % 2) * 256 + c * 128:(t % 2) * 256 + c * 128 + 128]
                        i = tr(o, PT[:, chunks + c, t0:t0 + n])
                return i

            def stage_b():
                for c in range(4):
                    i = mm(PS[:, c, 0:T], K("turn"), PT[:, AQ + c, :], start=True, stop=True)
                i.then_inc(sem["turn_mm"], 1)
                tail = v3(big, SCR, 4, 27)
                pe.wait_ge(sem["pre_T"], 1)
                for c in range(4):
                    i = tr(PS[0:27, 4, c * 128:(c + 1) * 128], tail[:, c, :])
                i.then_inc(sem["tail27_mm"], 1)
                pe.wait_ge(sem["rope_done"], 1)
                tok(AK, 0, 0).then_inc(sem["tok_mm"], 1)
                tok(AV, 2, 0).then_inc(sem["tok_mm"], 1)
                tok(BV, 6, 0).then_inc(sem["tok_mm"], 1)
                pe.wait_ge(sem["tail27_ev"], 1)
                tok(CK, 4, 0).then_inc(sem["tok_mm"], 1)
                pe.wait_ge(sem["tok_ev"], 1)
                tok(CV, 0, 0).then_inc(sem["tok_mm"], 1)
                pe.wait_ge(sem["tok_ev"], 5)
                s, pt = v3(big, SCR, 4, 512), v4(big, SCR + 4096, 2, 4, 256)
                for qz, kc, v, oc, names in ((qzA, AK, vA, 0, ("a_scores_mm", "a_probs", "a_probs_turned", "a_probs_copied", "a_out_mm", "a_max", "a_out_copied")),
                                             (qzC, CK, vC, 4, ("c_logits_mm", "c_weights", "c_weights_turned", "c_weights_copied", "c_out_mm", "c_logits", "oC_ev"))):
                    if oc == 0:
                        pe.wait_ge(sem["qz_done"], 1)
                    else:
                        pe.wait_ge(sem["a_out_copied"], 1)
                    for h in range(4):
                        for qb in range(2):
                            i = mm(PS[:, h, qb * 256:qb * 256 + 256], qz[:, h, qb * 128:qb * 128 + 128],
                                   PT[:, kc + h // 2, 0:256], start=True, stop=True)
                    i.then_inc(sem[names[0]], 1)
                    pe.wait_ge(sem[names[1]], 1)
                    for kb in range(2):
                        for h in range(4):
                            for qb in range(2):
                                i = tr(PSF[:, kb * 1024 + h * 256 + qb * 128:kb * 1024 + h * 256 + qb * 128 + 128],
                                       s[:, h, qb * 256 + kb * 128:qb * 256 + kb * 128 + 128])
                    i.then_inc(sem[names[2]], 1)
                    pe.wait_ge(sem[names[3]], 1)
                    for h in range(4):
                        for kb in range(2):
                            i = mm(PS[64 * (h % 2):64 * (h % 2) + 64, 4 + h // 2, 0:256], v[:, kb, h * 64:h * 64 + 64],
                                   pt[:, kb, h, :], start=(kb == 0), stop=(kb == 1))
                    i.then_inc(sem[names[4]], 1)

            def stage_gla():
                i = mm(PS[:, 7, 0:T], wa2[0:16, :], lrT, start=True, stop=True)
                i.then_inc(sem["lr_mm"], 1)
                G = gla
                pe.wait_ge(sem["gla_operands"], 1)
                for t, (t0, n) in enumerate(SPANS):
                    mm(PS[0:n, t, 0:4 * n].rearrange("p (h t) -> p h t", h=4), G.kg[:, t0:t0 + n], G.qgz[:, :, t0:t0 + n], start=True, stop=True)
                for t, (t0, n) in enumerate(SPANS):
                    i = tr(PS[0:n, 3, t * 128:(t + 1) * 128], G.kdT[:, t0:t0 + n])
                i.then_inc(sem["gla_scores_mm"], 1)
                pe.wait_ge(sem["gla_scores_masked"], 1)
                for c in range(4):
                    r = 64 * (c % 2)
                    mm(PS[:, 4 + c % 2, (c // 2) * 256:(c // 2) * 256 + 256], G.kdt[r:r + 64, c // 2, :], vB[r:r + 64, c // 2, :],
                       start=True, stop=True)
                for b in range(DB):
                    i = mm(PSF[:, b * 256:b * 256 + 256], G.kdm[0:64, b, :], vB[0:64, 2, :], start=True, stop=True)
                i.then_inc(sem["gla_kv_mm"], 1)
                pe.wait_ge(sem["gla_states"], 1)
                for c in range(2):
                    o = PS[:, 6 + c, 0:T]
                    cs = slice(c * 128, c * 128 + 128)
                    for b in range(DB):
                        mm(o[:, 256 + 8 * b:264 + 8 * b], G.st0[:, b, cs], G.qg[:, 256 + 8 * b:264 + 8 * b],
                           start=(b == 0), stop=False, skip_group_check=True)
                    for j in range(1, 4):
                        mm(o[:, 64 * j:64 * j + 64], G.stp[:, j - 1, cs], G.qg[:, 64 * j:64 * j + 64],
                           start=False, stop=False, skip_group_check=True)
                    for hh in range(2):
                        h = 2 * c + hh
                        for t, (t0, n) in enumerate(SPANS):
                            att = G.att[0:n, t, 0:4 * n].rearrange("p (h t) -> p h t", h=4)
                            i = mm(o[64 * hh:64 * hh + 64, t0:t0 + n], vB[0:n, t, h * 64:h * 64 + 64], att[:, h, :],
                                   start=False, stop=(t == 2), skip_group_check=True)
                i.then_inc(sem["gla_out_mm"], 1)
                pe.wait_ge(sem["mixer_squares"], 1)
                for c in range(2):
                    i = mm(PS[:, c, 0:T], K("blk64"), G.sq[:, c, :], start=True, stop=True)
                i.then_inc(sem["mixer_norm_mm"], 1)

            def stage_ssd(l):
                D = ssd
                pe.wait_ge(sem["conv_silu"], 1)
                for c in range(3):
                    for t, (t0, n) in enumerate(SPANS):
                        i = tr(PS[0:n, t, c * 128:(c + 1) * 128], D.xc[:, c, t0:t0 + n])
                i.then_inc(sem["xb_turned"], 1)
                pe.wait_ge(loads, l * LOADS + LOADS_PRE + LOADS)
                for b in range(DB):
                    i = tr(PSF[:, 1536 + b * 128:1536 + b * 128 + 128], D.raw[:, b, :])
                i.then_inc(sem["ssm_in_turned"], 1)
                pe.wait_ge(sem["log_decays"], 1)
                for t, (t0, n) in enumerate(SPANS):
                    tri, blk = (K("tri8"), K("blk8")) if t == 2 else (K("tri64"), K("blk64"))
                    mm(PS[0:n, 5, 4 * t:4 * t + 4], tri[0:n, 0:n], D.da[0:n, t, :], start=True, stop=True)
                    i = mm(PS[0:n, 5, 16 + 4 * t:20 + 4 * t], blk[0:n, 0:n], D.da[0:n, t, :], start=True, stop=True)
                i.then_inc(sem["cum_mm"], 1)
                for t, (t0, n) in enumerate(SPANS):
                    i = mm(PS[0:n, 6, 0:2 * n].rearrange("p (g t) -> p g t", g=2) if t == 2 else PS[0:n, 6 + t, 0:256].rearrange("p (g t) -> p g t", g=2),
                           D.xc[:, 2, t0:t0 + n], D.cz[:, :, t0:t0 + n], start=True, stop=True) if t < 2 else i
                i.then_inc(sem["cb_mm"], 1)
                pe.wait_ge(sem["decays_spread"], 1)
                for h in range(4):
                    for t, (t0, n) in enumerate(SPANS):
                        tri = K("tri8") if t == 2 else K("tri64")
                        i = mm(PS[:, h, t0:t0 + n], D.dab[0:n, t, h, :], tri[0:n, 0:n], start=True, stop=True)
                i.then_inc(sem["cum_rows_mm"], 1)
                t0, n = SPANS[2]
                i = mm(PS[0:n, 4, 0:2 * n].rearrange("p (g t) -> p g t", g=2), D.xc[:, 2, t0:t0 + n], D.cz[:, :, t0:t0 + n], start=True, stop=True)
                i.then_inc(sem["cb_sample_mm"], 1)
                pe.wait_ge(sem["ssd_operands"], 1)
                for c in range(4):
                    r = 64 * (c % 2)
                    for g in range(2):
                        mm(PS[64 * g:64 * g + 64, c % 2, (c // 2) * 128:(c // 2) * 128 + 128],
                           D.tok[r:r + 64, c // 2, 256 + 64 * g:320 + 64 * g], D.xw[r:r + 64, c // 2, 128 * g:128 * g + 128],
                           start=True, stop=True)
                for b in range(DB):
                    for g in range(2):
                        i = mm(PSF[64 * g:64 * g + 64, 1024 + b * 128:1152 + b * 128], D.bm[0:64, b, 64 * g:64 * g + 64],
                               D.xw[0:64, 2, 128 * g:128 * g + 128], start=True, stop=True)
                i.then_inc(sem["bx_mm"], 1)
                pe.wait_ge(sem["ssm_states"], 1)
                for c in range(2):
                    for hh in range(2):
                        h = 2 * c + hh
                        o = PS[64 * hh:64 * hh + 64, 6 + c, 0:T]
                        for b in range(DB):
                            mm(o[:, 256 + 8 * b:264 + 8 * b], D.st0[:, b, 64 * hh:64 * hh + 64], D.ce[:, h, 256 + 8 * b:264 + 8 * b],
                               start=(b == 0), stop=False, skip_group_check=True)
                        for j in range(1, 4):
                            mm(o[:, 64 * j:64 * j + 64], D.stp[:, j - 1, 64 * hh:64 * hh + 64], D.ce[:, h, 64 * j:64 * j + 64],
                               start=False, stop=False, skip_group_check=True)
                        for t, (t0, n) in enumerate(SPANS):
                            i = mm(o[:, t0:t0 + n], D.xdt[0:n, t, 64 * h:64 * h + 64], D.dec[0:n, t, h, 0:n],
                                   start=False, stop=(t == 2), skip_group_check=True)
                i.then_inc(sem["ssd_out_mm"], 1)
                pe.wait_ge(sem["ssm_final"], 1)
                for j in range(9):
                    i = tr(PSF[:, j * 128:(j + 1) * 128], D.fin(j))
                i.then_inc(sem["ssm_turned"], 1)
                pe.wait_ge(sem["mixer_squares"], 1)
                for c in range(2):
                    i = mm(PS[:, 3, 0:T], ones, D.sq[:, c, :], start=(c == 0), stop=(c == 1))
                i.then_inc(sem["mixer_norm_mm"], 1)

            def seq_a(l, b):
                Q = seq
                pe.wait_ge(a_k_full, (l * DB + b + 1) * 32)
                kb, kn = v3(big, 0, 8, 256), v3(big, 2048, 4, 256)
                for c in range(2):
                    for r in range(8):
                        tr(PS[:, 3 * c + r // 4, (r % 4) * 96:(r % 4) * 96 + 96], kb[0:96, r, c * 128:(c + 1) * 128])
                    for j in range(4):
                        i = tr(PS[:, 3 * c + 2, j * 128:(j + 1) * 128], kn[:, j, c * 128:(c + 1) * 128])
                    i.then_inc(sem["a_keys_turned"], 1)
                pe.wait_ge(sem["a_keys_copied_dve"], 2)
                pe.wait_ge(sem["a_keys_copied_act"], 2)
                pe.wait_ge(sem["a_queries"], 1)
                for n0, n in ((0, 512), (512, 512), (1024, 256)):
                    for c in range(2):
                        mm(PS[0:32, n0 // 512, 0:n], v3(qb_, 0, 2, 32)[:, c, :], Q.kT[:, c, n0:n0 + n], start=(c == 0), stop=(c == 1))
                for c in range(2):
                    i = mm(PS[0:32, 2, 256:320], v3(qb_, 0, 2, 32)[:, c, :], kS[:, c, :], start=(c == 0), stop=(c == 1))
                i.then_inc(sem["a_scores_mm"], 1)
                pe.wait_ge(sem["a_probs"], 1)
                for r in range(8):
                    tr(PS[0:96, 6, r * 32:r * 32 + 32], Q.s[:, r * 96:(r + 1) * 96])
                for j in range(4):
                    tr(PS[:, 6, (8 + j) * 32:(9 + j) * 32], Q.s[:, NA1 + j * 128:NA1 + (j + 1) * 128])
                i = tr(PS[0:64, 6, 384:416], Q.s[:, NA:NA + 64])
                i.then_inc(sem["a_probs_turned"], 1)
                pe.wait_ge(a_v_full, (l * DB + b + 1) * 32)
                pe.wait_ge(sem["a_probs_copied"], 1)
                vb, vn = v3(big, 4096, 8, 256), v3(big, 6144, 4, 256)
                pS = v3(pS_, 0, 17, 32)
                for c in range(2):
                    for r in range(8):
                        mm(PS[:, 7, c * 32:c * 32 + 32], vb[0:96, r, c * 128:(c + 1) * 128], pS[0:96, r, :], start=(r == 0), stop=False)
                    for j in range(4):
                        mm(PS[:, 7, c * 32:c * 32 + 32], vn[:, j, c * 128:(c + 1) * 128], pS[:, 8 + j, :], start=False, stop=False)
                    i = mm(PS[:, 7, c * 32:c * 32 + 32], vA[0:64, 2, c * 128:(c + 1) * 128], pS[0:64, 12, :], start=False, stop=True)
                i.then_inc(sem["a_out_mm"], 1)

            def seq_c(l, b):
                Q = seq
                pe.wait_ge(gathered_k, (l * DB + b + 1) * 32)
                pe.wait_ge(sem["a_scores_mm"], 1)
                kb = v4(big, 0, 2, 8, 256)
                for n in range(8):
                    c, g, jh = n // 4, (n // 2) % 2, n % 2
                    if n >= 3:
                        pe.wait_ge(sem["c_keys_copied_dve" if n % 2 == 0 else "c_keys_copied_act"], (n - 3) // 2 + 1)
                    for j in range(4):
                        i = tr(PS[:, 3 + n % 3, j * 128:(j + 1) * 128], kb[:, g, jh * 4 + j, c * 128:(c + 1) * 128])
                    i.then_inc(sem["c_keys_turned"], 1)
                pe.wait_ge(sem["c_keys_turned"], 8)
                pe.sem_inc(k_free, 1)
                pe.wait_ge(sem["c_keys_copied_act"], 4)
                pe.wait_ge(sem["c_keys_copied_dve"], 4)
                pe.wait_ge(sem["c_queries"], 1)
                for n0 in range(0, 2048, 512):
                    for c in range(2):
                        mm(PS[0:32, n0 // 512, 0:512], v3(qb_, 0, 2, 32)[:, c, :], Q.kT[:, c, n0:n0 + 512], start=(c == 0), stop=(c == 1))
                for c in range(2):
                    i = mm(PS[0:32, 4, 0:64], v3(qb_, 0, 2, 32)[:, c, :], kS[:, 2 + c, :], start=(c == 0), stop=(c == 1))
                i.then_inc(sem["c_logits_mm"], 1)
                pe.wait_ge(sem["c_weights"], 1)
                for g in range(2):
                    for j in range(8):
                        tr(PS[:, 5 + g, j * 32:(j + 1) * 32], Q.s[:, g * 1024 + j:(g + 1) * 1024:8])
                i = tr(PS[0:64, 5, 256:288], Q.s[:, 2048:2112])
                i.then_inc(sem["c_weights_turned"], 1)
                pe.wait_ge(sem["c_weights_copied"], 1)
                pe.wait_ge(sem["a_out_copied"], 2)
                pe.wait_ge(gathered_v, (l * DB + b + 1) * 32)
                vb = v4(big, 4096, 2, 8, 256)
                pS = v3(pS_, 0, 17, 32)
                for c in range(2):
                    for g in range(2):
                        for j in range(8):
                            mm(PS[:, 7, c * 32:c * 32 + 32], vb[:, g, j, c * 128:(c + 1) * 128], pS[:, g * 8 + j, :],
                               start=(g + j == 0), stop=False)
                    i = mm(PS[:, 7, c * 32:c * 32 + 32], vC[0:64, 2, c * 128:(c + 1) * 128], pS[0:64, 16, :], start=False, stop=True)
                i.then_inc(sem["c_out_mm"], 1)
                pe.wait_ge(sem["c_out_mm"], 1)
                pe.sem_inc(v_free, 1)

            def stage_out(l):
                for c in range(8):
                    j, m = divmod(c, 4)
                    if m == 0:
                        full(l, 2 + j, 4)
                    if c >= 4:
                        pe.wait_ge(sem["proj_ev"], c - 3)
                    for k in range(KT8):
                        i = mm(PS[:, 4 + c % 4, 0:T], ring3(2 + j, 8)[:, k, m * 128:(m + 1) * 128], mT[:, k, :], start=(k == 0), stop=(k == 7))
                    i.then_inc(sem["proj_mm"], 1)
                    if m == 3:
                        pe.wait_ge(sem["proj_mm"], c + 1)
                        pe.sem_inc(ring_free[2 + j], 1)
                rms()
                pe.wait_ge(sem["h_done"], 1)
                for t, (t0, n) in enumerate(SPANS):
                    for k in range(KT8):
                        i = mm(PS[0:n, 2, t * 36:(t + 1) * 36], mT[:, k, t0:t0 + n], wr[:, k, :], start=(k == 0), stop=(k == 7))
                i.then_inc(sem["router_mm"], 1)
                pe.wait_ge(sem["gates_done"], 1)
                for t, (t0, n) in enumerate(SPANS):
                    i = tr(PS[0:32, 3, t0:t0 + n], moe.gt[0:n, t, :])
                i.then_inc(sem["gates_turned"], 1)
                pe.wait_ge(sem["selected"], 1)
                for t, (t0, n) in enumerate(SPANS):
                    for t2 in range(t):
                        mm(PS[0:n, 4, 32 * t:32 * t + 32], ones[:, 0:n], moe.sel[:, t2, :], start=(t2 == 0), stop=False)
                    mm(PS[0:n, 4, 32 * t:32 * t + 32], K("before")[0:n, 0:n], moe.sel[0:n, t, :], start=(t == 0), stop=True)
                for t, (t0, n) in enumerate(SPANS):
                    i = mm(PS[:, 4, 96:128], ones[0:n, :], moe.sel[0:n, t, :], start=(t == 0), stop=(t == 2))
                i.then_inc(sem["ranks_mm"], 1)
                for t, (t0, n) in enumerate(SPANS):
                    if t:
                        pe.wait_ge(sem["rows_kept"], t)
                    for k in range(KT8):
                        i = tr(PS[0:n, 5 + k // 4, (k % 4) * 128:(k % 4) * 128 + 128], mT[:, k, t0:t0 + n])
                    i.then_inc(sem["rows_turned"], 1)

            def group(l, it):
                M = moe

                def pairwise(pair, at, out_bank, stationary, steps, halves):
                    for x in range(2):
                        q = at[2 * pair + x]
                        full(l, q % RING, it * 3 + 5 + q // RING)
                    for half in range(halves):
                        for k in range(steps):
                            for x in range(2):
                                w = ring3(at[2 * pair + x] % RING, steps)[:, k, half * 512:half * 512 + 512]
                                i = mm(PS[SLOTS * x:SLOTS * x + SLOTS, out_bank + half, :], stationary(k, x), w,
                                       start=(k == 0), stop=(k == steps - 1))
                    i.then_inc(sem["pair_mm"], 1)
                    return i

                def gate(pair):
                    pairwise(pair, GATE_AT, 2 * pair, lambda k, x: M.hsel[:, k, (2 * pair + x) * SLOTS:(2 * pair + x + 1) * SLOTS], 8, 1)

                def up(pair):
                    pairwise(pair, UP_AT, 2 * pair + 1, lambda k, x: M.hsel[:, k, (2 * pair + x) * SLOTS:(2 * pair + x + 1) * SLOTS], 8, 1)

                def turn(pair):
                    pe.wait_ge(sem["hidden"], pair + 1)
                    for f in range(4):
                        i = tr(PS[:, 6 + pair, f * 128:(f + 1) * 128], M.hid[:, pair, f * 128:(f + 1) * 128])
                    i.then_inc(sem["hidden_turned"], 1)

                def down(pair):
                    pe.wait_ge(sem["hidden_kept"], pair + 1)
                    if pair:
                        pe.wait_ge(sem["slot_out_copied"], 1)
                    pairwise(pair, DOWN_AT, 4, lambda k, x: M.hidT[:, pair, k, x * SLOTS:(x + 1) * SLOTS], 4, 2)

                def release(n, at, pair):
                    pe.wait_ge(sem["pair_mm"], n)
                    for x in range(2):
                        pe.sem_inc(ring_free[at[2 * pair + x] % RING], 1)

                pe.wait_ge(sem["picks"], 1)
                for k in range(KT8):
                    for t, (t0, n) in enumerate(SPANS):
                        i = mm(PS[:, 4 + k // 2, (k % 2) * 256:(k % 2) * 256 + 256], M.htok[0:n, t, k * 128:(k + 1) * 128],
                               M.pick[0:n, t, :], start=(t == 0), stop=(t == 2))
                i.then_inc(sem["gather_mm"], 1)
                pe.wait_ge(sem["weighted_picks"], 1)
                for pair in range(2):
                    for t, (t0, n) in enumerate(SPANS):
                        i = tr(PS[:, 2 + pair, t0:t0 + n], M.wpick[0:n, t, pair * 128:(pair + 1) * 128])
                i.then_inc(sem["spread_turned"], 1)
                pe.wait_ge(sem["gathered"], 1)
                gate(0)
                release(1, GATE_AT, 0)
                up(0)
                release(2, UP_AT, 0)
                pe.wait_ge(sem["spread_copied"], 1)
                gate(1)
                release(3, GATE_AT, 1)
                turn(0)
                up(1)
                release(4, UP_AT, 1)
                down(0)
                release(5, DOWN_AT, 0)
                turn(1)
                down(1)
                release(6, DOWN_AT, 1)
                pe.wait_ge(sem["slot_out_copied"], 2)
                for d in range(8):
                    if d >= 2:
                        pe.wait_ge(sem["down_added"], d - 1)
                    for pair in range(2):
                        i = mm(PS[:, 6 + d % 2, 0:T], M.outs[:, pair, d * 128:(d + 1) * 128], M.spread[:, pair, :],
                               start=(pair == 0), stop=(pair == 1))
                    i.then_inc(sem["slot_sum_mm"], 1)

            def dense_group(l, it):
                M = moe
                for u in range(GE):
                    pe.wait_ge(sem["gate_row"], u + 1)
                    if u:
                        pe.wait_ge(sem["gate_copied"], u)
                    mm(PS[:, 4, 0:T], ones[0:32, :], M.gm[0:32, :], start=True, stop=True).then_inc(sem["gate_mm"], 1)
                    for q in (GATE_AT[u], UP_AT[u]):
                        full(l, q % RING, it * 3 + 5 + q // RING)
                    for f in range(4):
                        if u * 4 + f >= 2:
                            pe.wait_ge(sem["hidden"], u * 4 + f - 1)
                        for q, o in ((GATE_AT[u], 0), (UP_AT[u], 2)):
                            for k in range(KT8):
                                i = mm(PS[:, o + f % 2, 0:T], ring3(q % RING, 8)[:, k, f * 128:(f + 1) * 128], mT[:, k, :], start=(k == 0), stop=(k == 7))
                        i.then_inc(sem["up_mm"], 1)
                    pe.wait_ge(sem["up_mm"], 4 * u + 4)
                    for q in (GATE_AT[u], UP_AT[u]):
                        pe.sem_inc(ring_free[q % RING], 1)
                pe.wait_ge(sem["hidden"], 4 * GE)
                pe.wait_ge(sem["gate_copied"], GE)
                for u in range(GE):
                    q = DOWN_AT[u]
                    full(l, q % RING, it * 3 + 5 + q // RING)
                    for d in range(8):
                        if u * 8 + d >= 4:
                            pe.wait_ge(sem["down_added"], 8 * u + d - 3)
                        for f in range(4):
                            i = mm(PS[:, 4 + d % 4, 0:T], ring3(q % RING, 4)[:, f, d * 128:(d + 1) * 128], M.a[:, 4 * u + f, :], start=(f == 0), stop=(f == 3))
                        i.then_inc(sem["down_mm"], 1)
                    pe.wait_ge(sem["down_mm"], 8 * u + 8)
                    pe.sem_inc(ring_free[q % RING], 1)

            def final():
                rms()
                pe.wait_ge(sem["h_done"], 1)
                for t, (t0, n) in enumerate(SPANS):
                    for half in range(2):
                        for k in range(4):
                            i = tr(PS[0:n, 2 * t + half, k * 128:(k + 1) * 128], mT[:, 4 * half + k, t0:t0 + n])
                i.then_inc(sem["rows_turned"], 1)

            for s in range(RING):
                pe.sem_inc(ring_free[s], 1)
            pre()
            barrier(pe)
            with pe.Fori(0, DEPTH) as l:
                stage_a(l)
                barrier(pe)
                stage_b()
                barrier(pe)
                stage_gla()
                barrier(pe)
                stage_ssd(l)
                barrier(pe)
                pe.sem_inc(k_free, 1)
                pe.sem_inc(v_free, 1)
                with pe.Fori(0, DB) as b:
                    seq_a(l, b)
                    seq_c(l, b)
                    barrier(pe)
                stage_out(l)
                barrier(pe)
                many = pe.value_load(crowded[0:1, 0:1], min_val=0, max_val=1)
                with pe.If(many > 0):
                    with pe.Fori(0, NE // 4) as it:
                        dense_group(l, it)
                        barrier(pe)
                with pe.Else():
                    with pe.Fori(0, NE // 4) as it:
                        group(l, it)
                        barrier(pe)
                barrier(pe)
            final()
            barrier(pe)

        @block.scalar
        def _(act):
            own[act] = [sem["act_step"], 0]
            def f(out, in_, func, scale=1.0, bias=None):
                if bias is None:
                    return nc.scalar.activation(out, in_, func, scale=scale)
                return nc.scalar.activation(out, in_, func, scale=scale, bias=bias)

            def copy(out, in_):
                return nc.scalar.activation(out, in_, ACT.Copy)

            def squares():
                f(v3(big, SCR, KT8, T), xT, ACT.Square).then_inc(sem["sq"], 1)

            def rsqrt(out):
                v = rv[:, :].rearrange("p (a b) -> p a b", a=2) if len(out.shape) == 3 else rv[:, 0:T]
                act.wait_ge(sem["variance"], 1)
                step(act, f(out, v, ACT.Ln))
                f(out, out, ACT.Exp, scale=-0.5).then_inc(sem["rstd"], 1)

            def pre():
                act.wait_ge(loads, LOADS_PRE)
                f(big[0:9, 5248:6272], big[0:9, 4096:5120], ACT.Exp, scale=-1.0).then_inc(sem["silu_e"], 1)

            def stage_a():
                squares()
                rsqrt(rr[:, :])
                for c in range(24):
                    act.wait_ge(sem["proj_mm"], c + 1)
                    if c < 20:
                        copy(PT[:, c, :], PS[:, c % 4, 0:T]).then_inc(sem["proj_ev"], 1)
                    else:
                        if c == 20:
                            act.wait_ge(sem["xp_done"], 1)
                        step(act, copy(XP[:, c - 20, 3:259], PS[:, c % 4, 0:256]))
                        copy(XPs[:, c - 20, :, 3:11], PS[:, c % 4, 256:T].rearrange("p (b i) -> p b i", b=DB)).then_inc(sem["proj_ev"], 1)
                act.wait_ge(sem["tail_mm"], 1)
                copy(lrT, PS[0:16, 4, 0:T])
                copy(sm[:, 0:8], PS[:, 5, 0:8])
                copy(sm[0:64, 8:12], PS[0:64, 5, 8:12])

            def stage_b():
                act.wait_ge(sem["tail27_mm"], 1)
                copy(cvo[0:27, :], PS[0:27, 4, :]).then_inc(sem["tail27_ev"], 1)
                for n, (buf, bank) in enumerate(((kA, 0), (vA, 2), (vB, 6), (kC, 4), (vC, 0))):
                    act.wait_ge(sem["tok_mm"], n + 1)
                    step(act, copy(buf[:, 0:2, :], PS[:, bank, :].rearrange("p (t c) -> p t c", t=2)))
                    copy(buf[0:64, 2, :], PS[0:64, bank + 1, 0:256]).then_inc(sem["tok_ev"], 1)
                s, t = v3(big, SCR, 4, 512), v3(big, SCR + 2048, 4, 512)
                act.wait_ge(sem["a_max"], 1)
                for j in range(8):
                    x = s[:, j // 2, (j % 2) * 256:(j % 2) * 256 + 256]
                    i = f(x, x, ACT.Exp, scale=HD ** -0.5, bias=sm[:, 24 + j:25 + j])
                i.then_inc(sem["a_exp"], 1)
                act.wait_ge(sem["a_probs_turned"], 1)
                copy(big[:, SCR + 4096:SCR + 6144], PSF[:, 0:2048]).then_inc(sem["a_probs_copied"], 1)
                act.wait_ge(sem["a_probs_copied"], 1)
                act.wait_ge(sem["a_out_mm"], 1)
                copy(mT[:, 0:2, 0:256], PS[:, 4:6, 0:256]).then_inc(sem["a_out_copied"], 1)
                act.wait_ge(sem["c_logits_mm"], 1)
                for h in range(4):
                    i = f(s[:, h, :], PS[:, h, :], ACT.Identity, scale=HD ** -0.5, bias=bc[:, h:h + 1])
                i.then_inc(sem["c_logits"], 1)
                act.wait_ge(sem["c_abs"], 1)
                step(act, f(t, t, ACT.Exp, scale=-1.0))
                f(t, t, ACT.Ln, bias=1.0).then_inc(sem["c_log"], 1)
                act.wait_ge(sem["c_exponents"], 1)
                f(s, s, ACT.Exp).then_inc(sem["c_weights"], 1)
                act.wait_ge(sem["c_weights_turned"], 1)
                copy(big[:, SCR + 4096:SCR + 6144], PSF[:, 0:2048]).then_inc(sem["c_weights_copied"], 1)
                act.wait_ge(sem["c_out_mm"], 1)
                copy(mT[:, 4:6, 0:256], PS[:, 4:6, 0:256])

            def stage_gla():
                G = gla
                act.wait_ge(sem["lr_mm"], 1)
                f(G.la, PS[:, 7, 0:T], ACT.Identity, bias=vec[:, 86:87]).then_inc(sem["gate_logits"], 1)
                act.wait_ge(sem["gate_abs"], 1)
                step(act, f(G.cum, G.cum, ACT.Exp, scale=-1.0))
                f(G.cum, G.cum, ACT.Ln, bias=1.0).then_inc(sem["gate_log"], 1)
                act.wait_ge(sem["gla_cum"], 1)
                f(G.ec, G.cum, ACT.Exp)
                f(G.en, G.cum, ACT.Exp, scale=-1.0)
                f(G.el, G.el, ACT.Exp).then_inc(sem["gla_exps"], 1)
                act.wait_ge(sem["gla_scores_mm"], 1)
                f(G.qgz, PT[:, GATE:GATE + 4, :], ACT.Exp, scale=-1.0).then_inc(sem["silu_exp"], 1)
                rsqrt(G.sq)

            def stage_ssd():
                D = ssd
                act.wait_ge(sem["conv_done"], 1)
                f(D.ex, D.xc, ACT.Exp, scale=-1.0).then_inc(sem["conv_exp"], 1)
                f(D.alog, bc[:, 8:12], ACT.Exp)
                f(D.u, D.tt, ACT.Exp, scale=-1.0).then_inc(sem["dt_exp"], 1)
                act.wait_ge(sem["dt_plus1"], 1)
                f(D.l, D.w1, ACT.Ln).then_inc(sem["dt_log"], 1)
                act.wait_ge(sem["ssm_in_turned"], 1)
                copy(D.st0, PSF[:, 1536:2560].rearrange("p (b n) -> p b n", b=DB)).then_inc(sem["ssm_in_copied"], 1)
                act.wait_ge(sem["decay_left"], 1)
                f(D.w, D.w, ACT.Exp).then_inc(sem["decay_left_exp"], 1)
                act.wait_ge(sem["cum_rows_mm"], 1)
                f(D.ec, PS[:, 0:4, 0:T], ACT.Exp).then_inc(sem["cum_exps"], 1)
                act.wait_ge(sem["decay_args"], 1)
                f(D.dec[:, 0:2], D.dec[:, 0:2], ACT.Exp)
                f(D.dec[0:64, 2, :, 0:64], D.dec[0:64, 2, :, 0:64], ACT.Exp).then_inc(sem["decay_exps"], 1)
                act.wait_ge(sem["ssm_turned"], 1)
                copy(D.outb, PSF[:, 0:1152]).then_inc(sem["ssm_out_copied"], 1)
                rsqrt(rr[:, :])

            def seq_a(b):
                Q = seq
                act.wait_ge(sem["a_keys_turned"], 2)
                kt = Q.kT[:, 1, 0:768].rearrange("p (a n) -> p a n", a=2)
                copy(kt, PS[:, 3:5, 0:384]).then_inc(sem["a_keys_copied_act"], 1)
                copy(Q.kT[:, 1, 768:1280], PS[:, 5, :]).then_inc(sem["a_keys_copied_act"], 1)
                act.wait_ge(sem["a_max"], 1)
                f(Q.s[:, 0:1344], Q.s[:, 0:1344], ACT.Exp, scale=HD ** -0.5, bias=sm[0:32, 24:25]).then_inc(sem["a_exp"], 1)
                act.wait_ge(sem["a_probs_turned"], 1)
                pS = v3(pS_, 0, 17, 32)
                copy(pS[0:96, 0:8, :], PS[0:96, 6, 0:256].rearrange("p (a n) -> p a n", a=8))
                copy(pS[:, 8:12, :], PS[:, 6, 256:384].rearrange("p (a n) -> p a n", a=4))
                copy(pS[0:64, 12, :], PS[0:64, 6, 384:416]).then_inc(sem["a_probs_copied"], 1)
                act.wait_ge(sem["a_out_mm"], 1)
                out(b, 0, "a_out_copied")

            def out(b, c0, name):
                for hh in range(2):
                    src = PS[64 * hh:64 * hh + 64, 7, 0:96].rearrange("p (c n) -> p c n", c=2)[:, :, 8 * hh:8 * hh + 8]
                    copy(mT[64 * hh:64 * hh + 64, c0:c0 + 2, bass.ds(SEQ + b * 8, 8)], src).then_inc(sem[name], 1)
                    act.wait_ge(sem[name], hh + 1)

            def seq_c(b):
                Q = seq
                act.wait_ge(sem["a_scores_mm"], 1)
                for n in range(0, 8, 2):
                    act.wait_ge(sem["c_keys_turned"], n + 1)
                    c, g, jh = n // 4, (n // 2) % 2, n % 2
                    copy(Q.kt8(c, g, jh), PS[:, 3 + n % 3, :].rearrange("p (j q) -> p j q", j=4)).then_inc(sem["c_keys_copied_act"], 1)
                act.wait_ge(sem["c_logits_mm"], 1)
                f(Q.s, PSF[0:32, 0:2112], ACT.Identity, scale=HD ** -0.5, bias=bsb[0:32, 0:1]).then_inc(sem["c_logits"], 1)
                act.wait_ge(sem["c_abs"], 1)
                step(act, f(Q.t, Q.t, ACT.Exp, scale=-1.0))
                f(Q.t, Q.t, ACT.Ln, bias=1.0).then_inc(sem["c_log"], 1)
                act.wait_ge(sem["c_exponents"], 1)
                f(Q.s, Q.s, ACT.Exp).then_inc(sem["c_weights"], 1)
                act.wait_ge(sem["c_weights_turned"], 1)
                pS = v3(pS_, 0, 17, 32)
                for g in range(2):
                    copy(pS[:, 8 * g:8 * g + 8, :], PS[:, 5 + g, 0:256].rearrange("p (a n) -> p a n", a=8))
                copy(pS[0:64, 16, :], PS[0:64, 5, 256:288]).then_inc(sem["c_weights_copied"], 1)
                act.wait_ge(sem["c_out_mm"], 1)
                out(b, 4, "c_out_copied")

            def stage_out():
                act.wait_ge(sem["proj_ev"], 8)
                squares()
                rsqrt(rr[:, :])
                act.wait_ge(sem["group_args"], 1)
                f(moe.gx, moe.gx, ACT.Exp).then_inc(sem["group_exps"], 1)
                act.wait_ge(sem["pair_args"], 1)
                f(moe.dx, moe.dx, ACT.Exp).then_inc(sem["pair_exps"], 1)
                for t, (t0, n) in enumerate(SPANS):
                    act.wait_ge(sem["rows_turned"], t + 1)
                    copy(moe.htok[0:n, t, :].rearrange("p (a n) -> p a n", a=2), PS[0:n, 5:7, :]).then_inc(sem["rows_kept"], 1)

            def group():
                M = moe
                act.wait_ge(sem["gather_mm"], 1)
                copy(M.hsel[:, :, :].rearrange("p (a b) n -> p a (b n)", a=4), PS[:, 4:8, :]).then_inc(sem["gathered"], 1)
                act.wait_ge(sem["spread_turned"], 1)
                copy(M.spread, PS[:, 2:4, 0:T]).then_inc(sem["spread_copied"], 1)

                for pair, (n_gate, n_down) in enumerate(((1, 5), (3, 6))):
                    act.wait_ge(sem["pair_mm"], n_gate)
                    f(M.silu[:, pair, :], PS[:, 2 * pair, :], ACT.Silu).then_inc(sem["gate_act"], 1)
                    if pair == 0:
                        act.wait_ge(sem["hidden_turned"], 1)
                        copy(M.hidT[:, 0].rearrange("p a n -> p (a n)"), PS[:, 6, :]).then_inc(sem["hidden_kept"], 1)
                act.wait_ge(sem["pair_mm"], 5)
                copy(M.outs[:, 0, :], PSF[:, 2048:3072]).then_inc(sem["slot_out_copied"], 1)
                act.wait_ge(sem["hidden_turned"], 2)
                copy(M.hidT[:, 1].rearrange("p a n -> p (a n)"), PS[:, 7, :]).then_inc(sem["hidden_kept"], 1)
                act.wait_ge(sem["pair_mm"], 6)
                copy(M.outs[:, 1, :], PSF[:, 2048:3072]).then_inc(sem["slot_out_copied"], 1)

            def dense_expert(u):
                M = moe
                act.wait_ge(sem["gate_mm"], u + 1)
                if u:
                    act.wait_ge(sem["hidden"], 4 * u)
                copy(M.gb, PS[:, 4, 0:T]).then_inc(sem["gate_copied"], 1)
                for ff in range(4):
                    act.wait_ge(sem["up_mm"], 4 * u + ff + 1)
                    if 4 * u + ff >= 2:
                        act.wait_ge(sem["hidden"], 4 * u + ff - 1)
                    f(M.e[:, ff % 2, :], PS[:, ff % 2, 0:T], ACT.Silu).then_inc(sem["gate_act"], 1)

            def final():
                squares()
                rsqrt(rr[:, :])
                act.wait_ge(sem["rows_turned"], 1)
                rows = v3(big, 0, 3, 1024)
                for t, (t0, n) in enumerate(SPANS):
                    i = copy(rows[0:n, t, :].rearrange("p (a n) -> p a n", a=2), PS[0:n, 2 * t:2 * t + 2, :])
                i.then_inc(sem["rows_copied"], 1)

            pre()
            barrier(act)
            with act.Fori(0, DEPTH):
                stage_a()
                barrier(act)
                stage_b()
                barrier(act)
                stage_gla()
                barrier(act)
                stage_ssd()
                barrier(act)
                with act.Fori(0, DB) as b:
                    seq_a(b)
                    seq_c(b)
                    barrier(act)
                stage_out()
                barrier(act)
                many = act.value_load(crowded[0:1, 0:1], min_val=0, max_val=1)
                with act.If(many > 0):
                    with act.Fori(0, NE // 4):
                        for u in range(4):
                            dense_expert(u)
                        barrier(act)
                with act.Else():
                    with act.Fori(0, NE // 4):
                        group()
                        barrier(act)
                barrier(act)
            final()
            barrier(act)

        @block.vector
        def _(dve):
            own[dve] = [sem["dve_step"], 0]
            V = nc.vector

            def c(ins):
                step(dve, ins)

            def tt(out, a, b, op):
                return V.tensor_tensor(out, a, b, op)

            def ts(out, a, s1, s2, op0, op1=None):
                return V.tensor_scalar(out, a, s1, s2, op0, op1) if op1 is not None else V.tensor_scalar(out, a, s1, None, op0)

            def stt(out, a, s, b, op0, op1):
                return V.scalar_tensor_tensor(out=out, in0=a, scalar=s, in1=b, op0=op0, op1=op1)

            M_, A_, S_ = ALU.mult, ALU.add, ALU.subtract

            def pre():
                c(V.memset(qzA_[:, :], 0.0))
                c(V.memset(qzC_[:, :], 0.0))
                c(V.memset(qb_[:, :], 0.0))
                c(V.memset(sm[:, :], 0.0))
                dve.wait_ge(loads, LOADS_PRE)
                c(V.tensor_copy(idxf[:, :], idxi[:, :]))
                c(stt(idxf[:, :], idxf[:, :], 16.0, K("sub").to_broadcast([128, 16]), M_, A_))
                dve.wait_ge(sem["silu_e"], 1)
                e, x = big[0:9, 5248:6272], big[0:9, 4096:5120]
                c(ts(e, e, 1.0, None, A_))
                c(V.reciprocal(e, e))
                tt(x, x, e, M_).then_inc(sem["rows_in"], 1)
                dve.wait_ge(sem["rows_T"], 1)
                V.tensor_copy(xT, PS[:, :, 0:T]).then_inc(sem["xp_done"], 1)
                dve.wait_ge(sem["c_T"], 1)
                V.tensor_copy(cT_[:, :], PS[:, 0, 0:72])
                V.tensor_copy(gfin[:, :], PS[:, 1, 0:8])

            def rsqrt(out, in_, n):
                v, t = (x[:, :] if len(out.shape) == 3 else x[:, 0:T] for x in (rv, rt))
                if len(out.shape) == 3:
                    v, t = (x.rearrange("p (a b) -> p a b", a=2) for x in (v, t))
                ts(v, in_, 1.0 / n, EPS, M_, A_).then_inc(sem["variance"], 1)
                dve.wait_ge(sem["variance"], 1)
                dve.wait_ge(sem["rstd"], 1)
                c(tt(t, out, out, M_))
                c(tt(t, t, v, M_))
                c(ts(t, t, -0.5, 1.5, M_, A_))
                c(tt(out, out, t, M_))

            def norm(g, shift):
                sc = v3(scaleT_, 0, 8, 9)
                c(tt(sc, modT[:, shift + 8:shift + 16, :], spread(vec[:, g:g + 8], 2, 9), M_))
                dve.wait_ge(sem["rms_mm"], 1)
                rsqrt(rr[:, :], PS[:, 1, 0:T], DM)
                c(tt(mT, xT, spread(rr[:, :], 1, KT8), M_))
                hp = mT[:, :, 0:SEQ]
                c(tt(hp, hp, sc[:, :, 0:1].to_broadcast([128, 8, SEQ]), M_))
                c(tt(hp, hp, modT[:, shift:shift + 8, 0:1].to_broadcast([128, 8, SEQ]), A_))
                hs = mT[:, :, SEQ:T].rearrange("p k (b i) -> p k b i", b=DB)
                c(tt(hs, hs, spread(sc[:, :, 1:9], 3, 8), M_))
                tt(hs, hs, spread(modT[:, shift:shift + 8, 1:9], 3, 8), A_).then_inc(sem["h_done"], 1)
                dve.wait_ge(sem["h_done"], 1)

            def stage_a():
                c(V.memset(XP[:, :, 0:3], 0.0))
                c(V.tensor_copy(idxu[:, :], idxf[:, :]))
                c(ts(idxf[:, :], idxf[:, :], float(N_POOL * 16), None, A_))
                dve.wait_ge(sem["vec_T"], 1)
                c(V.tensor_copy(vec[:, :], PS[:, 1, 0:NVEC]))
                dve.wait_ge(sem["convT_mm"], 1)
                V.tensor_copy(XPs[:, :, :, 0:3], PS[:, 2, 0:96].rearrange("p (c b k) -> p c b k", c=4, b=DB)).then_inc(sem["xp_done"], 1)
                dve.wait_ge(sem["xp_done"], 1)
                dve.wait_ge(sem["mod_mm"], 1)
                c(tt(modT, PS[:, 0, 0:432].rearrange("p (m s) -> p m s", s=9), spread(vec[:, 0:48], 2, 9), A_))
                c(ts(modT[:, 8:16, :], modT[:, 8:16, :], 1.0, None, A_))
                ts(modT[:, 32:40, :], modT[:, 32:40, :], 1.0, None, A_).then_inc(sem["mod_done"], 1)
                dve.wait_ge(sem["mod_done"], 1)
                norm(48, 0)

            def stage_b():
                tail = v3(big, SCR, 4, 27)
                c(V.tensor_copy(tail[:, :, 0:3], XP[:, :, 256:259]))
                for k in range(4):
                    i = V.tensor_copy(tail[:, k, 3:27].rearrange("p (b k) -> p b k", b=DB), XPs[:, k, :, 8:11])
                    if k < 3:
                        c(i)
                    else:
                        i.then_inc(sem["pre_T"], 1)
                        dve.wait_ge(sem["pre_T"], 1)
                dve.wait_ge(sem["turn_mm"], 1)
                t1 = v3(big, SCR + 512, 4, T)
                c(tt(t1, PS[:, 0:4, 0:T], spread(K("sin"), 1, 4), M_))
                c(tt(PT[:, 0:4, :], PT[:, 0:4, :], spread(K("cos"), 1, 4), M_))
                tt(PT[:, 0:4, :], PT[:, 0:4, :], t1, A_).then_inc(sem["rope_done"], 1)
                dve.wait_ge(sem["rope_done"], 1)
                for qz, q in ((qzA, AQ), (qzC, CQ)):
                    c(V.tensor_copy(qz[0:64, 0:4:2, :], PT[0:64, q:q + 2, :]))
                    c(V.tensor_copy(qz[64:128, 1:4:2, :], PT[64:128, q:q + 2, :]))
                c(V.tensor_copy(kS[:, 0:2, :], PT[:, AK:AK + 2, SEQ:T]))
                V.tensor_copy(kS[:, 2:4, :], PT[:, CK:CK + 2, SEQ:T]).then_inc(sem["qz_done"], 1)
                dve.wait_ge(sem["qz_done"], 1)
                s, t = v3(big, SCR, 4, 512), v3(big, SCR + 2048, 4, 512)
                s8, t8 = v3(big, SCR, 8, 256), v3(big, SCR + 2048, 8, 256)
                dve.wait_ge(sem["a_scores_mm"], 1)
                dve.wait_ge(sem["tail27_mm"], 1)
                c(tt(s, PS[:, 0:4, :], spread(K("cap_a"), 1, 4), ALU.min))
                c(V.tensor_reduce(sm[:, 24:32], s8, AX.X, ALU.max))
                ts(sm[:, 24:32], sm[:, 24:32], -HD ** -0.5, None, M_).then_inc(sem["a_max"], 1)
                dve.wait_ge(sem["a_max"], 1)
                dve.wait_ge(sem["a_exp"], 1)
                c(stt(s, spread(K("cap_a"), 1, 4), 1.0 / BIG_F, s, M_, M_))
                c(V.tensor_reduce(sm[:, 24:32], s8, AX.X, ALU.add))
                c(V.reciprocal(sm[:, 24:32], sm[:, 24:32]))
                tt(s8, s8, spread(sm[:, 24:32], 2, 256), M_).then_inc(sem["a_probs"], 1)
                dve.wait_ge(sem["a_probs"], 1)
                dve.wait_ge(sem["c_logits"], 1)
                c(tt(s, s, spread(K("cap_c"), 1, 4), ALU.min))
                stt(t, s, -1.0, s, M_, ALU.max).then_inc(sem["c_abs"], 1)
                dve.wait_ge(sem["c_abs"], 1)
                dve.wait_ge(sem["c_log"], 1)
                c(stt(t, s, 0.0, t, ALU.max, A_))
                for j in range(8):
                    x = t8[:, j, ::-1]
                    i = V.tensor_tensor_scan(x, K("ones1").to_broadcast([128, 256]), x, 0.0, M_, A_)
                c(i)
                tt(s, s, t, S_).then_inc(sem["c_exponents"], 1)
                dve.wait_ge(sem["c_exponents"], 1)

            def stage_gla(l):
                G = gla
                c(V.memset(G.qgz, 0.0))
                dve.wait_ge(sem["gate_logits"], 1)
                stt(G.cum, G.la, -1.0, G.la, M_, ALU.max).then_inc(sem["gate_abs"], 1)
                dve.wait_ge(sem["gate_abs"], 1)
                dve.wait_ge(loads, l * LOADS + LOADS_PRE + LOADS_A + LOADS_B)
                c(tt(G.st0.rearrange("p b (h v) -> p b h v", h=4), spread(G.raw, 2, 4),
                     spread(K("diag_gla").rearrange("p (h v) -> p h v", h=4), 1, DB), M_))
                dve.wait_ge(sem["gate_log"], 1)
                c(stt(G.la, G.la, 0.0, G.cum, ALU.min, S_))
                c(ts(G.la, G.la, 1.0 / 16.0, None, M_))
                c(V.tensor_tensor_scan(G.cum, K("reset"), G.la, 0.0, M_, A_))
                for a, b_, n, w in ((0, SEQ, 4, 64), (SEQ, T, 8, 8)):
                    x = G.cum[:, a:b_].rearrange("p (n w) -> p n w", w=w)
                    y = G.el[:, a:b_].rearrange("p (n w) -> p n w", w=w)
                    i = tt(y, x[:, :, w - 1:w].to_broadcast([128, n, w]), x, S_)
                    if a == 0:
                        c(i)
                    else:
                        i.then_inc(sem["gla_cum"], 1)
                        dve.wait_ge(sem["gla_cum"], 1)
                dve.wait_ge(sem["gla_exps"], 1)
                c(stt(G.qg, PT[:, BQ, :], 32 ** -0.5, G.ec, M_, M_))
                for h in range(4):
                    c(V.tensor_copy(G.qgz[32 * h:32 * h + 32, h, :], G.qg[32 * h:32 * h + 32, :]))
                c(V.tensor_copy(G.last[:, 0:4], G.ec[:, 63:SEQ:64]))
                c(V.tensor_copy(G.last[:, 4:12], G.ec[:, SEQ + 7:T:8]))
                c(tt(G.kg, PT[:, BK, :], G.en, M_))
                tt(G.kdT, PT[:, BK, :], G.el, M_).then_inc(sem["gla_operands"], 1)
                dve.wait_ge(sem["gla_operands"], 1)
                dve.wait_ge(sem["gla_scores_mm"], 1)
                for t, (t0, n) in enumerate(SPANS):
                    tri = K("tri8") if t == 2 else K("tri64")
                    c(tt(G.att[0:n, t, 0:4 * n].rearrange("p (h t) -> p h t", h=4), PS[0:n, t, 0:4 * n].rearrange("p (h t) -> p h t", h=4),
                         spread(tri[0:n, 0:n], 1, 4), M_))
                c(V.tensor_copy(G.kdt[:, 0:2, :], PS[:, 3, 0:256].rearrange("p (t n) -> p t n", t=2)))
                c(V.tensor_copy(G.kdt[0:64, 2, :], PS[0:64, 3, 256:384]))
                tt(G.kdm[0:64], spread(G.kdt[0:64, 2, :], 1, DB), spread(K("seq_of")[0:64], 2, 128), M_).then_inc(sem["gla_scores_masked"], 1)
                dve.wait_ge(sem["gla_scores_masked"], 1)
                dve.wait_ge(sem["gla_kv_mm"], 1)
                d4 = spread(K("diag_gla"), 1, 2)
                for k in range(2):
                    x = PS[:, 4 + k, :].rearrange("p (j n) -> p j n", j=2)
                    c(tt(x, x, d4, M_))
                c(V.tensor_copy(G.stp[:, 0, :], PS[:, 4, 0:256]))
                for j in range(1, 4):
                    i = stt(G.stp[:, j, :], G.stp[:, j - 1, :], G.last[:, j:j + 1], PS[:, 4 + j % 2, (j // 2) * 256:(j // 2) * 256 + 256], M_, A_)
                    if j < 3:
                        c(i)
                    else:
                        i.then_inc(sem["gla_states"], 1)
                        dve.wait_ge(sem["gla_states"], 1)
                x = PSF[:, 0:2048].rearrange("p (b n) -> p b n", b=DB)
                c(tt(x, x, spread(K("diag_gla"), 1, DB), M_))
                dve.wait_ge(sem["gla_out_mm"], 1)
                c(tt(G.st0, G.st0, spread(G.last[:, 4:12], 2, 256), M_))
                tt(G.st0, G.st0, x, A_).then_inc(sem["gla_final_states"], 1)
                dve.wait_ge(sem["gla_final_states"], 1)
                c(V.tensor_copy(G.o, PS[:, 6:8, 0:T]))
                tt(G.sq, G.o, G.o, M_).then_inc(sem["mixer_squares"], 1)
                dve.wait_ge(sem["mixer_squares"], 1)
                dve.wait_ge(sem["silu_exp"], 1)
                c(ts(G.qgz, G.qgz, 1.0, None, A_))
                c(V.reciprocal(G.qgz, G.qgz))
                c(tt(PT[:, GATE:GATE + 4, :], PT[:, GATE:GATE + 4, :], G.qgz, M_))
                dve.wait_ge(sem["mixer_norm_mm"], 1)
                rsqrt(G.sq, PS[:, 0:2, 0:T], HD)
                c(stt(G.o, G.o, vec[:, 87:88], G.sq, M_, M_))
                c(tt(mT[:, 2:4, :], G.o, PT[:, GATE:GATE + 2, :], M_))

            def stage_ssd():
                D = ssd
                c(tt(D.v, v3(sm, 0, 3, 4), spread(bc[:, 4:8], 1, 3), A_))
                c(stt(D.tt, D.v, -1.0, D.v, M_, ALU.max))
                for k in range(4):
                    w = lambda j: vec[:, 64 + 4 * j + k:65 + 4 * j + k]
                    xp, xs = D.xc[:, k, 0:SEQ], D.xc[:, k, SEQ:T].rearrange("p (b i) -> p b i", b=DB)
                    c(ts(xp, XP[:, k, 0:256], w(0), vec[:, 80 + k:81 + k], M_, A_))
                    c(ts(xs, XPs[:, k, :, 0:8], w(0), vec[:, 80 + k:81 + k], M_, A_))
                    for j in range(1, 4):
                        c(stt(xp, XP[:, k, j:j + 256], w(j), xp, M_, A_))
                        i = stt(xs, XPs[:, k, :, j:j + 8], w(j), xs, M_, A_)
                        if (k, j) != (3, 3):
                            c(i)
                        else:
                            i.then_inc(sem["conv_done"], 1)
                            dve.wait_ge(sem["conv_done"], 1)
                c(V.memset(D.cz, 0.0))
                dve.wait_ge(sem["conv_exp"], 1)
                c(ts(D.ex, D.ex, 1.0, None, A_))
                c(V.reciprocal(D.ex, D.ex))
                c(tt(D.xc, D.xc, D.ex, M_))
                c(V.tensor_copy(D.cz[0:64, 0, :], D.xc[0:64, 3, :]))
                V.tensor_copy(D.cz[64:128, 1, :], D.xc[64:128, 3, :]).then_inc(sem["conv_silu"], 1)
                dve.wait_ge(sem["conv_silu"], 1)
                dve.wait_ge(sem["dt_exp"], 1)
                ts(D.w1, D.u, 1.0, None, A_).then_inc(sem["dt_plus1"], 1)
                dve.wait_ge(sem["dt_plus1"], 1)
                c(ts(D.d, D.w1, -1.0, None, A_))
                c(ts(D.eq, D.d, 0.0, None, ALU.is_equal))
                c(tt(D.d, D.d, D.eq, A_))
                c(V.reciprocal(D.d, D.d))
                c(tt(D.u, D.u, D.d, M_))
                dve.wait_ge(sem["dt_log"], 1)
                c(tt(D.l, D.l, D.eq, A_))
                c(tt(D.u, D.u, D.l, M_))
                c(stt(D.dt, D.v, 0.0, D.u, ALU.max, A_))
                stt(D.da, D.dt, -1.0, spread(D.alog, 1, 3), M_, M_).then_inc(sem["log_decays"], 1)
                dve.wait_ge(sem["log_decays"], 1)
                dve.wait_ge(sem["xb_turned"], 1)
                c(V.tensor_copy(D.tok[:, 0:2, :], PS[:, 0:2, 0:384]))
                c(V.tensor_copy(D.tok[0:64, 2, :], PS[0:64, 2, 0:384]))
                dve.wait_ge(sem["ssm_in_copied"], 1)
                V.tensor_copy(D.dab, spread(D.da, 3, 128)).then_inc(sem["decays_spread"], 1)
                dve.wait_ge(sem["decays_spread"], 1)
                c(V.memset(D.cum, 0.0))
                c(V.memset(D.w, 0.0))
                dve.wait_ge(sem["cum_mm"], 1)
                for n, t in ((128, slice(0, 2)), (64, slice(2, 3))):
                    cs = slice(4 * t.start, 4 * t.stop)
                    c(V.tensor_copy(D.cum[0:n, t, :].rearrange("p a b -> p (a b)"), PS[0:n, 5, cs]))
                    i = tt(D.w[0:n, t, :].rearrange("p a b -> p (a b)"), PS[0:n, 5, 16 + cs.start:16 + cs.stop], D.cum[0:n, t, :].rearrange("p a b -> p (a b)"), S_)
                    if n == 128:
                        c(i)
                    else:
                        i.then_inc(sem["decay_left"], 1)
                        dve.wait_ge(sem["decay_left"], 1)
                dve.wait_ge(sem["cum_exps"], 1)
                for t, (t0, n) in enumerate(SPANS):
                    d = D.dec[0:n, t, :, 0:n]
                    tri = K("tri8c") if t == 2 else K("tri64c")
                    c(tt(d, PS[0:n, 0:4, t0:t0 + n], spread(D.cum[0:n, t, :], 2, n), S_))
                    i = tt(d, d, spread(tri[0:n, 0:n], 1, 4), ALU.min)
                    if t < 2:
                        c(i)
                    else:
                        i.then_inc(sem["decay_args"], 1)
                        dve.wait_ge(sem["decay_args"], 1)
                dve.wait_ge(sem["decay_left_exp"], 1)
                for n, t in ((128, slice(0, 2)), (64, slice(2, 3))):
                    k = t.stop - t.start
                    x = D.tok[0:n, t, 0:256].rearrange("p t (h q) -> p t h q", h=4)
                    xd, xw = (v[0:n, t, :].rearrange("p t (h q) -> p t h q", h=4) for v in (D.xdt, D.xw))
                    c(tt(xd, x, spread(D.dt[0:n, t, :], 3, 64), M_))
                    c(tt(xw, xd, spread(D.w[0:n, t, :], 3, 64), M_))
                c(tt(D.bm[0:64], spread(D.tok[0:64, 2, 256:384], 1, DB), spread(K("seq_of")[0:64], 2, 128), M_))
                dve.wait_ge(sem["cum_exps"], 1)
                tt(D.ce.rearrange("p (g x) t -> p g x t", g=2), spread(D.cz, 2, 2), D.ec.rearrange("p (g x) t -> p g x t", g=2), M_).then_inc(sem["ssd_operands"], 1)
                dve.wait_ge(sem["ssd_operands"], 1)
                for g in range(2):
                    r = slice(64 * g, 64 * g + 64)
                    c(V.tensor_copy(D.last[r, 0:4, :].rearrange("p j h -> p h j"), D.ec[r, 2 * g:2 * g + 2, 63:SEQ:64]))
                    c(V.tensor_copy(D.last[r, 4:12, :].rearrange("p j h -> p h j"), D.ec[r, 2 * g:2 * g + 2, SEQ + 7:T:8]))
                dve.wait_ge(sem["decay_exps"], 1)
                dve.wait_ge(sem["cb_sample_mm"], 1)
                for t, (t0, n) in enumerate(SPANS):
                    bank = (6, 7, 4)[t]
                    d = D.dec[0:n, t, :, 0:n].rearrange("p (g x) t -> p g x t", g=2)
                    c(tt(d, d, spread(PS[0:n, bank, 0:2 * n].rearrange("p (g t) -> p g t", g=2), 2, 2), M_))
                dve.wait_ge(sem["bx_mm"], 1)
                hp = lambda x: x.rearrange("p (h q) -> p h q", h=2)
                c(V.tensor_copy(D.stp[:, 0, :], PS[:, 0, 0:128]))
                for j in range(1, 4):
                    c(tt(hp(D.stp[:, j, :]), hp(D.stp[:, j - 1, :]), spread(D.last[:, j, :], 2, 64), M_))
                    i = tt(D.stp[:, j, :], D.stp[:, j, :], PS[:, j % 2, (j // 2) * 128:(j // 2) * 128 + 128], A_)
                    if j < 3:
                        c(i)
                    else:
                        i.then_inc(sem["ssm_states"], 1)
                        dve.wait_ge(sem["ssm_states"], 1)
                dve.wait_ge(sem["ssd_out_mm"], 1)
                c(tt(D.st0.rearrange("p b (h q) -> p b h q", h=2), D.st0.rearrange("p b (h q) -> p b h q", h=2),
                     spread(D.last[:, 4:12, :], 3, 64), M_))
                tt(D.st0, D.st0, PSF[:, 1024:2048].rearrange("p (b n) -> p b n", b=DB), A_).then_inc(sem["ssm_final"], 1)
                dve.wait_ge(sem["ssm_final"], 1)
                c(V.tensor_copy(D.dsk[0:64, :], bc[0:64, 12:16:2]))
                c(V.tensor_copy(D.dsk[64:128, :], bc[64:128, 13:16:2]))
                for k in range(2):
                    c(stt(D.y[:, k, :], D.xc[:, k, :], D.dsk[:, k:k + 1], PS[:, 6 + k, 0:T], M_, A_))
                c(tt(D.y, D.y, PT[:, Z:Z + 2, :], M_))
                tt(D.sq, D.y, D.y, M_).then_inc(sem["mixer_squares"], 1)
                dve.wait_ge(sem["mixer_squares"], 1)
                dve.wait_ge(sem["mixer_norm_mm"], 1)
                rsqrt(rr[:, :], PS[:, 3, 0:T], 256)
                for k in range(2):
                    c(stt(mT[:, 6 + k, :], D.y[:, k, :], vec[:, 84 + k:85 + k], rr[:, :], M_, M_))

            def queries(qz, b, name):
                qb = v3(qb_, 0, 2, 32)
                for k in range(2):
                    i = V.tensor_copy(qb[:, k, 16 * k:16 * k + 16].rearrange("p (h i) -> p h i", h=2),
                                      qz[:, 2 * k:2 * k + 2, bass.ds(SEQ + b * 8, 8)])
                    if k == 0:
                        c(i)
                    else:
                        i.then_inc(sem[name], 1)
                        dve.wait_ge(sem[name], 1)

            def seq_a(b):
                Q = seq
                queries(qzA, b, "a_queries")
                dve.wait_ge(sem["a_keys_turned"], 1)
                kt = Q.kT[:, 0, 0:768].rearrange("p (a n) -> p a n", a=2)
                V.tensor_copy(kt, PS[:, 0:2, 0:384]).then_inc(sem["a_keys_copied_dve"], 1)
                V.tensor_copy(Q.kT[:, 0, 768:1280], PS[:, 2, :]).then_inc(sem["a_keys_copied_dve"], 1)
                dve.wait_ge(sem["a_scores_mm"], 1)
                new = K("cap_na", 32)[:, bass.ds(b * NS, NS)]
                c(tt(Q.s[:, 0:NA], PSF[0:32, 0:NA], K("cap_sa", 32), ALU.min))
                c(tt(Q.s[:, NA:NA + NS], PSF[0:32, NA:NA + NS], new, ALU.min))
                c(V.tensor_reduce(sm[0:32, 24:25], Q.s[:, 0:NA + NS], AX.X, ALU.max))
                ts(sm[0:32, 24:25], sm[0:32, 24:25], -HD ** -0.5, None, M_).then_inc(sem["a_max"], 1)
                dve.wait_ge(sem["a_max"], 1)
                queries(qzC, b, "c_queries")
                dve.wait_ge(sem["a_exp"], 1)
                c(stt(Q.s[:, 0:NA], K("cap_sa", 32), 1.0 / BIG_F, Q.s[:, 0:NA], M_, M_))
                c(stt(Q.s[:, NA:NA + NS], new, 1.0 / BIG_F, Q.s[:, NA:NA + NS], M_, M_))
                c(V.tensor_reduce(sm[0:32, 25:26], Q.s[:, 0:NA + NS], AX.X, ALU.add))
                c(V.reciprocal(sm[0:32, 25:26], sm[0:32, 25:26]))
                ts(Q.s[:, 0:NA + NS], Q.s[:, 0:NA + NS], sm[0:32, 25:26], None, M_).then_inc(sem["a_probs"], 1)
                dve.wait_ge(sem["a_probs"], 1)

            def seq_c(b):
                Q = seq
                for n in range(1, 8, 2):
                    dve.wait_ge(sem["c_keys_turned"], n + 1)
                    k, g, jh = n // 4, (n // 2) % 2, n % 2
                    V.tensor_copy(Q.kt8(k, g, jh), PS[:, 3 + n % 3, :].rearrange("p (j q) -> p j q", j=4)).then_inc(sem["c_keys_copied_dve"], 1)
                dve.wait_ge(sem["c_logits"], 1)
                x = Q.s[:, 2048:2112]
                c(tt(x, x, K("cap_nc", 32)[:, bass.ds(b * NS, NS)], ALU.min))
                stt(Q.t, Q.s, -1.0, Q.s, M_, ALU.max).then_inc(sem["c_abs"], 1)
                dve.wait_ge(sem["c_abs"], 1)
                dve.wait_ge(sem["c_log"], 1)
                c(stt(Q.t, Q.s, 0.0, Q.t, ALU.max, A_))
                x = Q.t[:, ::-1]
                c(V.tensor_tensor_scan(x, K("ones1", 32).to_broadcast([32, 2112]), x, 0.0, M_, A_))
                tt(Q.s, Q.s, Q.t, S_).then_inc(sem["c_exponents"], 1)
                dve.wait_ge(sem["c_exponents"], 1)

            def stage_out():
                c(V.memset(moe.y, 0.0))
                c(V.memset(moe.L, 0.0))
                tmp = rr[:, 0:64].rearrange("p (b i) -> p b i", b=DB)
                for k in range(8):
                    dve.wait_ge(sem["proj_mm"], k + 1)
                    o = PS[:, 4 + k % 4, 0:T]
                    c(stt(xT[:, k, 0:SEQ], o[:, 0:SEQ], modT[:, 16 + k, 0:1], xT[:, k, 0:SEQ], M_, A_))
                    c(tt(tmp, o[:, SEQ:T].rearrange("p (b i) -> p b i", b=DB), spread(modT[:, 16 + k, 1:9], 2, 8), M_))
                    tt(xT[:, k, SEQ:T], xT[:, k, SEQ:T], rr[:, 0:64], A_).then_inc(sem["proj_ev"], 1)
                    dve.wait_ge(sem["proj_ev"], k + 1)
                norm(56, 24)
                Mo = moe
                dve.wait_ge(sem["router_mm"], 1)
                for n, t in ((128, slice(0, 2)), (64, slice(2, 3))):
                    k = t.stop - t.start
                    c(tt(Mo.L[0:n, t, :], PS[0:n, 2, 36 * t.start:36 * t.stop].rearrange("p (t n) -> p t n", n=36),
                         spread(bc[0:n, 16:52], 1, k), A_))
                gl, el = Mo.L[:, :, 0:4], Mo.L[:, :, 4:36].rearrange("p t (g e) -> p t g e", g=4)

                def first_max(values, mx, hot, n):
                    tmp = Mo.tmp[:, :, 0:n]
                    c(V.tensor_reduce(mx, values, AX.X, ALU.max))
                    c(tt(tmp, values, spread(mx, 2, n), ALU.is_equal))
                    c(tt(tmp, tmp, spread(K("rev")[:, 0:n], 1, 3), M_))
                    c(V.tensor_reduce(Mo.km, tmp, AX.X, ALU.max))
                    c(tt(hot, tmp, spread(Mo.km, 2, n), ALU.is_equal))

                first_max(gl, Mo.gmax, Mo.ghot, 4)
                tt(Mo.gx, gl, spread(Mo.gmax, 2, 4), S_).then_inc(sem["group_args"], 1)
                dve.wait_ge(sem["group_args"], 1)
                c(tt(Mo.gt4, el, spread(Mo.ghot, 3, 8), M_))
                c(V.tensor_reduce(Mo.e8, Mo.gt4.rearrange("p t g e -> p t e g"), AX.X, ALU.add))
                first_max(Mo.e8, Mo.m1, Mo.h1, 8)
                c(stt(Mo.e8, Mo.h1, NEG, Mo.e8, M_, A_))
                first_max(Mo.e8, Mo.m2, Mo.h2, 8)
                tt(Mo.dx, Mo.m2, Mo.m1, S_).then_inc(sem["pair_args"], 1)
                dve.wait_ge(sem["pair_args"], 1)
                dve.wait_ge(sem["group_exps"], 1)
                c(V.tensor_reduce(Mo.gp, Mo.gx, AX.X, ALU.add))
                dve.wait_ge(sem["pair_exps"], 1)
                c(ts(Mo.m1, Mo.dx, 1.0, None, A_))
                c(tt(Mo.m1, Mo.m1, Mo.gp, M_))
                c(V.reciprocal(Mo.m1, Mo.m1))
                c(tt(Mo.m2, Mo.m1, Mo.dx, M_))
                c(tt(Mo.h1, Mo.h1, spread(Mo.m1, 2, 8), M_))
                c(tt(Mo.h2, Mo.h2, spread(Mo.m2, 2, 8), M_))
                c(tt(Mo.h1, Mo.h1, Mo.h2, A_))
                tt(Mo.gt4, spread(Mo.ghot, 3, 8), spread(Mo.h1, 2, 4), M_).then_inc(sem["gates_done"], 1)
                dve.wait_ge(sem["gates_done"], 1)
                step(dve, ts(Mo.sel, Mo.gt, 0.0, None, ALU.is_gt))
                V.tensor_copy(Mo.selc, Mo.sel).then_inc(sem["selected"], 1)
                dve.wait_ge(sem["gates_turned"], 1)
                c(V.tensor_copy(Mo.gT[0:32, :], PS[0:32, 3, 0:T]))
                dve.wait_ge(sem["ranks_mm"], 1)
                c(ts(Mo.rank, Mo.selc, -1000.0, 1000.0, M_, A_))
                for n, t in ((128, slice(0, 2)), (64, slice(2, 3))):
                    c(tt(Mo.rank[0:n, t, :], Mo.rank[0:n, t, :],
                         PS[0:n, 4, 32 * t.start:32 * t.stop].rearrange("p (t n) -> p t n", n=32), A_))
                c(V.tensor_reduce(Mo.km[:, 0:1], PS[:, 4, 96:128], AX.X, ALU.max))
                c(ts(Mo.km[:, 0:1], Mo.km[:, 0:1], float(SLOTS), None, ALU.is_gt))
                c(V.tensor_copy(crowded[:, :], Mo.km[:, 0:1]))

            def group(it):
                Mo = moe
                for n, t in ((128, slice(0, 2)), (64, slice(2, 3))):
                    k = t.stop - t.start
                    for j in range(t.start, t.stop):
                        rank = Mo.rank[0:n, j, bass.ds(it * GE, GE)]
                        i = tt(Mo.pick[0:n, j, :].rearrange("p (e s) -> p e s", e=GE), spread(K("iota")[0:n], 1, GE), spread(rank, 2, SLOTS), ALU.is_equal)
                        if j < 2:
                            c(i)
                i.then_inc(sem["picks"], 1)
                dve.wait_ge(sem["picks"], 1)
                for j, (t0, n) in enumerate(SPANS):
                    gate = Mo.gt[0:n, j, bass.ds(it * GE, GE)]
                    i = tt(Mo.wpick[0:n, j, :].rearrange("p (e s) -> p e s", e=GE), Mo.pick[0:n, j, :].rearrange("p (e s) -> p e s", e=GE),
                           spread(gate, 2, SLOTS), M_)
                    if j < 2:
                        c(i)
                i.then_inc(sem["weighted_picks"], 1)
                for pair, n_up in enumerate((2, 4)):
                    dve.wait_ge(sem["gate_act"], pair + 1)
                    dve.wait_ge(sem["pair_mm"], n_up)
                    tt(Mo.hid[:, pair, :], Mo.silu[:, pair, :], PS[:, 2 * pair + 1, :], M_).then_inc(sem["hidden"], 1)
                for d in range(8):
                    dve.wait_ge(sem["slot_sum_mm"], d + 1)
                    tt(Mo.y[:, d, :], Mo.y[:, d, :], PS[:, 6 + d % 2, 0:T], A_).then_inc(sem["down_added"], 1)

            def dense_group(it):
                Mo = moe
                for u in range(GE):
                    if u:
                        dve.wait_ge(sem["gate_mm"], u)
                    ts(Mo.gm[0:32, :], Mo.gT[0:32, :], ident[0:32, bass.ds(it * GE + u, 1)], None, M_).then_inc(sem["gate_row"], 1)
                    dve.wait_ge(sem["gate_copied"], u + 1)
                    for ff in range(4):
                        e = Mo.e[:, ff % 2, :]
                        dve.wait_ge(sem["gate_act"], 4 * u + ff + 1)
                        c(tt(e, e, PS[:, 2 + ff % 2, 0:T], M_))
                        tt(Mo.a[:, 4 * u + ff, :], e, Mo.gb, M_).then_inc(sem["hidden"], 1)
                        dve.wait_ge(sem["hidden"], 4 * u + ff + 1)
                for u in range(GE):
                    for d in range(8):
                        dve.wait_ge(sem["down_mm"], 8 * u + d + 1)
                        tt(Mo.y[:, d, :], Mo.y[:, d, :], PS[:, 4 + d % 4, 0:T], A_).then_inc(sem["down_added"], 1)

            def add_moe():
                y = moe.y
                c(tt(y[:, :, 0:SEQ], y[:, :, 0:SEQ], modT[:, 40:48, 0:1].to_broadcast([128, 8, SEQ]), M_))
                ys = y[:, :, SEQ:T].rearrange("p k (b i) -> p k b i", b=DB)
                c(tt(ys, ys, spread(modT[:, 40:48, 1:9], 3, 8), M_))
                c(tt(xT, xT, y, A_))

            def final():
                dve.wait_ge(sem["rms_mm"], 1)
                rsqrt(rr[:, :], PS[:, 1, 0:T], DM)
                c(tt(mT, xT, spread(rr[:, :], 1, KT8), M_))
                tt(mT, mT, spread(gfin[:, :], 2, T), M_).then_inc(sem["h_done"], 1)
                dve.wait_ge(sem["h_done"], 1)

            pre()
            barrier(dve)
            with dve.Fori(0, DEPTH) as l:
                stage_a()
                barrier(dve)
                stage_b()
                barrier(dve)
                stage_gla(l)
                barrier(dve)
                stage_ssd()
                barrier(dve)
                with dve.Fori(0, DB) as b:
                    seq_a(b)
                    seq_c(b)
                    barrier(dve)
                stage_out()
                barrier(dve)
                many = dve.value_load(crowded[0:1, 0:1], min_val=0, max_val=1)
                with dve.If(many > 0):
                    with dve.Fori(0, NE // 4) as it:
                        dense_group(it)
                        barrier(dve)
                with dve.Else():
                    with dve.Fori(0, NE // 4) as it:
                        group(it)
                        barrier(dve)
                add_moe()
                barrier(dve)
            final()
            barrier(dve)

        @block.gpsimd
        def _(pool):
            own[pool] = [sem["pool_step"], 0]
            def dma(out, in_, sem):
                pool.dma_start(out, in_).then_inc(sem, 16)

            def pre():
                dma(cst[:, :], consts, loads)
                rows = v3(big, 0, 3, 1024)
                dma(rows[:, 0:2, :], x_rows[0:256].rearrange("(t p) c -> p t c", p=128), loads)
                dma(rows[0:64, 2, :], x_rows[256:T], loads)
                dma(big[0:9, 4096:5120], c_rows, loads)
                dma(big[0:8, 5120:5248], g_final.rearrange("(k p) -> k p", p=128), loads)
                for t in range(8):
                    src = pages.rearrange("b (g t) -> t (b g)", t=8)[t:t + 1, :]
                    pool.dma_start(idxi[16 * t:16 * t + 16, :], src.to_broadcast([16, 16]), allow_slow_non_contiguous=True).then_inc(loads, 16)
                pool.wait_ge(loads, LOADS_PRE)

            def stage_a(l):
                dma(vrow[0:NVEC, :], vecs[l], loads)
                dma(bc[:, :], bcs[bass.ds(l, 1), :].to_broadcast([128, 52]), loads)
                for h in range(4):
                    dma(bsb[8 * h:8 * h + 8, :], b_sb[bass.ds(l, 1), h:h + 1].to_broadcast([8, 1]), loads)
                dma(wtail, w_tail[l].rearrange("(k p) n -> p k n", p=128), loads)
                dma(wr, w_router[l].rearrange("(k p) n -> p k n", p=128), loads)
                dma(wa2[0:16, :], w_a2[l], loads)
                dma(big[0:24, SCR + 2560:SCR + 3072], st_conv[l].rearrange("b k c -> (b k) c"), loads)
                pool.wait_ge(loads, l * LOADS + LOADS_PRE + LOADS_A)

            def stage_b(l):
                pool.wait_ge(sem["tail27_ev"], 1)
                dma(cv_p[l, 0], cvo[0:3, :], outputs)
                dma(cv_s[l].rearrange("b k c -> (b k) c"), cvo[3:27, :], outputs)
                for n, (buf, op, os) in enumerate(((kA, wk_p, wk_s), (vA, wv_p, wv_s), (None, None, None), (kC, sk_p, sk_s), (vC, sv_p, sv_s))):
                    if buf is None:
                        continue
                    pool.wait_ge(sem["tok_ev"], n + 1)
                    dma(op[l].rearrange("(t p) c -> p t c", p=128), buf[:, 0:2, :], outputs)
                    dma(os[l], buf[0:64, 2, :], outputs)
                pool.wait_ge(outputs, l * OUTS + OUTS_B)

            def stage_gla(l):
                G = gla
                dma(G.raw, st_gla[l].rearrange("b h k v -> (h k) b v"), loads)
                pool.wait_ge(sem["gla_final_states"], 1)
                for h in range(4):
                    dma(gla_p[l, 0, h], G.stp[32 * h:32 * h + 32, 3, 64 * h:64 * h + 64], outputs)
                    dma(gla_s[l, :, h].rearrange("b k v -> k b v"), G.st0[32 * h:32 * h + 32, :, 64 * h:64 * h + 64], outputs)
                pool.wait_ge(outputs, l * OUTS + OUTS_B + OUTS_G)

            def stage_ssd(l):
                D = ssd
                for g in range(2):
                    dma(D.raw[:, :, 64 * g:64 * g + 64], st_ssm[l, :, 2 * g:2 * g + 2].rearrange("b h p n -> (h p) b n"), loads)
                pool.wait_ge(sem["ssm_out_copied"], 1)
                ob = D.outb.rearrange("p (j n) -> p j n", j=9)
                for g in range(2):
                    dma(ssm_p[l, 0, 2 * g:2 * g + 2].rearrange("h p n -> (h p) n"), ob[:, 0, 64 * g:64 * g + 64], outputs)
                    dma(ssm_s[l, :, 2 * g:2 * g + 2].rearrange("b h p n -> (h p) b n"), ob[:, 1:9, 64 * g:64 * g + 64], outputs)
                pool.wait_ge(outputs, l * OUTS + OUTS)

            def gather(cache, off, sem):
                for g in range(2):
                    i = pool.indirect_dma_start(
                        out=big[:, off + 2048 * g:off + 2048 * g + 2048], out_offset=None, in_=cache,
                        in_offset=bass.IndirectOffsetOnAxis(ap=idxb[:, g:g + 1], axis=0))
                    i.then_inc(sem, 16)

            def seq_step(l, b):
                step(pool, nc.gpsimd.tensor_copy(idxb[:, :], idxu[:, bass.ds(b * 2, 2)]))
                pool.wait_ge(sem["a_keys_turned"], 2)
                gather(sb_k, 0, gathered_k)
                pool.wait_ge(sem["a_out_mm"], 1)
                gather(sb_v, 4096, gathered_v)
                pool.wait_ge(gathered_k, (l * DB + b + 1) * 32)
                pool.wait_ge(gathered_v, (l * DB + b + 1) * 32)

            def final():
                pool.wait_ge(sem["rows_copied"], 1)
                rows = v3(big, 0, 3, 1024)
                dma(y_p.rearrange("(t p) c -> p t c", p=128), rows[:, 0:2, :], outputs)
                dma(y_s, rows[0:64, 2, :], outputs)
                pool.wait_ge(outputs, DEPTH * OUTS + 32)

            pre()
            barrier_lead(pool)
            with pool.Fori(0, DEPTH) as l:
                for stage in (stage_a, stage_b, stage_gla, stage_ssd):
                    stage(l)
                    barrier_lead(pool)
                with pool.Fori(0, DB) as b:
                    seq_step(l, b)
                    barrier_lead(pool)
                barrier_lead(pool)
                with pool.Fori(0, NE // 4):
                    barrier_lead(pool)
                barrier_lead(pool)
            final()
            barrier_lead(pool)


def kernel(x_prompt, x_sample, cache_win_k, cache_win_v, cache_sb_k, cache_sb_v, state_gla, state_ssm, state_conv,
           page_table, c_prompt, c_sample, w_ada, b_ada, g_norm1, g_norm2, w_in, w_gla_a2, b_gla_a, g_gla, b_sb,
           w_conv, b_conv, dt_bias, a_log, d_skip, g_ssm, w_out, w_router_grp, b_router_grp, w_router_exp,
           b_router_exp, w_exp_gate, w_exp_up, w_exp_down, g_final):
    import concourse.bacc as bacc
    from concourse.bass_utils import run_bass_kernel_spmd

    a = {k: np.asarray(v) for k, v in locals().items() if k not in ("bacc", "run_bass_kernel_spmd")}
    L = DEPTH
    cols = np.split(a["w_in"], np.cumsum([256, 256, 256, 128, 128, 256, 16, 256, 256, 256, 256, 256, 512])[:13].tolist(), axis=-1)
    aq, ak, av, bq, bk, bv, lr, gate, cq, ck, cv, z, xbc, dt = cols
    vec = np.concatenate([a["b_ada"], a["g_norm1"], a["g_norm2"], a["w_conv"].reshape(L, -1), a["b_conv"], a["g_ssm"],
                          a["b_gla_a"], a["g_gla"], a["g_gla"]], axis=-1).reshape(L, NVEC, 128)
    ins = {
        "x_rows": np.concatenate([a["x_prompt"].reshape(-1, DM), a["x_sample"].reshape(-1, DM)]),
        "c_rows": np.concatenate([a["c_prompt"], a["c_sample"]]),
        "win_k": a["cache_win_k"].reshape(L, DB, PAST, 256), "win_v": a["cache_win_v"].reshape(L, DB, PAST, 256),
        "sb_k": a["cache_sb_k"].reshape(L * N_POOL * 16, 2048), "sb_v": a["cache_sb_v"].reshape(L * N_POOL * 16, 2048),
        "st_gla": a["state_gla"], "st_ssm": a["state_ssm"], "st_conv": a["state_conv"], "pages": a["page_table"],
        "w_ada": a["w_ada"], "vecs": vec,
        "w_in": np.concatenate([aq, ak, av, bq, bk, bv, cq, ck, cv, gate, z, xbc], axis=-1),
        "w_tail": np.concatenate([lr, dt], axis=-1), "w_a2": a["w_gla_a2"],
        "bcs": np.concatenate([a["b_sb"], a["dt_bias"], a["a_log"], a["d_skip"], a["b_router_grp"], a["b_router_exp"]], axis=-1),
        "b_sb": a["b_sb"], "w_out": a["w_out"],
        "w_router": np.concatenate([a["w_router_grp"], a["w_router_exp"]], axis=-1),
        "w_gate": a["w_exp_gate"], "w_up": a["w_exp_up"], "w_down": a["w_exp_down"], "g_final": a["g_final"],
        "consts": np.concatenate(list(CONST.values()), axis=1),
    }
    outs = [("y_p", (SEQ, DM)), ("y_s", (NS, DM)), ("wk_p", (L, SEQ, 256)), ("wv_p", (L, SEQ, 256)), ("wk_s", (L, NS, 256)),
            ("wv_s", (L, NS, 256)), ("sk_p", (L, SEQ, 256)), ("sv_p", (L, SEQ, 256)), ("sk_s", (L, NS, 256)),
            ("sv_s", (L, NS, 256)), ("gla_p", (L, 1, NH, 32, 64)), ("gla_s", (L, DB, NH, 32, 64)),
            ("ssm_p", (L, 1, NH, 64, 64)), ("ssm_s", (L, DB, NH, 64, 64)), ("cv_p", (L, 1, 3, CONV_CH)), ("cv_s", (L, DB, 3, CONV_CH))]
    nc = bacc.Bacc("TRN2", target_bir_lowering=False, num_devices=1)
    args, arrays = [], {}
    for name, x in ins.items():
        arrays["in_" + name] = np.ascontiguousarray(x)
        args.append(nc.dram_tensor("in_" + name, x.shape, mybir.dt.from_np(x.dtype), kind="ExternalInput").ap())
    for name, shape in outs:
        args.append(nc.dram_tensor("out_" + name, shape, F32, kind="ExternalOutput").ap())
    trunk(nc, *args)
    r = run_bass_kernel_spmd(nc, [arrays], core_ids=[0]).results[0]
    g = {n: r["out_" + n] for n, _ in outs}
    heads = (NH, HD)
    return (g["y_p"].reshape(1, SEQ, DM), g["y_s"].reshape(DB, DS, DM),
            g["wk_p"].reshape(L, 1, SEQ, *heads), g["wv_p"].reshape(L, 1, SEQ, *heads),
            g["wk_s"].reshape(L, DB, DS, *heads), g["wv_s"].reshape(L, DB, DS, *heads),
            g["sk_p"].reshape(L, 1, SEQ // PAGE, PAGE, *heads), g["sv_p"].reshape(L, 1, SEQ // PAGE, PAGE, *heads),
            g["sk_s"].reshape(L, DB, DS, *heads), g["sv_s"].reshape(L, DB, DS, *heads),
            g["gla_p"], g["gla_s"], g["ssm_p"], g["ssm_s"], g["cv_p"], g["cv_s"])
```

```python
from contextlib import ExitStack

import numpy as np

import concourse.bass as bass
from concourse import mybir

F32, I32, U32 = mybir.dt.float32, mybir.dt.int32, mybir.dt.uint32
ALU, ACT, AX = mybir.AluOpType, mybir.ActivationFunctionType, mybir.AxisListType

DM, SEQ, DEPTH, DB, DS, PAST, PAGE = 1024, 256, 2, 8, 8, 2048, 128
KT8 = DM // 128
NS = DB * DS
T = SEQ + NS
SPANS = ((0, 128), (128, 128), (256, 64))
NH, HD = 4, 64
N_POOL = DB * (PAST // PAGE) * 5 // 4
NE, FE = 32, 512
CONV_CH = 512
EPS = 1e-6
BIG_F = float(2.0 ** 100)
NEG = -1e30
ROPE_DIM, THETA = 16, 500000.0
AQ, AK, AV, BQ, BK, BV, CQ, CK, CV, GATE, Z, XBC = 0, 2, 4, 6, 7, 8, 10, 12, 14, 16, 18, 20
PLACE = [20, 21, 22, 23, 16, 17, 18, 19] + list(range(16))
RING = 4
CHUNKS = 12 + 6 + 2 + 3 * NE
PER_SLOT = CHUNKS // RING
NG, NU = 4, 4
NA, NC = 320, PAST // 4
SLOTS, GE = 64, 4
GATE_AT, UP_AT, DOWN_AT = (0, 1, 4, 5), (2, 3, 6, 7), (8, 9, 10, 11)
NVEC = 88


def constants():
    out = {}
    p = np.arange(128)
    out["ident"] = np.eye(128)
    half = ROPE_DIM // 2
    freq = np.exp(-np.log(THETA) * np.arange(half, dtype=np.float32) * np.float32(2.0 / ROPE_DIM)).astype(np.float32)
    pos = np.concatenate([np.arange(SEQ), np.tile(PAST + np.arange(DS), DB)]).astype(np.float32)
    ang = (pos[None, :] * freq[:, None]).astype(np.float32)
    cos, sin = np.ones((128, T)), np.zeros((128, T))
    turn = np.zeros((128, 128))
    for base in (0, 64):
        for d in range(half):
            cos[base + d] = cos[base + half + d] = np.cos(ang[d].astype(np.float64))
            sin[base + d] = sin[base + half + d] = np.sin(ang[d].astype(np.float64))
            turn[base + half + d, base + d] = -1
            turn[base + d, base + half + d] = 1
    out["cos"], out["sin"], out["turn"] = cos, sin, turn

    def mult(dist):
        return sum(((dist >= 0) & (dist <= w) & (dist % d == 0)).astype(int) for w, d in ((128, 1), (512, 4), (2048, 16)))

    def cap(m):
        return np.where(m == 0, NEG, m * BIG_F)

    q = np.stack([p, p + 128], 1)[:, :, None]
    k = np.arange(SEQ)[None, None, :]
    out["cap_a"] = cap(mult(q - k)).reshape(128, -1)
    out["cap_c"] = cap((k < q).astype(int)).reshape(128, -1)
    qs = (PAST + p[0:32] % DS)[:, None]
    out["cap_sa"] = np.concatenate([cap(mult(qs - np.concatenate(
        [16 * np.arange(96) + 2 * g, 16 * np.arange(96) + 2 * g + 1, 1536 + 4 * p + g])[None, :])) for g in range(NG)])
    b = np.arange(DB)[None, :, None, None]
    bb, j = np.arange(DB)[None, None, :, None], np.arange(DS)[None, None, None, :]
    i, last = (p % DS)[:, None, None, None], (p // 32 == NG - 1)[:, None, None, None]
    for name, ok in (("cap_na", mult(i - j) * (b == bb) * last), ("cap_nc", (j < i) * (b == bb) * last)):
        out[name] = cap(ok).reshape(128, -1)
    out["in_group"] = p[:, None] // 32 == np.arange(NG)[None, :]
    out["of_head"] = p[:, None] // DS % NH == np.arange(NH)[None, :]
    out["same_row"] = p[:, None] % 32 == p[None, :] % 32
    out["later"] = -1 * ((p[:, None] % 32 == p[None, :] % 32) & (p[:, None] // 32 > p[None, :] // 32))
    out["fold"] = p[:, None] % 32 == np.arange(32)[None, :]
    s, t = p[:, None], p[None, :]
    for name, c in (("tri64", 64), ("tri8", 8)):
        out[name] = ((s // c == t // c) & (s <= t)).astype(int)
        out[name + "c"] = np.where(out[name] == 0, NEG, BIG_F)
    out["blk64"] = s // 64 == t // 64
    out["blk8"] = s // 8 == t // 8
    out["diag_gla"] = (s // 32) == (np.arange(256)[None, :] // 64)
    out["ones"] = np.ones((128, 128))
    out["seq_of"] = (p[:, None] // 8) == np.arange(8)[None, :]
    out["before"] = s < t
    out["iota"] = np.tile(np.arange(SLOTS), (128, 1))
    out["ones1"] = np.ones((128, 1))
    out["rev"] = np.tile(np.arange(8, 0, -1), (128, 1))
    reset = np.ones((128, T))
    reset[:, 0:SEQ:64] = 0
    reset[:, SEQ::8] = 0
    out["reset"] = reset
    out["sub"] = (p % 32)[:, None]
    return {n: np.ascontiguousarray(v, np.float32) for n, v in out.items()}


CONST = constants()
COFF, at = {}, 0
for _n, _v in CONST.items():
    COFF[_n] = (at, _v.shape[1])
    at += _v.shape[1]
NCONST = at


def trunk(nc, x_rows, c_rows, win_k, win_v, sb_k, sb_v, st_gla, st_ssm, st_conv, pages, w_ada, vecs, w_in,
          w_tail, w_a2, bcs, w_out, w_router, w_gate, w_up, w_down, g_final, consts,
          y_p, y_s, wk_p, wv_p, wk_s, wv_s, sk_p, sv_p, sk_s, sv_s, gla_p, gla_s, ssm_p, ssm_s, cv_p, cv_s):
    with ExitStack() as ctx:
        def sb(name, n, dt=F32):
            return ctx.enter_context(nc.sbuf_tensor(name, [128, n], dt))

        cst = sb("cst", NCONST)

        def K(name, parts=128):
            o, n = COFF[name]
            return cst[0:parts, o:o + n]

        ring = [sb(f"ring{i}", 4096) for i in range(RING)]
        xT_ = sb("xT", KT8 * T)
        mT_ = sb("mT", KT8 * T)
        modT_ = sb("modT", 48 * 9)
        scaleT_ = sb("scaleT", 8 * 9)
        cT_ = sb("cT", 8 * 32)
        vec = sb("vec", NVEC)
        vrow = sb("vrow", 128)
        bc = sb("bc", 52)
        gfin = sb("gfin", 8)
        wtail_ = sb("wtail", 8 * 20)
        wr_ = sb("wr", 8 * 36)
        wa2 = sb("wa2", 128)
        bsb = sb("bsb", 1)
        qzA_ = sb("qzA", 4 * T)
        qzC_ = sb("qzC", 4 * T)
        vA_ = sb("vA", 3 * 256)
        vC_ = sb("vC", 3 * 256)
        kS_ = sb("kS", 4 * NS)
        qA_, qC_ = sb("qA", 2 * 32), sb("qC", 2 * 32)
        pA_, pC_ = sb("pA", 4 * 128), sb("pC", 5 * 128)
        idxf = sb("idxf", NG * DB)
        idxi = sb("idxi", NG * DB, I32)
        idxu = sb("idxu", NG * DB, U32)
        rr = sb("rr", T)
        rv, rt = sb("rv", 2 * T), sb("rt", 2 * T)
        sm = sb("sm", 64)
        big = sb("big", 16896)
        PS = ctx.enter_context(nc.psum_tensor("PS", [128, 8, 512], F32))
        PSF = PS[:, :, :].rearrange("p b n -> p (b n)")

        def v3(t, off, a, b, parts=128):
            return t[0:parts, off:off + a * b].rearrange("p (a b) -> p a b", a=a)

        def v4(t, off, a, b, c, parts=128):
            return t[0:parts, off:off + a * b * c].rearrange("p (a b c) -> p a b c", a=a, b=b)

        def spread(ap, axis, n):
            u = ap.unsqueeze(axis)
            shape = list(u.shape)
            shape[axis] = n
            return u.to_broadcast(shape)

        xT, mT = v3(xT_, 0, KT8, T), v3(mT_, 0, KT8, T)
        modT = v3(modT_, 0, 48, 9)
        cT = v3(cT_, 0, KT8, 32)
        wtail, wr = v3(wtail_, 0, 8, 20), v3(wr_, 0, 8, 36)
        qzA, qzC = v3(qzA_, 0, 4, T), v3(qzC_, 0, 4, T)
        vA, vC = v3(vA_, 0, 3, 256), v3(vC_, 0, 3, 256)
        kS = v3(kS_, 0, 4, NS)
        ident, ones = K("ident"), K("ones")
        SCR = 10412
        PT = v3(big, 0, 20, T)
        lrT = big[0:16, 6400:6720]
        XP = v3(big, 6720, 4, 347)
        XPs = XP[:, :, 259:347].rearrange("p c (b k) -> p c b k", b=DB)
        kA, kC, vB = v3(big, 8108, 3, 256), v3(big, 8876, 3, 256), v3(big, 9644, 3, 256)

        def ring3(s, a):
            return v3(ring[s], 0, a, 4096 // a)

        cvo = rv[:, 0:512]
        idxb = sb("idxb", 2 * NG, U32)
        crowded = sb("crowded", 1, I32)
        L3 = lambda off, a, b: v3(big, off, a, b)
        class gla:
            cum = ec = pA_[:, 0:T]
            en, el = pC_[:, 0:T], pC_[:, T:2 * T]
            kg = big[:, 1280:1600]
            kdT = big[:, 1600:1920]
            qg = big[:, 2560:2880]
            la = rr[:, :]
            qgz = L3(3200, 4, T)
            kdt = L3(4480, 3, 128)
            kdm = L3(8108, 8, 128)
            att = L3(SCR, 3, 512)
            st0 = L3(11948, 8, 256)
            stp = L3(13996, 4, 256)
            raw = L3(16044, 8, 64)
            o = L3(15020, 2, T)
            sq = L3(15660, 2, T)
            last = sm[:, 32:44]

        class ssd:
            xc = L3(0, 4, T)
            tok = L3(1280, 3, 384)
            cz = L3(2432, 2, T)
            ce = L3(3072, 4, T)
            ex = L3(3072, 4, T)
            dab = v4(big, 3072, 3, 4, 128)
            ec = L3(8108, 4, T)
            dec = v4(big, 9388, 3, 4, 128)
            xdt = L3(10924, 3, 256)
            xw = L3(11692, 3, 256)
            bm = L3(12460, 8, 128)
            raw = L3(13484, 8, 128)
            st0 = L3(14508, 8, 128)
            stp = L3(15532, 4, 128)
            y = L3(3072, 2, T)
            sq = L3(3712, 2, T)
            outb = big[:, 9388:10540]
            v = L3(16560, 3, 4)
            tt = L3(16572, 3, 4)
            u = L3(16584, 3, 4)
            w1 = L3(16596, 3, 4)
            l = L3(16608, 3, 4)
            d = L3(16620, 3, 4)
            eq = L3(16632, 3, 4)
            dt = L3(16644, 3, 4)
            da = L3(16656, 3, 4)
            cum = L3(16668, 3, 4)
            w = L3(16680, 3, 4)
            alog = big[:, 16692:16696]
            last = L3(16696, 12, 2)
            dsk = big[:, 16720:16722]

        ssd.conv = [rt[:, 0:T], rt[:, T:2 * T], rv[:, 0:T], rv[:, T:2 * T]]
        ssd.fin = lambda j: ssd.stp[:, 3, :] if j == 0 else ssd.st0[:, j - 1, :]
        class prompt:
            sa, pta = L3(SCR, 4, 512), v4(big, SCR + 2048, 2, 4, 256)
            sc, tc, ptc = v3(ring[2], 0, 4, 512), v3(ring[2], 2048, 4, 512), v4(ring[3], 0, 2, 4, 256)
            sa8, tc8 = L3(SCR, 8, 256), v3(ring[2], 2048, 8, 256)

        class seq:
            ka, kan = v3(ring[0], 0, 8, 256), v3(ring[0], 2048, 4, 256)
            va, van = v3(ring[1], 0, 8, 256), v3(ring[1], 2048, 4, 256)
            kc, vc = v4(big, 0, NG, NU, 256), v4(big, 4096, NG, NU, 256)
            kcT = L3(8192, 2, PAST)
            kaT = L3(12288, 2, NG * NA)
            s = big[:, 14848:14848 + NC + NS]
            t = big[:, 15424:15424 + NC + NS]
            sa = big[:, 16000:16000 + NA + NS]
            o = big[:, 16384:16640]
            gmax = big[:, 16640:16640 + NG]
            qA, qC = v3(qA_, 0, 2, 32), v3(qC_, 0, 2, 32)
            pA, pC = v3(pA_, 0, 4, 128), v3(pC_, 0, 5, 128)

        class moe:
            y = L3(0, 8, T)
            a = L3(8960, 4 * GE, T)
            gt = L3(3840, 3, 32)
            gt4 = v4(big, 3840, 3, 4, 8)
            gT = big[:, 3936:4256]
            gm = big[:, 4256:4576]
            gb = big[:, 4576:4896]
            e = L3(4896, 2, T)
            L = L3(5536, 3, 36)
            tmp = L3(5644, 3, 8)
            km = big[:, 5668:5671]
            gmax = big[:, 5671:5674]
            ghot = L3(5674, 3, 4)
            gx = L3(5686, 3, 4)
            e8 = L3(5698, 3, 8)
            m1 = big[:, 5722:5725]
            m2 = big[:, 5725:5728]
            h1 = L3(5728, 3, 8)
            h2 = L3(5752, 3, 8)
            dx = big[:, 5776:5779]
            gp = big[:, 5779:5782]
            htok = L3(5888, 3, 1024)
            pick = L3(8960, 3, GE * SLOTS)
            wpick = L3(9728, 3, GE * SLOTS)
            hsel = L3(10496, 8, GE * SLOTS)
            spread = L3(12544, 2, T)
            outs = L3(13184, 2, 1024)
            hid = L3(2560, 2, FE)
            silu = L3(15232, 2, FE)
            hidT = v4(big, 4576, 2, 4, 128)
            rank = L3(16256, 3, 32)
            sel = L3(16352, 3, 32)
            selc = L3(16448, 3, 32)


        ring_full = [ctx.enter_context(nc.semaphore(f"ring_full{i}")) for i in range(RING)]
        ring_free = [ctx.enter_context(nc.semaphore(f"ring_free{i}")) for i in range(RING)]
        a_k_full = ctx.enter_context(nc.semaphore("a_k_full"))
        a_v_full = ctx.enter_context(nc.semaphore("a_v_full"))
        loads = ctx.enter_context(nc.semaphore("loads"))
        outputs = ctx.enter_context(nc.semaphore("outputs"))
        gathered_k = ctx.enter_context(nc.semaphore("gathered_k"))
        gathered_v = ctx.enter_context(nc.semaphore("gathered_v"))
        a_k_free = ctx.enter_context(nc.semaphore("a_k_free"))
        a_v_free = ctx.enter_context(nc.semaphore("a_v_free"))
        arrived = ctx.enter_context(nc.semaphore("arrived"))
        cleared = ctx.enter_context(nc.semaphore("cleared"))
        seen = ctx.enter_context(nc.semaphore("seen"))
        go = ctx.enter_context(nc.semaphore("go"))

        LOADS_PRE, LOADS_A, LOADS_B = 16 * 9, 16 * 6, 16
        LOADS = LOADS_A + LOADS_B + 32
        OUTS_B, OUTS_G = 160, 128
        OUTS = OUTS_B + OUTS_G + 64
        sem = {}
        for n in ("dve_step act_step pool_step variance rstd rows_in rows_T c_T  vec_T mod_mm mod_rows_mm mod_rows_kept mod_done sq rms_mm "
                  "h_done proj_mm proj_ev tail_mm convT_mm xp_done pre_T turn_mm rope_done qz_done tok_mm tok_ev "
                  "tail27_mm tail27_ev a_scores_mm a_max a_exp a_probs a_probs_turned a_probs_copied a_out_mm "
                  "a_out_copied c_logits_mm c_logits c_abs c_log c_exponents c_weights c_weights_turned "
                  "c_weights_copied c_out_mm lr_mm gla_operands gla_scores_mm gla_scores_masked gla_kv_mm gla_states "
                  "gla_out_mm mixer_squares mixer_norm_mm conv_silu xb_turned ssm_in_turned log_decays cum_mm cb_mm "
                  "decays_spread cum_rows_mm cb_sample_mm ssd_operands bx_mm ssm_states ssd_out_mm ssm_final ssm_turned "
                  "a_keys_turned a_keys_copied_dve a_keys_copied_act a_queries c_keys_copied_dve c_keys_copied_act "
                  "c_keys_turned c_queries router_mm gates_done gates_turned gate_row down_added gate_mm hidden up_mm "
                  "gate_copied down_mm rows_turned gate_logits gate_abs gate_log gla_cum tails_kept conv_done "
                  "dt_exp dt_plus1 dt_log ssm_in_copied decay_left decay_left_exp cum_exps decay_args "
                  "decay_exps ssm_out_copied c_out_copied group_args group_exps pair_args pair_exps gate_act "
                  "rows_copied gla_final_states ranks_mm rows_kept spread_copied slot_out_copied picks gather_mm "
                  "weighted_picks spread_turned gathered slot_sum_mm selected pair_mm hidden_turned hidden_kept").split():
            sem[n] = ctx.enter_context(nc.semaphore(n))
        for n, past in (("a_group_max", "gate_log"), ("a_max_mm", "gla_cum"), ("a_sums", "gla_scores_mm"),
                        ("a_sums_mm", "gla_kv_mm"), ("a_rows_mm", "gla_out_mm"), ("a_rows_scaled", "gla_states"),
                        ("c_sums", "ssm_in_turned"), ("c_later_mm", "ssd_out_mm"), ("c_rows_mm", "cum_mm"),
                        ("c_rows_copied", "cb_mm"), ("first_indices", "vec_T")):
            sem[n] = sem[past]

        own = {}

        def step(eng, ins):
            own[eng][1] += 1
            ins.then_inc(own[eng][0], 1)
            eng.wait_ge(own[eng][0], own[eng][1])

        def barrier(eng):
            eng.drain().then_inc(arrived, 1)
            eng.wait_ge(cleared, 1)
            eng.sem_inc(seen, 1)
            eng.wait_ge(go, 1)
            own[eng][1] = 0

        def barrier_lead(pool):
            pool.sem_inc(arrived, 1)
            pool.wait_ge(arrived, 4)
            nums = sorted({s.num for s in sem.values()})
            assert nums[-1] - nums[0] == len(nums) - 1
            pool.sem_clear(range(nums[0], nums[-1] + 1))
            pool.sem_clear(arrived)
            pool.sem_clear(go)
            pool.sem_inc(cleared, 1)
            pool.wait_ge(seen, 3)
            pool.sem_clear(seen)
            pool.sem_clear(cleared)
            pool.sem_inc(go, 1)
            own[pool][1] = 0

        STAGES_BEFORE, STAGES_AFTER = 0, 0
        block = ctx.enter_context(nc.Block())

        @block.sync
        def _(sp):
            def load(l, src, slot, idx):
                sp.wait_ge(ring_free[slot], l * PER_SLOT + idx + 1)
                a = src.shape[1]
                sp.dma_start(ring3(slot, a), src).then_inc(ring_full[slot], 16)

            sp.wait_ge(loads, LOADS_PRE)
            with sp.Fori(0, DEPTH) as l:
                with sp.Fori(0, 3) as it:
                    for s in range(4):
                        src = w_ada[l, :, bass.ds(it * 2048 + s * 512, 512)]
                        load(l, src.rearrange("(k p) n -> p k n", p=128), s, it)
                for j in range(6):
                    load(l, w_in[l, :, j * 512:(j + 1) * 512].rearrange("(k p) n -> p k n", p=128), j % 4, 3 + j // 4)
                with sp.Fori(0, DB) as b:
                    Q = seq
                    sp.wait_ge(a_k_free, l * (DB + 1) + b + 1)
                    for cache, far, near, full in ((win_k, Q.ka, Q.kan, a_k_full), (win_v, Q.va, Q.van, a_v_full)):
                        if cache is win_v:
                            sp.wait_ge(a_v_free, l * (DB + 1) + b + 1)
                        sp.dma_start(far[0:96], cache[l, b, 0:1536].rearrange("(a r) c -> a r c", r=16)[:, 0:8, :]).then_inc(full, 16)
                        sp.dma_start(near, cache[l, b, 1536:2048].rearrange("(p r) c -> p r c", r=4)).then_inc(full, 16)
                for j in range(2):
                    if j == 1:
                        sp.wait_ge(a_k_free, l * (DB + 1) + DB + 1)
                        sp.wait_ge(a_v_free, l * (DB + 1) + DB + 1)
                    load(l, w_out[l, :, j * 512:(j + 1) * 512].rearrange("(k p) n -> p k n", p=128), 2 + j, 4)
                with sp.Fori(0, NE // 4) as it:
                    for q in range(3 * GE):
                        u, w = next((u, w) for u in range(GE) for w, at in ((w_gate, GATE_AT), (w_up, UP_AT), (w_down, DOWN_AT)) if at[u] == q)
                        load(l, w[l, it * GE + u].rearrange("(k p) n -> p k n", p=128), q % RING, it * 3 + 5 + q // RING)

        @block.tensor
        def _(pe):
            own[pe] = [None, 0]
            mm = nc.tensor.matmul

            def tr(out, in_):
                return nc.tensor.transpose(out, in_, ident[0:in_.shape[0], 0:in_.shape[0]])

            def full(l, slot, idx):
                pe.wait_ge(ring_full[slot], (l * PER_SLOT + idx + 1) * 16)

            def pre():
                pe.wait_ge(loads, LOADS_PRE)
                rows = v3(big, 0, 3, 1024)
                for k in range(KT8):
                    for t, (t0, n) in enumerate(SPANS):
                        i = tr(PS[:, k, t0:t0 + n], rows[0:n, t, k * 128:(k + 1) * 128])
                i.then_inc(sem["rows_T"], 1)
                pe.wait_ge(sem["rows_in"], 1)
                pe.wait_ge(sem["xp_done"], 1)
                for k in range(KT8):
                    i = tr(PS[:, 0, k * 9:(k + 1) * 9], big[0:9, 4096 + k * 128:4096 + (k + 1) * 128])
                i = tr(PS[:, 1, 0:8], big[0:8, 5120:5248])
                i.then_inc(sem["c_T"], 1)

            def rms():
                pe.wait_ge(sem["sq"], 1)
                sq = v3(big, SCR, KT8, T)
                for k in range(KT8):
                    i = mm(PS[:, 1, 0:T], ones, sq[:, k, :], start=(k == 0), stop=(k == KT8 - 1))
                i.then_inc(sem["rms_mm"], 1)

            def stage_a(l):
                pe.wait_ge(loads, l * LOADS + LOADS_PRE + LOADS_A)
                i = tr(PS[:, 1, 0:NVEC], vrow[0:NVEC, :])
                i.then_inc(sem["vec_T"], 1)
                crow = big[0:24, SCR + 2560:SCR + 3072]
                for c in range(4):
                    i = tr(PS[:, 2, 24 * c:24 * c + 24], crow[:, c * 128:(c + 1) * 128])
                i.then_inc(sem["convT_mm"], 1)
                with pe.Fori(0, 3) as it:
                    def rows(s):
                        full(l, s, it)
                        for k in range(KT8):
                            g = k % 4
                            i = mm(PS[32 * g:32 * g + 32, 3 + s, :], cT[:, k, :], ring3(s, 8)[:, k, :], start=(k < 4), stop=(k >= 4))
                        i.then_inc(sem["mod_rows_mm"], 1)
                        pe.wait_ge(sem["mod_rows_mm"], it * 4 + s + 1)
                        pe.sem_inc(ring_free[s], 1)

                    def turn(s):
                        pe.wait_ge(sem["mod_rows_kept"], it * 4 + s + 1)
                        for m in range(4):
                            mm(PS[:, 0, bass.ds(it * 144 + s * 36 + m * 9, 9)], v3(big, SCR, 4, 512)[:, s, m * 128:(m + 1) * 128],
                               K("fold")[:, 0:9], start=True, stop=True)

                    rows(0)
                    for s in range(1, 4):
                        rows(s)
                        turn(s - 1)
                    turn(3)
                pe.drain().then_inc(sem["mod_mm"], 1)
                pe.wait_ge(sem["vec_T"], 1)
                pe.wait_ge(sem["mod_done"], 1)
                rms()
                pe.wait_ge(sem["h_done"], 1)
                for k in range(KT8):
                    mm(PS[0:16, 4, 0:T], wtail[:, k, 0:16], mT[:, k, :], start=(k == 0), stop=(k == 7))
                for t, (t0, n) in enumerate(SPANS):
                    for k in range(KT8):
                        i = mm(PS[0:n, 5, 4 * t:4 * t + 4], mT[:, k, t0:t0 + n], wtail[:, k, 16:20], start=(k == 0), stop=(k == 7))
                i.then_inc(sem["tail_mm"], 1)
                pe.wait_ge(sem["xp_done"], 1)
                for c in range(24):
                    j, m = divmod(c, 4)
                    if m == 0:
                        full(l, j % 4, 3 + j // 4)
                    if c >= 4:
                        pe.wait_ge(sem["proj_ev"], c - 3)
                    for k in range(KT8):
                        i = mm(PS[:, c % 4, 0:T], ring3(j % 4, 8)[:, k, m * 128:(m + 1) * 128], mT[:, k, :],
                               start=(k == 0), stop=(k == 7))
                    i.then_inc(sem["proj_mm"], 1)
                    if m == 3:
                        pe.wait_ge(sem["proj_mm"], c + 1)
                        pe.sem_inc(ring_free[j % 4], 1)
                    if c == 0:
                        pe.wait_ge(sem["tails_kept"], 1)
                        mm(PS[:, 7, 0:T], wa2[0:16, :], lrT, start=True, stop=True).then_inc(sem["lr_mm"], 1)
                    if c == 15:
                        pe.wait_ge(sem["proj_ev"], 12)
                        pe.wait_ge(sem["gate_logits"], 1)
                        for q in range(4):
                            i = mm(PS[:, 4 + q, 0:T], K("turn"), PT[:, AQ + q, :], start=True, stop=True)
                        i.then_inc(sem["turn_mm"], 1)

            def tok(chunks, bank, n_free):
                for t, (t0, n) in enumerate(SPANS):
                    for c in range(2):
                        o = PS[0:n, bank + t // 2, (t % 2) * 256 + c * 128:(t % 2) * 256 + c * 128 + 128]
                        i = tr(o, PT[:, chunks + c, t0:t0 + n])
                return i

            def stage_b():
                tail = v3(big, SCR, 4, 27)
                pe.wait_ge(sem["pre_T"], 1)
                for c in range(4):
                    i = tr(PS[0:27, 4, c * 128:(c + 1) * 128], tail[:, c, :])
                i.then_inc(sem["tail27_mm"], 1)
                tok(AK, 0, 0).then_inc(sem["tok_mm"], 1)
                tok(AV, 2, 0).then_inc(sem["tok_mm"], 1)
                tok(BV, 6, 0).then_inc(sem["tok_mm"], 1)
                pe.wait_ge(sem["tail27_ev"], 1)
                tok(CK, 4, 0).then_inc(sem["tok_mm"], 1)
                pe.wait_ge(sem["tok_ev"], 1)
                tok(CV, 0, 0).then_inc(sem["tok_mm"], 1)
                pe.wait_ge(sem["tok_ev"], 5)
                P = prompt

                def scores(qz, kc, bank, name):
                    for h in range(4):
                        for qb in range(2):
                            i = mm(PS[:, bank + h, qb * 256:qb * 256 + 256], qz[:, h, qb * 128:qb * 128 + 128],
                                   PT[:, kc + h // 2, 0:256], start=True, stop=True)
                    i.then_inc(sem[name], 1)

                def turn(s, name):
                    for kb in range(2):
                        for h in range(4):
                            for qb in range(2):
                                i = tr(PSF[:, kb * 1024 + h * 256 + qb * 128:kb * 1024 + h * 256 + qb * 128 + 128],
                                       s[:, h, qb * 256 + kb * 128:qb * 256 + kb * 128 + 128])
                    i.then_inc(sem[name], 1)

                def weigh(pt, v, bank, name):
                    for h in range(4):
                        for kb in range(2):
                            i = mm(PS[64 * (h % 2):64 * (h % 2) + 64, bank + h // 2, 0:256], v[:, kb, h * 64:h * 64 + 64],
                                   pt[:, kb, h, :], start=(kb == 0), stop=(kb == 1))
                    i.then_inc(sem[name], 1)

                scores(qzA, AK, 0, "a_scores_mm")
                scores(qzC, CK, 4, "c_logits_mm")
                pe.wait_ge(sem["a_probs"], 1)
                turn(P.sa, "a_probs_turned")
                pe.wait_ge(sem["a_probs_copied"], 1)
                pe.wait_ge(sem["c_logits"], 1)
                weigh(P.pta, vA, 4, "a_out_mm")
                pe.wait_ge(sem["c_weights"], 1)
                turn(P.sc, "c_weights_turned")
                pe.wait_ge(sem["c_weights_copied"], 1)
                weigh(P.ptc, vC, 6, "c_out_mm")

            def stage_gla():
                G = gla
                pe.wait_ge(sem["gla_operands"], 1)
                for t, (t0, n) in enumerate(SPANS):
                    mm(PS[0:n, t, 0:4 * n].rearrange("p (h t) -> p h t", h=4), G.kg[:, t0:t0 + n], G.qgz[:, :, t0:t0 + n], start=True, stop=True)
                for t, (t0, n) in enumerate(SPANS):
                    i = tr(PS[0:n, 3, t * 128:(t + 1) * 128], G.kdT[:, t0:t0 + n])
                i.then_inc(sem["gla_scores_mm"], 1)
                pe.wait_ge(sem["gla_scores_masked"], 1)
                for c in range(4):
                    r = 64 * (c % 2)
                    mm(PS[:, 4 + c % 2, (c // 2) * 256:(c // 2) * 256 + 256], G.kdt[r:r + 64, c // 2, :], vB[r:r + 64, c // 2, :],
                       start=True, stop=True)
                for b in range(DB):
                    i = mm(PSF[:, b * 256:b * 256 + 256], G.kdm[0:64, b, :], vB[0:64, 2, :], start=True, stop=True)
                i.then_inc(sem["gla_kv_mm"], 1)
                pe.wait_ge(sem["gla_states"], 1)
                for c in range(2):
                    o = PS[:, 6 + c, 0:T]
                    cs = slice(c * 128, c * 128 + 128)
                    for b in range(DB):
                        mm(o[:, 256 + 8 * b:264 + 8 * b], G.st0[:, b, cs], G.qg[:, 256 + 8 * b:264 + 8 * b],
                           start=(b == 0), stop=False, skip_group_check=True)
                    for j in range(1, 4):
                        mm(o[:, 64 * j:64 * j + 64], G.stp[:, j - 1, cs], G.qg[:, 64 * j:64 * j + 64],
                           start=False, stop=False, skip_group_check=True)
                    for hh in range(2):
                        h = 2 * c + hh
                        for t, (t0, n) in enumerate(SPANS):
                            att = G.att[0:n, t, 0:4 * n].rearrange("p (h t) -> p h t", h=4)
                            i = mm(o[64 * hh:64 * hh + 64, t0:t0 + n], vB[0:n, t, h * 64:h * 64 + 64], att[:, h, :],
                                   start=False, stop=(t == 2), skip_group_check=True)
                i.then_inc(sem["gla_out_mm"], 1)
                pe.wait_ge(sem["mixer_squares"], 1)
                for c in range(2):
                    i = mm(PS[:, 6 + c, 0:T], K("blk64"), G.sq[:, c, :], start=True, stop=True)
                i.then_inc(sem["mixer_norm_mm"], 1)

            def stage_ssd(l):
                D = ssd
                pe.wait_ge(sem["conv_silu"], 1)
                for c in range(3):
                    for t, (t0, n) in enumerate(SPANS):
                        i = tr(PS[0:n, t, c * 128:(c + 1) * 128], D.xc[:, c, t0:t0 + n])
                i.then_inc(sem["xb_turned"], 1)
                pe.wait_ge(loads, l * LOADS + LOADS_PRE + LOADS)
                for b in range(DB):
                    i = tr(PSF[:, 1536 + b * 128:1536 + b * 128 + 128], D.raw[:, b, :])
                i.then_inc(sem["ssm_in_turned"], 1)
                for t, (t0, n) in enumerate(SPANS):
                    tri, blk = (K("tri8"), K("blk8")) if t == 2 else (K("tri64"), K("blk64"))
                    mm(PS[0:n, 5, 4 * t:4 * t + 4], tri[0:n, 0:n], D.da[0:n, t, :], start=True, stop=True)
                    i = mm(PS[0:n, 5, 16 + 4 * t:20 + 4 * t], blk[0:n, 0:n], D.da[0:n, t, :], start=True, stop=True)
                i.then_inc(sem["cum_mm"], 1)
                for t, (t0, n) in enumerate(SPANS):
                    i = mm(PS[0:n, 6, 0:2 * n].rearrange("p (g t) -> p g t", g=2) if t == 2 else PS[0:n, 6 + t, 0:256].rearrange("p (g t) -> p g t", g=2),
                           D.xc[:, 2, t0:t0 + n], D.cz[:, :, t0:t0 + n], start=True, stop=True) if t < 2 else i
                i.then_inc(sem["cb_mm"], 1)
                pe.wait_ge(sem["decays_spread"], 1)
                for h in range(4):
                    for t, (t0, n) in enumerate(SPANS):
                        tri = K("tri8") if t == 2 else K("tri64")
                        i = mm(PS[:, h, t0:t0 + n], D.dab[0:n, t, h, :], tri[0:n, 0:n], start=True, stop=True)
                i.then_inc(sem["cum_rows_mm"], 1)
                t0, n = SPANS[2]
                i = mm(PS[0:n, 4, 0:2 * n].rearrange("p (g t) -> p g t", g=2), D.xc[:, 2, t0:t0 + n], D.cz[:, :, t0:t0 + n], start=True, stop=True)
                i.then_inc(sem["cb_sample_mm"], 1)
                pe.wait_ge(sem["ssd_operands"], 1)
                for c in range(4):
                    r = 64 * (c % 2)
                    for g in range(2):
                        mm(PS[64 * g:64 * g + 64, c % 2, (c // 2) * 128:(c // 2) * 128 + 128],
                           D.tok[r:r + 64, c // 2, 256 + 64 * g:320 + 64 * g], D.xw[r:r + 64, c // 2, 128 * g:128 * g + 128],
                           start=True, stop=True)
                for b in range(DB):
                    for g in range(2):
                        i = mm(PSF[64 * g:64 * g + 64, 1024 + b * 128:1152 + b * 128], D.bm[0:64, b, 64 * g:64 * g + 64],
                               D.xw[0:64, 2, 128 * g:128 * g + 128], start=True, stop=True)
                i.then_inc(sem["bx_mm"], 1)
                pe.wait_ge(sem["ssm_states"], 1)
                for c in range(2):
                    for hh in range(2):
                        h = 2 * c + hh
                        o = PS[64 * hh:64 * hh + 64, 6 + c, 0:T]
                        for b in range(DB):
                            mm(o[:, 256 + 8 * b:264 + 8 * b], D.st0[:, b, 64 * hh:64 * hh + 64], D.ce[:, h, 256 + 8 * b:264 + 8 * b],
                               start=(b == 0), stop=False, skip_group_check=True)
                        for j in range(1, 4):
                            mm(o[:, 64 * j:64 * j + 64], D.stp[:, j - 1, 64 * hh:64 * hh + 64], D.ce[:, h, 64 * j:64 * j + 64],
                               start=False, stop=False, skip_group_check=True)
                        for t, (t0, n) in enumerate(SPANS):
                            i = mm(o[:, t0:t0 + n], D.xdt[0:n, t, 64 * h:64 * h + 64], D.dec[0:n, t, h, 0:n],
                                   start=False, stop=(t == 2), skip_group_check=True)
                i.then_inc(sem["ssd_out_mm"], 1)
                pe.wait_ge(sem["ssm_final"], 1)
                for j in range(9):
                    i = tr(PSF[:, j * 128:(j + 1) * 128], D.fin(j))
                i.then_inc(sem["ssm_turned"], 1)
                pe.wait_ge(sem["mixer_squares"], 1)
                for c in range(2):
                    i = mm(PS[:, 3, 0:T], ones, D.sq[:, c, :], start=(c == 0), stop=(c == 1))
                i.then_inc(sem["mixer_norm_mm"], 1)

            def seq_step(l, b):
                Q = seq
                pe.wait_ge(a_k_full, (l * DB + b + 1) * 32)
                for c in range(2):
                    cols = slice(c * 128, (c + 1) * 128)
                    for g in range(NG):
                        for u in range(2):
                            tr(PS[:, 4 * c + g, u * 96:u * 96 + 96], Q.ka[0:96, 2 * g + u, cols])
                        tr(PS[:, 4 * c + g, 192:NA], Q.kan[:, g, cols]).then_inc(sem["a_keys_turned"], 1)
                pe.wait_ge(sem["a_keys_copied_dve"], 2)
                pe.wait_ge(sem["a_keys_copied_act"], 2)
                pe.sem_inc(a_k_free, 1)
                pe.wait_ge(sem["a_queries"], 1)
                for c in range(2):
                    for g in range(NG):
                        mm(PS[32 * g:32 * g + 32, 0, 0:NA], Q.qA[:, c, :], Q.kaT[:, c, g * NA:(g + 1) * NA], start=(c == 0), stop=(c == 1))
                for c in range(2):
                    for g in range(NG):
                        i = mm(PS[32 * g:32 * g + 32, 0, NA:NA + NS], Q.qA[:, c, :], kS[:, c, :], start=(c == 0), stop=(c == 1))
                i.then_inc(sem["a_scores_mm"], 1)
                pe.wait_ge(gathered_k, (l * DB + b + 1) * 16 * NG)
                for n in range(2 * NG):
                    c, g = divmod(n, NG)
                    if n >= 5:
                        pe.wait_ge(sem["c_keys_copied_dve" if (n - 5) % 2 else "c_keys_copied_act"], (n - 5) // 2 + 1)
                    if n == 5:
                        pe.wait_ge(sem["a_group_max"], 1)
                        mm(PS[:, 0, 384:384 + NG], K("same_row"), Q.gmax, start=True, stop=True).then_inc(sem["a_max_mm"], 1)
                    for j in range(NU):
                        i = tr(PS[:, 1 + n % 5, j * 128:(j + 1) * 128], Q.kc[:, g, j, c * 128:(c + 1) * 128])
                    i.then_inc(sem["c_keys_turned"], 1)
                pe.wait_ge(sem["a_probs"], 1)
                for u in range(2):
                    tr(PS[0:96, 6, u * 128:(u + 1) * 128], Q.sa[:, u * 96:(u + 1) * 96])
                tr(PS[:, 6, 256:384], Q.sa[:, 192:NA])
                tr(PS[0:NS, 6, 384:512], Q.sa[:, NA:NA + NS]).then_inc(sem["a_probs_turned"], 1)
                pe.wait_ge(sem["c_keys_copied_act"], NG)
                pe.wait_ge(sem["c_keys_copied_dve"], NG)
                pe.wait_ge(sem["c_queries"], 1)
                for c in range(2):
                    for g in range(NG):
                        mm(PS[32 * g:32 * g + 32, 1, 0:NC], Q.qC[:, c, :], Q.kcT[:, c, g * NC:(g + 1) * NC], start=(c == 0), stop=(c == 1))
                for c in range(2):
                    for g in range(NG):
                        i = mm(PS[32 * g:32 * g + 32, 2, 0:NS], Q.qC[:, c, :], kS[:, 2 + c, :], start=(c == 0), stop=(c == 1))
                i.then_inc(sem["c_logits_mm"], 1)
                pe.wait_ge(sem["a_sums"], 1)
                mm(PS[:, 0, 388:389], K("same_row"), sm[:, 25:26], start=True, stop=True).then_inc(sem["a_sums_mm"], 1)
                pe.wait_ge(a_v_full, (l * DB + b + 1) * 32)
                pe.wait_ge(sem["a_probs_copied"], 1)
                for u in range(3):
                    for g in range(NG):
                        n, v = (96, Q.va[0:96, 2 * g + u, :]) if u < 2 else (128, Q.van[:, g, :])
                        i = mm(PS[32 * g:32 * g + 32, 7, 0:256], Q.pA[0:n, u, 32 * g:32 * g + 32], v,
                               start=(u == 0), stop=(u == 2 and g < NG - 1))
                i = mm(PS[96:128, 7, 0:256], Q.pA[0:NS, 3, 96:128], vA[0:NS, 2, :], start=False, stop=True)
                i.then_inc(sem["a_rows_mm"], 1)
                pe.wait_ge(sem["c_sums"], 1)
                mm(PS[:, 2, 64:65], K("later"), Q.t[:, 0:1], start=True, stop=True).then_inc(sem["c_later_mm"], 1)
                pe.wait_ge(sem["a_rows_scaled"], 1)
                for c in range(2):
                    i = mm(PS[:, 7, 256 + c * 32:288 + c * 32], Q.o[:, c * 128:(c + 1) * 128], K("fold"), start=True, stop=True)
                i.then_inc(sem["a_out_mm"], 1)
                pe.sem_inc(a_v_free, 1)
                pe.wait_ge(sem["c_weights"], 1)
                for j in range(NU):
                    tr(PS[:, 3, j * 128:(j + 1) * 128], Q.s[:, j:NC:NU])
                tr(PS[0:NS, 4, 0:128], Q.s[:, NC:NC + NS]).then_inc(sem["c_weights_turned"], 1)
                pe.wait_ge(sem["c_weights_copied"], 1)
                pe.wait_ge(gathered_v, (l * DB + b + 1) * 16 * NG)
                for j in range(NU):
                    for g in range(NG):
                        mm(PS[32 * g:32 * g + 32, 5, 0:256], Q.pC[:, j, 32 * g:32 * g + 32], Q.vc[:, g, j, :],
                           start=(j == 0), stop=(j == NU - 1 and g < NG - 1))
                i = mm(PS[96:128, 5, 0:256], Q.pC[0:NS, 4, 96:128], vC[0:NS, 2, :], start=False, stop=True)
                i.then_inc(sem["c_rows_mm"], 1)
                pe.wait_ge(sem["c_rows_copied"], 1)
                for c in range(2):
                    i = mm(PS[:, 5, 256 + c * 32:288 + c * 32], Q.o[:, c * 128:(c + 1) * 128], K("fold"), start=True, stop=True)
                i.then_inc(sem["c_out_mm"], 1)

            def stage_out(l):
                for c in range(8):
                    j, m = divmod(c, 4)
                    if m == 0:
                        full(l, 2 + j, 4)
                    if c >= 4:
                        pe.wait_ge(sem["proj_ev"], c - 3)
                    for k in range(KT8):
                        i = mm(PS[:, 4 + c % 4, 0:T], ring3(2 + j, 8)[:, k, m * 128:(m + 1) * 128], mT[:, k, :], start=(k == 0), stop=(k == 7))
                    i.then_inc(sem["proj_mm"], 1)
                    if m == 3:
                        pe.wait_ge(sem["proj_mm"], c + 1)
                        pe.sem_inc(ring_free[2 + j], 1)
                rms()
                pe.wait_ge(sem["h_done"], 1)
                for t, (t0, n) in enumerate(SPANS):
                    for k in range(KT8):
                        i = mm(PS[0:n, 2, t * 36:(t + 1) * 36], mT[:, k, t0:t0 + n], wr[:, k, :], start=(k == 0), stop=(k == 7))
                i.then_inc(sem["router_mm"], 1)
                pe.wait_ge(sem["gates_done"], 1)
                for t, (t0, n) in enumerate(SPANS):
                    i = tr(PS[0:32, 3, t0:t0 + n], moe.gt[0:n, t, :])
                i.then_inc(sem["gates_turned"], 1)
                pe.wait_ge(sem["selected"], 1)
                for t, (t0, n) in enumerate(SPANS):
                    for t2 in range(t):
                        mm(PS[0:n, 4, 32 * t:32 * t + 32], ones[:, 0:n], moe.sel[:, t2, :], start=(t2 == 0), stop=False)
                    mm(PS[0:n, 4, 32 * t:32 * t + 32], K("before")[0:n, 0:n], moe.sel[0:n, t, :], start=(t == 0), stop=True)
                for t, (t0, n) in enumerate(SPANS):
                    i = mm(PS[:, 4, 96:128], ones[0:n, :], moe.sel[0:n, t, :], start=(t == 0), stop=(t == 2))
                i.then_inc(sem["ranks_mm"], 1)
                for t, (t0, n) in enumerate(SPANS):
                    if t:
                        pe.wait_ge(sem["rows_kept"], t)
                    for k in range(KT8):
                        i = tr(PS[0:n, 5 + k // 4, (k % 4) * 128:(k % 4) * 128 + 128], mT[:, k, t0:t0 + n])
                    i.then_inc(sem["rows_turned"], 1)

            def gather(chunks):
                pe.wait_ge(sem["picks"], 1)
                for k in chunks:
                    for t, (t0, n) in enumerate(SPANS):
                        i = mm(PS[:, k // 2, (k % 2) * 256:(k % 2) * 256 + 256], moe.htok[0:n, t, k * 128:(k + 1) * 128],
                               moe.pick[0:n, t, :], start=(t == 0), stop=(t == 2))
                i.then_inc(sem["gather_mm"], 1)

            def slot_sums(ds):
                for d in ds:
                    if d >= 2:
                        pe.wait_ge(sem["down_added"], d - 1)
                    for pair in range(2):
                        i = mm(PS[:, 6 + d % 2, 0:T], moe.outs[:, pair, d * 128:(d + 1) * 128], moe.spread[:, pair, :],
                               start=(pair == 0), stop=(pair == 1))
                    i.then_inc(sem["slot_sum_mm"], 1)

            def group(l, it, prev, more):
                M = moe

                def pairwise(pair, at, out_bank, stationary, steps, halves):
                    for x in range(2):
                        q = at[2 * pair + x]
                        full(l, q % RING, it * 3 + 5 + q // RING)
                    for half in range(halves):
                        for k in range(steps):
                            for x in range(2):
                                w = ring3(at[2 * pair + x] % RING, steps)[:, k, half * 512:half * 512 + 512]
                                i = mm(PS[SLOTS * x:SLOTS * x + SLOTS, out_bank + half, :], stationary(k, x), w,
                                       start=(k == 0), stop=(k == steps - 1))
                    i.then_inc(sem["pair_mm"], 1)
                    return i

                def gate(pair):
                    pairwise(pair, GATE_AT, 2 * pair, lambda k, x: M.hsel[:, k, (2 * pair + x) * SLOTS:(2 * pair + x + 1) * SLOTS], 8, 1)

                def up(pair):
                    pairwise(pair, UP_AT, 2 * pair + 1, lambda k, x: M.hsel[:, k, (2 * pair + x) * SLOTS:(2 * pair + x + 1) * SLOTS], 8, 1)

                def turn(pair):
                    pe.wait_ge(sem["hidden"], pair + 1)
                    for f in range(4):
                        i = tr(PS[:, 6 + pair, f * 128:(f + 1) * 128], M.hid[:, pair, f * 128:(f + 1) * 128])
                    i.then_inc(sem["hidden_turned"], 1)

                def down(pair):
                    pe.wait_ge(sem["hidden_kept"], pair + 1)
                    if pair:
                        pe.wait_ge(sem["slot_out_copied"], 1)
                    pairwise(pair, DOWN_AT, 4, lambda k, x: M.hidT[:, pair, k, x * SLOTS:(x + 1) * SLOTS], 4, 2)

                def release(n, at, pair):
                    pe.wait_ge(sem["pair_mm"], n)
                    for x in range(2):
                        pe.sem_inc(ring_free[at[2 * pair + x] % RING], 1)

                gate(0)
                release(1, GATE_AT, 0)
                if prev:
                    slot_sums(range(0, 4))
                up(0)
                release(2, UP_AT, 0)
                if prev:
                    slot_sums(range(4, 8))
                pe.wait_ge(sem["weighted_picks"], 1)
                for pair in range(2):
                    for t, (t0, n) in enumerate(SPANS):
                        i = tr(PS[:, 4 + pair, t0:t0 + n], M.wpick[0:n, t, pair * 128:(pair + 1) * 128])
                i.then_inc(sem["spread_turned"], 1)
                gate(1)
                release(3, GATE_AT, 1)
                if prev:
                    pe.wait_ge(sem["down_added"], 8)
                turn(0)
                if more:
                    gather((0, 1))
                up(1)
                release(4, UP_AT, 1)
                if more:
                    gather((2, 3))
                pe.wait_ge(sem["spread_copied"], 1)
                down(0)
                release(5, DOWN_AT, 0)
                turn(1)
                if more:
                    gather((4, 5, 6, 7))
                down(1)
                release(6, DOWN_AT, 1)
                if not more:
                    pe.wait_ge(sem["slot_out_copied"], 2)

            def dense_group(l, it):
                M = moe
                for u in range(GE):
                    pe.wait_ge(sem["gate_row"], u + 1)
                    if u:
                        pe.wait_ge(sem["gate_copied"], u)
                    mm(PS[:, 4, 0:T], ones[0:32, :], M.gm[0:32, :], start=True, stop=True).then_inc(sem["gate_mm"], 1)
                    for q in (GATE_AT[u], UP_AT[u]):
                        full(l, q % RING, it * 3 + 5 + q // RING)
                    for f in range(4):
                        if u * 4 + f >= 2:
                            pe.wait_ge(sem["hidden"], u * 4 + f - 1)
                        for q, o in ((GATE_AT[u], 0), (UP_AT[u], 2)):
                            for k in range(KT8):
                                i = mm(PS[:, o + f % 2, 0:T], ring3(q % RING, 8)[:, k, f * 128:(f + 1) * 128], mT[:, k, :], start=(k == 0), stop=(k == 7))
                        i.then_inc(sem["up_mm"], 1)
                    pe.wait_ge(sem["up_mm"], 4 * u + 4)
                    for q in (GATE_AT[u], UP_AT[u]):
                        pe.sem_inc(ring_free[q % RING], 1)
                pe.wait_ge(sem["hidden"], 4 * GE)
                pe.wait_ge(sem["gate_copied"], GE)
                for u in range(GE):
                    q = DOWN_AT[u]
                    full(l, q % RING, it * 3 + 5 + q // RING)
                    for d in range(8):
                        if u * 8 + d >= 4:
                            pe.wait_ge(sem["down_added"], 8 * u + d - 3)
                        for f in range(4):
                            i = mm(PS[:, 4 + d % 4, 0:T], ring3(q % RING, 4)[:, f, d * 128:(d + 1) * 128], M.a[:, 4 * u + f, :], start=(f == 0), stop=(f == 3))
                        i.then_inc(sem["down_mm"], 1)
                    pe.wait_ge(sem["down_mm"], 8 * u + 8)
                    pe.sem_inc(ring_free[q % RING], 1)

            def final():
                rms()
                pe.wait_ge(sem["h_done"], 1)
                for t, (t0, n) in enumerate(SPANS):
                    for half in range(2):
                        for k in range(4):
                            i = tr(PS[0:n, 2 * t + half, k * 128:(k + 1) * 128], mT[:, 4 * half + k, t0:t0 + n])
                i.then_inc(sem["rows_turned"], 1)

            for s in range(RING):
                pe.sem_inc(ring_free[s], 1)
            pre()
            barrier(pe)
            with pe.Fori(0, DEPTH) as l:
                stage_a(l)
                barrier(pe)
                pe.sem_inc(a_k_free, 1)
                pe.sem_inc(a_v_free, 1)
                stage_b()
                barrier(pe)
                stage_gla()
                barrier(pe)
                stage_ssd(l)
                barrier(pe)
                with pe.Fori(0, DB) as b:
                    seq_step(l, b)
                    barrier(pe)
                stage_out(l)
                barrier(pe)
                many = pe.value_load(crowded[0:1, 0:1], min_val=0, max_val=1)
                with pe.If(many > 0):
                    barrier(pe)
                    with pe.Fori(0, NE // 4) as it:
                        dense_group(l, it)
                        barrier(pe)
                with pe.Else():
                    gather(range(KT8))
                    barrier(pe)
                    group(l, 0, False, True)
                    barrier(pe)
                    with pe.Fori(1, NE // GE - 1) as it:
                        group(l, it, True, True)
                        barrier(pe)
                    group(l, NE // GE - 1, True, False)
                    barrier(pe)
                    slot_sums(range(8))
                barrier(pe)
            final()
            barrier(pe)

        @block.scalar
        def _(act):
            own[act] = [sem["act_step"], 0]
            def f(out, in_, func, scale=1.0, bias=None):
                if bias is None:
                    return nc.scalar.activation(out, in_, func, scale=scale)
                return nc.scalar.activation(out, in_, func, scale=scale, bias=bias)

            def copy(out, in_):
                return nc.scalar.activation(out, in_, ACT.Copy)

            def squares():
                f(v3(big, SCR, KT8, T), xT, ACT.Square).then_inc(sem["sq"], 1)

            def rsqrt(out):
                v = rv[:, :].rearrange("p (a b) -> p a b", a=2) if len(out.shape) == 3 else rv[:, 0:T]
                act.wait_ge(sem["variance"], 1)
                step(act, f(out, v, ACT.Ln))
                f(out, out, ACT.Exp, scale=-0.5).then_inc(sem["rstd"], 1)

            def pre():
                act.wait_ge(loads, LOADS_PRE)
                f(big[0:9, 4096:5120], big[0:9, 4096:5120], ACT.Silu).then_inc(sem["rows_in"], 1)

            def stage_a():
                with act.Fori(0, 3) as it:
                    for s in range(4):
                        act.wait_ge(sem["mod_rows_mm"], it * 4 + s + 1)
                        copy(v3(big, SCR, 4, 512)[:, s, :], PS[:, 3 + s, :]).then_inc(sem["mod_rows_kept"], 1)
                act.wait_ge(sem["mod_mm"], 1)
                squares()
                rsqrt(rr[:, :])
                G, D = gla, ssd
                act.wait_ge(sem["tail_mm"], 1)
                copy(lrT, PS[0:16, 4, 0:T])
                copy(sm[:, 0:8], PS[:, 5, 0:8])
                copy(sm[0:64, 8:12], PS[0:64, 5, 8:12]).then_inc(sem["tails_kept"], 1)
                for c in range(24):
                    act.wait_ge(sem["proj_mm"], c + 1)
                    if c >= 4:
                        copy(PT[:, PLACE[c], :], PS[:, c % 4, 0:T]).then_inc(sem["proj_ev"], 1)
                    else:
                        if c == 0:
                            act.wait_ge(sem["xp_done"], 1)
                        step(act, copy(XP[:, c, 3:259], PS[:, c % 4, 0:256]))
                        copy(XPs[:, c, :, 3:11], PS[:, c % 4, 256:T].rearrange("p (b i) -> p b i", b=DB)).then_inc(sem["proj_ev"], 1)
                    if c == 0:
                        act.wait_ge(sem["lr_mm"], 1)
                        f(G.la, PS[:, 7, 0:T], ACT.Identity, bias=vec[:, 86:87]).then_inc(sem["gate_logits"], 1)
                    elif c == 1:
                        act.wait_ge(sem["gate_abs"], 1)
                        step(act, f(G.cum, G.cum, ACT.Exp, scale=-1.0))
                        f(G.cum, G.cum, ACT.Ln, bias=1.0).then_inc(sem["gate_log"], 1)
                    elif c == 3:
                        act.wait_ge(sem["gla_cum"], 1)
                        f(G.en, G.cum, ACT.Exp, scale=-1.0)
                        f(G.el, G.el, ACT.Exp)
                        f(G.ec, G.cum, ACT.Exp)
                        f(D.alog, bc[:, 8:12], ACT.Exp)
                        f(D.u, D.tt, ACT.Exp, scale=-1.0).then_inc(sem["dt_exp"], 1)
                    elif c == 5:
                        act.wait_ge(sem["dt_plus1"], 1)
                        f(D.l, D.w1, ACT.Ln).then_inc(sem["dt_log"], 1)
                    elif c == 7:
                        act.wait_ge(sem["proj_ev"], 8)
                        f(PT[:, GATE:GATE + 4, :], PT[:, GATE:GATE + 4, :], ACT.Silu)
                    elif c in (12, 15):
                        for k in ((0, 1) if c == 12 else (2, 3)):
                            act.wait_ge(sem["conv_done"], k + 1)
                            x = D.conv[k]
                            f(XP[:, k, 0:256], x[:, 0:SEQ], ACT.Silu)
                            f(XPs[:, k, :, 0:8], x[:, SEQ:T].rearrange("p (b i) -> p b i", b=DB), ACT.Silu)

            def stage_b():
                act.wait_ge(sem["tail27_mm"], 1)
                copy(cvo[0:27, :], PS[0:27, 4, :]).then_inc(sem["tail27_ev"], 1)
                for n, (buf, bank) in enumerate(((kA, 0), (vA, 2), (vB, 6), (kC, 4), (vC, 0))):
                    act.wait_ge(sem["tok_mm"], n + 1)
                    step(act, copy(buf[:, 0:2, :], PS[:, bank, :].rearrange("p (t c) -> p t c", t=2)))
                    copy(buf[0:64, 2, :], PS[0:64, bank + 1, 0:256]).then_inc(sem["tok_ev"], 1)
                P = prompt
                act.wait_ge(sem["c_logits_mm"], 1)
                for h in range(4):
                    i = f(P.sc[:, h, :], PS[:, 4 + h, :], ACT.Identity, scale=HD ** -0.5, bias=bc[:, h:h + 1])
                i.then_inc(sem["c_logits"], 1)
                act.wait_ge(sem["a_max"], 1)
                for j in range(8):
                    x = P.sa8[:, j, :]
                    i = f(x, x, ACT.Exp, scale=HD ** -0.5, bias=sm[:, 24 + j:25 + j])
                i.then_inc(sem["a_exp"], 1)
                act.wait_ge(sem["c_abs"], 1)
                step(act, f(P.tc, P.tc, ACT.Exp, scale=-1.0))
                f(P.tc, P.tc, ACT.Ln, bias=1.0).then_inc(sem["c_log"], 1)
                act.wait_ge(sem["a_probs_turned"], 1)
                copy(P.pta.rearrange("p a h q -> p (a h q)"), PSF[:, 0:2048]).then_inc(sem["a_probs_copied"], 1)
                act.wait_ge(sem["c_exponents"], 1)
                f(P.sc, P.sc, ACT.Exp).then_inc(sem["c_weights"], 1)
                act.wait_ge(sem["a_out_mm"], 1)
                copy(mT[:, 0:2, 0:256], PS[:, 4:6, 0:256])
                act.wait_ge(sem["c_weights_turned"], 1)
                copy(P.ptc.rearrange("p a h q -> p (a h q)"), PSF[:, 0:2048]).then_inc(sem["c_weights_copied"], 1)
                act.wait_ge(sem["c_out_mm"], 1)
                copy(mT[:, 4:6, 0:256], PS[:, 6:8, 0:256])

            def stage_gla():
                G = gla
                rsqrt(G.sq)

            def stage_ssd():
                D = ssd
                act.wait_ge(sem["ssm_in_turned"], 1)
                copy(D.st0, PSF[:, 1536:2560].rearrange("p (b n) -> p b n", b=DB)).then_inc(sem["ssm_in_copied"], 1)
                act.wait_ge(sem["decay_left"], 1)
                f(D.w, D.w, ACT.Exp).then_inc(sem["decay_left_exp"], 1)
                act.wait_ge(sem["cum_rows_mm"], 1)
                f(D.ec, PS[:, 0:4, 0:T], ACT.Exp).then_inc(sem["cum_exps"], 1)
                act.wait_ge(sem["decay_args"], 1)
                f(D.dec[:, 0:2], D.dec[:, 0:2], ACT.Exp)
                f(D.dec[0:64, 2, :, 0:64], D.dec[0:64, 2, :, 0:64], ACT.Exp).then_inc(sem["decay_exps"], 1)
                act.wait_ge(sem["ssm_turned"], 1)
                copy(D.outb, PSF[:, 0:1152]).then_inc(sem["ssm_out_copied"], 1)
                rsqrt(rr[:, :])

            def out(b, bank, c0, name):
                for hh in range(2):
                    src = PS[64 * hh:64 * hh + 64, bank, 256:352].rearrange("p (c n) -> p c n", c=2)[:, :, 8 * hh:8 * hh + 8]
                    copy(mT[64 * hh:64 * hh + 64, c0:c0 + 2, bass.ds(SEQ + b * 8, 8)], src).then_inc(sem[name], 1)
                    act.wait_ge(sem[name], hh + 1)

            def seq_step(b):
                Q = seq

                def copy_keys(n):
                    c, g = divmod(n, NG)
                    act.wait_ge(sem["c_keys_turned"], n + 1)
                    copy(Q.kcT[:, c, g * NC:(g + 1) * NC].rearrange("p (q e) -> p e q", e=NU),
                         PS[:, 1 + n % 5, :].rearrange("p (j q) -> p j q", j=NU)).then_inc(sem["c_keys_copied_act"], 1)

                for half in range(2):
                    act.wait_ge(sem["a_keys_turned"], 6 + 2 * half)
                    copy(v3(Q.kaT[:, 1, :], 2 * half * NA, 2, NA), PS[:, 4 + 2 * half:6 + 2 * half, 0:NA]).then_inc(sem["a_keys_copied_act"], 1)
                for n in (0, 2, 4):
                    copy_keys(n)
                act.wait_ge(sem["a_max"], 1)
                f(Q.sa, Q.sa, ACT.Exp, scale=HD ** -0.5, bias=sm[:, 24:25]).then_inc(sem["a_exp"], 1)
                copy_keys(6)
                act.wait_ge(sem["a_probs_turned"], 1)
                copy(Q.pA[0:96, 0:2, :], v3(PS[:, 6, :], 0, 2, 128, 96))
                copy(Q.pA[:, 2, :], PS[:, 6, 256:384])
                copy(Q.pA[0:NS, 3, :], PS[0:NS, 6, 384:512]).then_inc(sem["a_probs_copied"], 1)
                act.wait_ge(sem["c_logits_mm"], 1)
                f(Q.s[:, 0:NC], PS[:, 1, :], ACT.Identity, scale=HD ** -0.5, bias=bsb[:, 0:1])
                f(Q.s[:, NC:NC + NS], PS[:, 2, 0:NS], ACT.Identity, scale=HD ** -0.5, bias=bsb[:, 0:1]).then_inc(sem["c_logits"], 1)
                act.wait_ge(sem["c_abs"], 1)
                step(act, f(Q.t, Q.t, ACT.Exp, scale=-1.0))
                f(Q.t, Q.t, ACT.Ln, bias=1.0).then_inc(sem["c_log"], 1)
                act.wait_ge(sem["a_out_mm"], 1)
                out(b, 7, 0, "a_out_copied")
                act.wait_ge(sem["c_exponents"], 1)
                f(Q.s, Q.s, ACT.Exp, bias=sm[:, 27:28]).then_inc(sem["c_weights"], 1)
                act.wait_ge(sem["c_weights_turned"], 1)
                copy(Q.pC[:, 0:4, :], v3(PS[:, 3, :], 0, 4, 128))
                copy(Q.pC[0:NS, 4, :], PS[0:NS, 4, 0:128]).then_inc(sem["c_weights_copied"], 1)
                act.wait_ge(sem["c_out_mm"], 1)
                out(b, 5, 4, "c_out_copied")

            def stage_out():
                act.wait_ge(sem["proj_ev"], 8)
                squares()
                rsqrt(rr[:, :])
                act.wait_ge(sem["group_args"], 1)
                f(moe.gx, moe.gx, ACT.Exp).then_inc(sem["group_exps"], 1)
                act.wait_ge(sem["pair_args"], 1)
                f(moe.dx, moe.dx, ACT.Exp).then_inc(sem["pair_exps"], 1)
                for t, (t0, n) in enumerate(SPANS):
                    act.wait_ge(sem["rows_turned"], t + 1)
                    copy(moe.htok[0:n, t, :].rearrange("p (a n) -> p a n", a=2), PS[0:n, 5:7, :]).then_inc(sem["rows_kept"], 1)

            def keep_gathered(parts):
                act.wait_ge(sem["gather_mm"], parts)
                copy(moe.hsel[:, :, :].rearrange("p (a b) n -> p a (b n)", a=4), PS[:, 0:4, :]).then_inc(sem["gathered"], 1)

            def group(more):
                M = moe
                act.wait_ge(sem["pair_mm"], 1)
                f(M.silu[:, 0, :], PS[:, 0, :], ACT.Silu).then_inc(sem["gate_act"], 1)
                act.wait_ge(sem["spread_turned"], 1)
                copy(M.spread, PS[:, 4:6, 0:T]).then_inc(sem["spread_copied"], 1)
                act.wait_ge(sem["pair_mm"], 3)
                f(M.silu[:, 1, :], PS[:, 2, :], ACT.Silu).then_inc(sem["gate_act"], 1)
                act.wait_ge(sem["hidden_turned"], 1)
                copy(M.hidT[:, 0].rearrange("p a n -> p (a n)"), PS[:, 6, :]).then_inc(sem["hidden_kept"], 1)
                act.wait_ge(sem["pair_mm"], 5)
                copy(M.outs[:, 0, :], PSF[:, 2048:3072]).then_inc(sem["slot_out_copied"], 1)
                act.wait_ge(sem["hidden_turned"], 2)
                copy(M.hidT[:, 1].rearrange("p a n -> p (a n)"), PS[:, 7, :]).then_inc(sem["hidden_kept"], 1)
                if more:
                    keep_gathered(3)
                act.wait_ge(sem["pair_mm"], 6)
                copy(M.outs[:, 1, :], PSF[:, 2048:3072]).then_inc(sem["slot_out_copied"], 1)

            def dense_expert(u):
                M = moe
                act.wait_ge(sem["gate_mm"], u + 1)
                if u:
                    act.wait_ge(sem["hidden"], 4 * u)
                copy(M.gb, PS[:, 4, 0:T]).then_inc(sem["gate_copied"], 1)
                for ff in range(4):
                    act.wait_ge(sem["up_mm"], 4 * u + ff + 1)
                    if 4 * u + ff >= 2:
                        act.wait_ge(sem["hidden"], 4 * u + ff - 1)
                    f(M.e[:, ff % 2, :], PS[:, ff % 2, 0:T], ACT.Silu).then_inc(sem["gate_act"], 1)

            def final():
                squares()
                rsqrt(rr[:, :])
                act.wait_ge(sem["rows_turned"], 1)
                rows = v3(big, 0, 3, 1024)
                for t, (t0, n) in enumerate(SPANS):
                    i = copy(rows[0:n, t, :].rearrange("p (a n) -> p a n", a=2), PS[0:n, 2 * t:2 * t + 2, :])
                i.then_inc(sem["rows_copied"], 1)

            pre()
            barrier(act)
            with act.Fori(0, DEPTH):
                stage_a()
                barrier(act)
                stage_b()
                barrier(act)
                stage_gla()
                barrier(act)
                stage_ssd()
                barrier(act)
                with act.Fori(0, DB) as b:
                    seq_step(b)
                    barrier(act)
                stage_out()
                barrier(act)
                many = act.value_load(crowded[0:1, 0:1], min_val=0, max_val=1)
                with act.If(many > 0):
                    barrier(act)
                    with act.Fori(0, NE // 4):
                        for u in range(4):
                            dense_expert(u)
                        barrier(act)
                with act.Else():
                    keep_gathered(1)
                    barrier(act)
                    group(True)
                    barrier(act)
                    with act.Fori(1, NE // GE - 1):
                        group(True)
                        barrier(act)
                    group(False)
                    barrier(act)
                barrier(act)
            final()
            barrier(act)

        @block.vector
        def _(dve):
            own[dve] = [sem["dve_step"], 0]
            V = nc.vector

            def c(ins):
                step(dve, ins)

            def tt(out, a, b, op):
                return V.tensor_tensor(out, a, b, op)

            def ts(out, a, s1, s2, op0, op1=None):
                return V.tensor_scalar(out, a, s1, s2, op0, op1) if op1 is not None else V.tensor_scalar(out, a, s1, None, op0)

            def stt(out, a, s, b, op0, op1):
                return V.scalar_tensor_tensor(out=out, in0=a, scalar=s, in1=b, op0=op0, op1=op1)

            M_, A_, S_ = ALU.mult, ALU.add, ALU.subtract

            def pre():
                c(V.memset(qzA_[:, :], 0.0))
                c(V.memset(qzC_[:, :], 0.0))
                c(V.memset(cT_[:, :], 0.0))
                c(V.memset(qA_[:, :], 0.0))
                c(V.memset(qC_[:, :], 0.0))
                c(V.memset(sm[:, :], 0.0))
                dve.wait_ge(loads, LOADS_PRE)
                c(V.tensor_copy(idxf[:, :], idxi[:, :]))
                c(stt(idxf[:, :], idxf[:, :], float(PAGE // NU), K("sub").to_broadcast([128, NG * DB]), M_, A_))
                dve.wait_ge(sem["rows_T"], 1)
                V.tensor_copy(xT, PS[:, :, 0:T]).then_inc(sem["xp_done"], 1)
                dve.wait_ge(sem["c_T"], 1)
                V.tensor_copy(cT[:, :, 0:9], v3(PS[:, 0, :], 0, 8, 9))
                V.tensor_copy(gfin[:, :], PS[:, 1, 0:8])

            def rsqrt(out, in_, n):
                v, t = (x[:, :] if len(out.shape) == 3 else x[:, 0:T] for x in (rv, rt))
                if len(out.shape) == 3:
                    v, t = (x.rearrange("p (a b) -> p a b", a=2) for x in (v, t))
                ts(v, in_, 1.0 / n, EPS, M_, A_).then_inc(sem["variance"], 1)
                dve.wait_ge(sem["variance"], 1)
                dve.wait_ge(sem["rstd"], 1)
                c(tt(t, out, out, M_))
                c(tt(t, t, v, M_))
                c(ts(t, t, -0.5, 1.5, M_, A_))
                c(tt(out, out, t, M_))

            def norm(g, shift):
                sc = v3(scaleT_, 0, 8, 9)
                c(tt(sc, modT[:, shift + 8:shift + 16, :], spread(vec[:, g:g + 8], 2, 9), M_))
                dve.wait_ge(sem["rms_mm"], 1)
                rsqrt(rr[:, :], PS[:, 1, 0:T], DM)
                c(tt(mT, xT, spread(rr[:, :], 1, KT8), M_))
                hp = mT[:, :, 0:SEQ]
                c(tt(hp, hp, sc[:, :, 0:1].to_broadcast([128, 8, SEQ]), M_))
                c(tt(hp, hp, modT[:, shift:shift + 8, 0:1].to_broadcast([128, 8, SEQ]), A_))
                hs = mT[:, :, SEQ:T].rearrange("p k (b i) -> p k b i", b=DB)
                c(tt(hs, hs, spread(sc[:, :, 1:9], 3, 8), M_))
                tt(hs, hs, spread(modT[:, shift:shift + 8, 1:9], 3, 8), A_).then_inc(sem["h_done"], 1)
                dve.wait_ge(sem["h_done"], 1)

            def stage_a():
                c(V.memset(XP[:, :, 0:3], 0.0))
                c(V.tensor_copy(idxu[:, :], idxf[:, :]))
                c(ts(idxf[:, :], idxf[:, :], float(N_POOL * PAGE // NU), None, A_))
                dve.wait_ge(sem["vec_T"], 1)
                c(V.tensor_copy(vec[:, :], PS[:, 1, 0:NVEC]))
                dve.wait_ge(sem["convT_mm"], 1)
                V.tensor_copy(XPs[:, :, :, 0:3], PS[:, 2, 0:96].rearrange("p (c b k) -> p c b k", c=4, b=DB)).then_inc(sem["xp_done"], 1)
                dve.wait_ge(sem["xp_done"], 1)
                dve.wait_ge(sem["mod_mm"], 1)
                c(tt(modT, PS[:, 0, 0:432].rearrange("p (m s) -> p m s", s=9), spread(vec[:, 0:48], 2, 9), A_))
                c(ts(modT[:, 8:16, :], modT[:, 8:16, :], 1.0, None, A_))
                ts(modT[:, 32:40, :], modT[:, 32:40, :], 1.0, None, A_).then_inc(sem["mod_done"], 1)
                dve.wait_ge(sem["mod_done"], 1)
                norm(48, 0)
                G, D = gla, ssd
                dve.wait_ge(sem["tails_kept"], 1)
                c(tt(D.v, v3(sm, 0, 3, 4), spread(bc[:, 4:8], 1, 3), A_))
                c(stt(D.tt, D.v, -1.0, D.v, M_, ALU.max))
                dve.wait_ge(sem["gate_logits"], 1)
                stt(G.cum, G.la, -1.0, G.la, M_, ALU.max).then_inc(sem["gate_abs"], 1)
                dve.wait_ge(sem["gate_abs"], 1)
                dve.wait_ge(sem["gate_log"], 1)
                c(stt(G.la, G.la, 0.0, G.cum, ALU.min, S_))
                c(ts(G.la, G.la, 1.0 / 16.0, None, M_))
                c(V.tensor_tensor_scan(G.cum, K("reset"), G.la, 0.0, M_, A_))
                for a, b_, n, w in ((0, SEQ, 4, 64), (SEQ, T, 8, 8)):
                    x = G.cum[:, a:b_].rearrange("p (n w) -> p n w", w=w)
                    y = G.el[:, a:b_].rearrange("p (n w) -> p n w", w=w)
                    i = tt(y, x[:, :, w - 1:w].to_broadcast([128, n, w]), x, S_)
                    if a == 0:
                        c(i)
                    else:
                        i.then_inc(sem["gla_cum"], 1)
                        dve.wait_ge(sem["gla_cum"], 1)
                dve.wait_ge(sem["dt_exp"], 1)
                ts(D.w1, D.u, 1.0, None, A_).then_inc(sem["dt_plus1"], 1)
                dve.wait_ge(sem["dt_plus1"], 1)
                c(ts(D.d, D.w1, -1.0, None, A_))
                c(ts(D.eq, D.d, 0.0, None, ALU.is_equal))
                c(tt(D.d, D.d, D.eq, A_))
                c(V.reciprocal(D.d, D.d))
                c(tt(D.u, D.u, D.d, M_))
                dve.wait_ge(sem["dt_log"], 1)
                c(tt(D.l, D.l, D.eq, A_))
                c(tt(D.u, D.u, D.l, M_))
                c(stt(D.dt, D.v, 0.0, D.u, ALU.max, A_))
                stt(D.da, D.dt, -1.0, spread(D.alog, 1, 3), M_, M_).then_inc(sem["log_decays"], 1)
                dve.wait_ge(sem["log_decays"], 1)
                dve.wait_ge(sem["proj_ev"], 4)
                for k in range(4):
                    w = lambda j: vec[:, 64 + 4 * j + k:65 + 4 * j + k]
                    xp, xs = D.conv[k][:, 0:SEQ], D.conv[k][:, SEQ:T].rearrange("p (b i) -> p b i", b=DB)
                    c(ts(xp, XP[:, k, 0:256], w(0), vec[:, 80 + k:81 + k], M_, A_))
                    c(ts(xs, XPs[:, k, :, 0:8], w(0), vec[:, 80 + k:81 + k], M_, A_))
                    for j in range(1, 4):
                        c(stt(xp, XP[:, k, j:j + 256], w(j), xp, M_, A_))
                        i = stt(xs, XPs[:, k, :, j:j + 8], w(j), xs, M_, A_)
                        if j < 3:
                            c(i)
                        else:
                            i.then_inc(sem["conv_done"], 1)
                dve.wait_ge(sem["turn_mm"], 1)
                t1 = v3(big, SCR + 512, 4, T)
                c(tt(t1, PS[:, 4:8, 0:T], spread(K("sin"), 1, 4), M_))
                c(tt(PT[:, 0:4, :], PT[:, 0:4, :], spread(K("cos"), 1, 4), M_))
                tt(PT[:, 0:4, :], PT[:, 0:4, :], t1, A_).then_inc(sem["rope_done"], 1)
                dve.wait_ge(sem["rope_done"], 1)
                for qz, q in ((qzA, AQ), (qzC, CQ)):
                    if q == CQ:
                        dve.wait_ge(sem["proj_ev"], 22)
                    c(V.tensor_copy(qz[0:64, 0:4:2, :], PT[0:64, q:q + 2, :]))
                    c(V.tensor_copy(qz[64:128, 1:4:2, :], PT[64:128, q:q + 2, :]))
                c(V.tensor_copy(kS[:, 0:2, :], PT[:, AK:AK + 2, SEQ:T]))
                V.tensor_copy(kS[:, 2:4, :], PT[:, CK:CK + 2, SEQ:T])

            def stage_b():
                tail = v3(big, SCR, 4, 27)
                c(V.tensor_copy(tail[:, :, 0:3], XP[:, :, 256:259]))
                for k in range(4):
                    i = V.tensor_copy(tail[:, k, 3:27].rearrange("p (b k) -> p b k", b=DB), XPs[:, k, :, 8:11])
                    if k < 3:
                        c(i)
                    else:
                        i.then_inc(sem["pre_T"], 1)
                        dve.wait_ge(sem["pre_T"], 1)
                P = prompt
                dve.wait_ge(sem["a_scores_mm"], 1)
                dve.wait_ge(sem["tail27_mm"], 1)
                c(tt(P.sa, PS[:, 0:4, :], spread(K("cap_a"), 1, 4), ALU.min))
                c(V.tensor_reduce(sm[:, 24:32], P.sa8, AX.X, ALU.max))
                ts(sm[:, 24:32], sm[:, 24:32], -HD ** -0.5, None, M_).then_inc(sem["a_max"], 1)
                dve.wait_ge(sem["c_logits"], 1)
                c(tt(P.sc, P.sc, spread(K("cap_c"), 1, 4), ALU.min))
                stt(P.tc, P.sc, -1.0, P.sc, M_, ALU.max).then_inc(sem["c_abs"], 1)
                dve.wait_ge(sem["a_exp"], 1)
                c(stt(P.sa, spread(K("cap_a"), 1, 4), 1.0 / BIG_F, P.sa, M_, M_))
                c(V.tensor_reduce(sm[:, 24:32], P.sa8, AX.X, ALU.add))
                c(V.reciprocal(sm[:, 24:32], sm[:, 24:32]))
                tt(P.sa8, P.sa8, spread(sm[:, 24:32], 2, 256), M_).then_inc(sem["a_probs"], 1)
                dve.wait_ge(sem["c_log"], 1)
                c(stt(P.tc, P.sc, 0.0, P.tc, ALU.max, A_))
                for j in range(8):
                    x = P.tc8[:, j, ::-1]
                    i = V.tensor_tensor_scan(x, K("ones1").to_broadcast([128, 256]), x, 0.0, M_, A_)
                c(i)
                tt(P.sc, P.sc, P.tc, S_).then_inc(sem["c_exponents"], 1)

            def stage_gla(l):
                G = gla
                c(V.memset(G.qgz, 0.0))
                dve.wait_ge(loads, l * LOADS + LOADS_PRE + LOADS_A + LOADS_B)
                c(tt(G.st0.rearrange("p b (h v) -> p b h v", h=4), spread(G.raw, 2, 4),
                     spread(K("diag_gla").rearrange("p (h v) -> p h v", h=4), 1, DB), M_))
                c(stt(G.qg, PT[:, BQ, :], 32 ** -0.5, G.ec, M_, M_))
                for h in range(4):
                    c(V.tensor_copy(G.qgz[32 * h:32 * h + 32, h, :], G.qg[32 * h:32 * h + 32, :]))
                c(V.tensor_copy(G.last[:, 0:4], G.ec[:, 63:SEQ:64]))
                c(V.tensor_copy(G.last[:, 4:12], G.ec[:, SEQ + 7:T:8]))
                c(tt(G.kg, PT[:, BK, :], G.en, M_))
                tt(G.kdT, PT[:, BK, :], G.el, M_).then_inc(sem["gla_operands"], 1)
                dve.wait_ge(sem["gla_operands"], 1)
                dve.wait_ge(sem["gla_scores_mm"], 1)
                for t, (t0, n) in enumerate(SPANS):
                    tri = K("tri8") if t == 2 else K("tri64")
                    c(tt(G.att[0:n, t, 0:4 * n].rearrange("p (h t) -> p h t", h=4), PS[0:n, t, 0:4 * n].rearrange("p (h t) -> p h t", h=4),
                         spread(tri[0:n, 0:n], 1, 4), M_))
                c(V.tensor_copy(G.kdt[:, 0:2, :], PS[:, 3, 0:256].rearrange("p (t n) -> p t n", t=2)))
                c(V.tensor_copy(G.kdt[0:64, 2, :], PS[0:64, 3, 256:384]))
                tt(G.kdm[0:64], spread(G.kdt[0:64, 2, :], 1, DB), spread(K("seq_of")[0:64], 2, 128), M_).then_inc(sem["gla_scores_masked"], 1)
                dve.wait_ge(sem["gla_scores_masked"], 1)
                dve.wait_ge(sem["gla_kv_mm"], 1)
                d4 = spread(K("diag_gla"), 1, 2)
                for k in range(2):
                    x = PS[:, 4 + k, :].rearrange("p (j n) -> p j n", j=2)
                    c(tt(x, x, d4, M_))
                c(V.tensor_copy(G.stp[:, 0, :], PS[:, 4, 0:256]))
                for j in range(1, 4):
                    i = stt(G.stp[:, j, :], G.stp[:, j - 1, :], G.last[:, j:j + 1], PS[:, 4 + j % 2, (j // 2) * 256:(j // 2) * 256 + 256], M_, A_)
                    if j < 3:
                        c(i)
                    else:
                        i.then_inc(sem["gla_states"], 1)
                        dve.wait_ge(sem["gla_states"], 1)
                x = PSF[:, 0:2048].rearrange("p (b n) -> p b n", b=DB)
                c(tt(x, x, spread(K("diag_gla"), 1, DB), M_))
                dve.wait_ge(sem["gla_out_mm"], 1)
                c(V.tensor_copy(G.o, PS[:, 6:8, 0:T]))
                tt(G.sq, G.o, G.o, M_).then_inc(sem["mixer_squares"], 1)
                dve.wait_ge(sem["mixer_squares"], 1)
                c(tt(G.st0, G.st0, spread(G.last[:, 4:12], 2, 256), M_))
                tt(G.st0, G.st0, x, A_).then_inc(sem["gla_final_states"], 1)
                dve.wait_ge(sem["gla_final_states"], 1)
                dve.wait_ge(sem["mixer_norm_mm"], 1)
                rsqrt(G.sq, PS[:, 6:8, 0:T], HD)
                c(stt(G.o, G.o, vec[:, 87:88], G.sq, M_, M_))
                c(tt(mT[:, 2:4, :], G.o, PT[:, GATE:GATE + 2, :], M_))

            def stage_ssd():
                D = ssd
                c(tt(sm[:, 28:32], bc[:, 0:4], K("of_head"), M_))
                c(V.tensor_reduce(bsb[:, 0:1], sm[:, 28:32], AX.X, A_))
                c(V.memset(D.cz, 0.0))
                c(V.tensor_copy(D.xc[:, :, 0:SEQ], XP[:, :, 0:SEQ]))
                for k in range(4):
                    c(V.tensor_copy(D.xc[:, k, SEQ:T].rearrange("p (b i) -> p b i", b=DB), XPs[:, k, :, 0:8]))
                c(V.tensor_copy(D.cz[0:64, 0, :], D.xc[0:64, 3, :]))
                V.tensor_copy(D.cz[64:128, 1, :], D.xc[64:128, 3, :]).then_inc(sem["conv_silu"], 1)
                dve.wait_ge(sem["conv_silu"], 1)
                dve.wait_ge(sem["xb_turned"], 1)
                c(V.tensor_copy(D.tok[:, 0:2, :], PS[:, 0:2, 0:384]))
                c(V.tensor_copy(D.tok[0:64, 2, :], PS[0:64, 2, 0:384]))
                dve.wait_ge(sem["ssm_in_copied"], 1)
                V.tensor_copy(D.dab, spread(D.da, 3, 128)).then_inc(sem["decays_spread"], 1)
                dve.wait_ge(sem["decays_spread"], 1)
                c(V.memset(D.cum, 0.0))
                c(V.memset(D.w, 0.0))
                dve.wait_ge(sem["cum_mm"], 1)
                for n, t in ((128, slice(0, 2)), (64, slice(2, 3))):
                    cs = slice(4 * t.start, 4 * t.stop)
                    c(V.tensor_copy(D.cum[0:n, t, :].rearrange("p a b -> p (a b)"), PS[0:n, 5, cs]))
                    i = tt(D.w[0:n, t, :].rearrange("p a b -> p (a b)"), PS[0:n, 5, 16 + cs.start:16 + cs.stop], D.cum[0:n, t, :].rearrange("p a b -> p (a b)"), S_)
                    if n == 128:
                        c(i)
                    else:
                        i.then_inc(sem["decay_left"], 1)
                        dve.wait_ge(sem["decay_left"], 1)
                dve.wait_ge(sem["cum_exps"], 1)
                for t, (t0, n) in enumerate(SPANS):
                    d = D.dec[0:n, t, :, 0:n]
                    tri = K("tri8c") if t == 2 else K("tri64c")
                    c(tt(d, PS[0:n, 0:4, t0:t0 + n], spread(D.cum[0:n, t, :], 2, n), S_))
                    i = tt(d, d, spread(tri[0:n, 0:n], 1, 4), ALU.min)
                    if t < 2:
                        c(i)
                    else:
                        i.then_inc(sem["decay_args"], 1)
                        dve.wait_ge(sem["decay_args"], 1)
                dve.wait_ge(sem["decay_left_exp"], 1)
                for n, t in ((128, slice(0, 2)), (64, slice(2, 3))):
                    k = t.stop - t.start
                    x = D.tok[0:n, t, 0:256].rearrange("p t (h q) -> p t h q", h=4)
                    xd, xw = (v[0:n, t, :].rearrange("p t (h q) -> p t h q", h=4) for v in (D.xdt, D.xw))
                    c(tt(xd, x, spread(D.dt[0:n, t, :], 3, 64), M_))
                    c(tt(xw, xd, spread(D.w[0:n, t, :], 3, 64), M_))
                c(tt(D.bm[0:64], spread(D.tok[0:64, 2, 256:384], 1, DB), spread(K("seq_of")[0:64], 2, 128), M_))
                dve.wait_ge(sem["cum_exps"], 1)
                tt(D.ce.rearrange("p (g x) t -> p g x t", g=2), spread(D.cz, 2, 2), D.ec.rearrange("p (g x) t -> p g x t", g=2), M_).then_inc(sem["ssd_operands"], 1)
                dve.wait_ge(sem["ssd_operands"], 1)
                for g in range(2):
                    r = slice(64 * g, 64 * g + 64)
                    c(V.tensor_copy(D.last[r, 0:4, :].rearrange("p j h -> p h j"), D.ec[r, 2 * g:2 * g + 2, 63:SEQ:64]))
                    c(V.tensor_copy(D.last[r, 4:12, :].rearrange("p j h -> p h j"), D.ec[r, 2 * g:2 * g + 2, SEQ + 7:T:8]))
                dve.wait_ge(sem["decay_exps"], 1)
                dve.wait_ge(sem["cb_sample_mm"], 1)
                for t, (t0, n) in enumerate(SPANS):
                    bank = (6, 7, 4)[t]
                    d = D.dec[0:n, t, :, 0:n].rearrange("p (g x) t -> p g x t", g=2)
                    c(tt(d, d, spread(PS[0:n, bank, 0:2 * n].rearrange("p (g t) -> p g t", g=2), 2, 2), M_))
                dve.wait_ge(sem["bx_mm"], 1)
                hp = lambda x: x.rearrange("p (h q) -> p h q", h=2)
                c(V.tensor_copy(D.stp[:, 0, :], PS[:, 0, 0:128]))
                for j in range(1, 4):
                    c(tt(hp(D.stp[:, j, :]), hp(D.stp[:, j - 1, :]), spread(D.last[:, j, :], 2, 64), M_))
                    i = tt(D.stp[:, j, :], D.stp[:, j, :], PS[:, j % 2, (j // 2) * 128:(j // 2) * 128 + 128], A_)
                    if j < 3:
                        c(i)
                    else:
                        i.then_inc(sem["ssm_states"], 1)
                        dve.wait_ge(sem["ssm_states"], 1)
                dve.wait_ge(sem["ssd_out_mm"], 1)
                c(tt(D.st0.rearrange("p b (h q) -> p b h q", h=2), D.st0.rearrange("p b (h q) -> p b h q", h=2),
                     spread(D.last[:, 4:12, :], 3, 64), M_))
                tt(D.st0, D.st0, PSF[:, 1024:2048].rearrange("p (b n) -> p b n", b=DB), A_).then_inc(sem["ssm_final"], 1)
                dve.wait_ge(sem["ssm_final"], 1)
                c(V.tensor_copy(D.dsk[0:64, :], bc[0:64, 12:16:2]))
                c(V.tensor_copy(D.dsk[64:128, :], bc[64:128, 13:16:2]))
                for k in range(2):
                    c(stt(D.y[:, k, :], D.xc[:, k, :], D.dsk[:, k:k + 1], PS[:, 6 + k, 0:T], M_, A_))
                c(tt(D.y, D.y, PT[:, Z:Z + 2, :], M_))
                tt(D.sq, D.y, D.y, M_).then_inc(sem["mixer_squares"], 1)
                dve.wait_ge(sem["mixer_squares"], 1)
                dve.wait_ge(sem["mixer_norm_mm"], 1)
                rsqrt(rr[:, :], PS[:, 3, 0:T], 256)
                for k in range(2):
                    c(stt(mT[:, 6 + k, :], D.y[:, k, :], vec[:, 84 + k:85 + k], rr[:, :], M_, M_))

            def queries(q, qz, b, name):
                for k in range(2):
                    i = V.tensor_copy(q[:, k, 16 * k:16 * k + 16].rearrange("p (h i) -> p h i", h=2),
                                      qz[:, 2 * k:2 * k + 2, bass.ds(SEQ + b * 8, 8)])
                    if k == 0:
                        c(i)
                    else:
                        i.then_inc(sem[name], 1)

            def seq_step(b):
                Q = seq

                def copy_keys(n):
                    k, g = divmod(n, NG)
                    dve.wait_ge(sem["c_keys_turned"], n + 1)
                    V.tensor_copy(Q.kcT[:, k, g * NC:(g + 1) * NC].rearrange("p (q e) -> p e q", e=NU),
                                  PS[:, 1 + n % 5, :].rearrange("p (j q) -> p j q", j=NU)).then_inc(sem["c_keys_copied_dve"], 1)

                queries(Q.qA, qzA, b, "a_queries")
                queries(Q.qC, qzC, b, "c_queries")
                for half in range(2):
                    dve.wait_ge(sem["a_keys_turned"], 2 + 2 * half)
                    V.tensor_copy(v3(Q.kaT[:, 0, :], 2 * half * NA, 2, NA), PS[:, 2 * half:2 + 2 * half, 0:NA]).then_inc(sem["a_keys_copied_dve"], 1)
                dve.wait_ge(sem["a_scores_mm"], 1)
                main, new = K("cap_sa"), K("cap_na")[:, bass.ds(b * NS, NS)]
                c(tt(Q.sa[:, 0:NA], PS[:, 0, 0:NA], main, ALU.min))
                c(tt(Q.sa[:, NA:NA + NS], PS[:, 0, NA:NA + NS], new, ALU.min))
                c(V.tensor_reduce(sm[:, 24:25], Q.sa, AX.X, ALU.max))
                ts(Q.gmax, K("in_group"), sm[:, 24:25], None, M_).then_inc(sem["a_group_max"], 1)
                for n in (1, 3):
                    copy_keys(n)
                dve.wait_ge(sem["a_max_mm"], 1)
                dve.wait_ge(sem["a_group_max"], 1)
                c(V.tensor_reduce(sm[:, 24:25], PS[:, 0, 384:384 + NG], AX.X, ALU.max))
                ts(sm[:, 24:25], sm[:, 24:25], -HD ** -0.5, None, M_).then_inc(sem["a_max"], 1)
                copy_keys(5)
                dve.wait_ge(sem["a_exp"], 1)
                stt(Q.sa[:, 0:NA], main, 1.0 / BIG_F, Q.sa[:, 0:NA], M_, M_)
                stt(Q.sa[:, NA:NA + NS], new, 1.0 / BIG_F, Q.sa[:, NA:NA + NS], M_, M_).then_inc(sem["a_probs"], 1)
                copy_keys(7)
                dve.wait_ge(sem["a_probs"], 1)
                V.tensor_reduce(sm[:, 25:26], Q.sa, AX.X, ALU.add).then_inc(sem["a_sums"], 1)
                dve.wait_ge(sem["a_sums_mm"], 1)
                c(V.reciprocal(sm[:, 26:27], PS[:, 0, 388:389]))
                dve.wait_ge(sem["c_logits"], 1)
                x = Q.s[:, NC:NC + NS]
                c(tt(x, x, K("cap_nc")[:, bass.ds(b * NS, NS)], ALU.min))
                stt(Q.t, Q.s, -1.0, Q.s, M_, ALU.max).then_inc(sem["c_abs"], 1)
                dve.wait_ge(sem["a_rows_mm"], 1)
                ts(Q.o, PS[:, 7, 0:256], sm[:, 26:27], None, M_).then_inc(sem["a_rows_scaled"], 1)
                dve.wait_ge(sem["c_log"], 1)
                c(stt(Q.t, Q.s, 0.0, Q.t, ALU.max, A_))
                x = Q.t[:, ::-1]
                V.tensor_tensor_scan(x, K("ones1").to_broadcast([128, NC + NS]), x, 0.0, M_, A_).then_inc(sem["c_sums"], 1)
                dve.wait_ge(sem["c_sums"], 1)
                c(tt(Q.s, Q.s, Q.t, S_))
                dve.wait_ge(sem["c_later_mm"], 1)
                V.tensor_copy(sm[:, 27:28], PS[:, 2, 64:65]).then_inc(sem["c_exponents"], 1)
                dve.wait_ge(sem["a_out_mm"], 1)
                dve.wait_ge(sem["c_rows_mm"], 1)
                V.tensor_copy(Q.o, PS[:, 5, 0:256]).then_inc(sem["c_rows_copied"], 1)

            def stage_out():
                c(V.memset(moe.y, 0.0))
                c(V.memset(moe.L, 0.0))
                tmp = rr[:, 0:64].rearrange("p (b i) -> p b i", b=DB)
                for k in range(8):
                    dve.wait_ge(sem["proj_mm"], k + 1)
                    o = PS[:, 4 + k % 4, 0:T]
                    c(stt(xT[:, k, 0:SEQ], o[:, 0:SEQ], modT[:, 16 + k, 0:1], xT[:, k, 0:SEQ], M_, A_))
                    c(tt(tmp, o[:, SEQ:T].rearrange("p (b i) -> p b i", b=DB), spread(modT[:, 16 + k, 1:9], 2, 8), M_))
                    tt(xT[:, k, SEQ:T], xT[:, k, SEQ:T], rr[:, 0:64], A_).then_inc(sem["proj_ev"], 1)
                    dve.wait_ge(sem["proj_ev"], k + 1)
                norm(56, 24)
                Mo = moe
                dve.wait_ge(sem["router_mm"], 1)
                for n, t in ((128, slice(0, 2)), (64, slice(2, 3))):
                    k = t.stop - t.start
                    c(tt(Mo.L[0:n, t, :], PS[0:n, 2, 36 * t.start:36 * t.stop].rearrange("p (t n) -> p t n", n=36),
                         spread(bc[0:n, 16:52], 1, k), A_))
                gl, el = Mo.L[:, :, 0:4], Mo.L[:, :, 4:36].rearrange("p t (g e) -> p t g e", g=4)

                def first_max(values, mx, hot, n):
                    tmp = Mo.tmp[:, :, 0:n]
                    c(V.tensor_reduce(mx, values, AX.X, ALU.max))
                    c(tt(tmp, values, spread(mx, 2, n), ALU.is_equal))
                    c(tt(tmp, tmp, spread(K("rev")[:, 0:n], 1, 3), M_))
                    c(V.tensor_reduce(Mo.km, tmp, AX.X, ALU.max))
                    c(tt(hot, tmp, spread(Mo.km, 2, n), ALU.is_equal))

                first_max(gl, Mo.gmax, Mo.ghot, 4)
                tt(Mo.gx, gl, spread(Mo.gmax, 2, 4), S_).then_inc(sem["group_args"], 1)
                dve.wait_ge(sem["group_args"], 1)
                c(tt(Mo.gt4, el, spread(Mo.ghot, 3, 8), M_))
                c(V.tensor_reduce(Mo.e8, Mo.gt4.rearrange("p t g e -> p t e g"), AX.X, ALU.add))
                first_max(Mo.e8, Mo.m1, Mo.h1, 8)
                c(stt(Mo.e8, Mo.h1, NEG, Mo.e8, M_, A_))
                first_max(Mo.e8, Mo.m2, Mo.h2, 8)
                tt(Mo.dx, Mo.m2, Mo.m1, S_).then_inc(sem["pair_args"], 1)
                dve.wait_ge(sem["pair_args"], 1)
                dve.wait_ge(sem["group_exps"], 1)
                c(V.tensor_reduce(Mo.gp, Mo.gx, AX.X, ALU.add))
                dve.wait_ge(sem["pair_exps"], 1)
                c(ts(Mo.m1, Mo.dx, 1.0, None, A_))
                c(tt(Mo.m1, Mo.m1, Mo.gp, M_))
                c(V.reciprocal(Mo.m1, Mo.m1))
                c(tt(Mo.m2, Mo.m1, Mo.dx, M_))
                c(tt(Mo.h1, Mo.h1, spread(Mo.m1, 2, 8), M_))
                c(tt(Mo.h2, Mo.h2, spread(Mo.m2, 2, 8), M_))
                c(tt(Mo.h1, Mo.h1, Mo.h2, A_))
                tt(Mo.gt4, spread(Mo.ghot, 3, 8), spread(Mo.h1, 2, 4), M_).then_inc(sem["gates_done"], 1)
                dve.wait_ge(sem["gates_done"], 1)
                step(dve, ts(Mo.sel, Mo.gt, 0.0, None, ALU.is_gt))
                V.tensor_copy(Mo.selc, Mo.sel).then_inc(sem["selected"], 1)
                dve.wait_ge(sem["gates_turned"], 1)
                c(V.tensor_copy(Mo.gT[0:32, :], PS[0:32, 3, 0:T]))
                dve.wait_ge(sem["ranks_mm"], 1)
                c(ts(Mo.rank, Mo.selc, -1000.0, 1000.0, M_, A_))
                for n, t in ((128, slice(0, 2)), (64, slice(2, 3))):
                    c(tt(Mo.rank[0:n, t, :], Mo.rank[0:n, t, :],
                         PS[0:n, 4, 32 * t.start:32 * t.stop].rearrange("p (t n) -> p t n", n=32), A_))
                c(V.tensor_reduce(Mo.km[:, 0:1], PS[:, 4, 96:128], AX.X, ALU.max))
                c(ts(Mo.km[:, 0:1], Mo.km[:, 0:1], float(SLOTS), None, ALU.is_gt))
                c(V.tensor_copy(crowded[:, :], Mo.km[:, 0:1]))

            def picks(at):
                for n, tiles in ((128, (0, 1)), (64, (2,))):
                    for j in tiles:
                        rank = moe.rank[0:n, j, bass.ds(at, GE)]
                        i = tt(moe.pick[0:n, j, :].rearrange("p (e s) -> p e s", e=GE), spread(K("iota")[0:n], 1, GE), spread(rank, 2, SLOTS), ALU.is_equal)
                        if j < 2:
                            c(i)
                i.then_inc(sem["picks"], 1)

            def slot_sums():
                for d in range(8):
                    dve.wait_ge(sem["slot_sum_mm"], d + 1)
                    tt(moe.y[:, d, :], moe.y[:, d, :], PS[:, 6 + d % 2, 0:T], A_).then_inc(sem["down_added"], 1)

            def group(it, prev, more):
                Mo = moe
                for j, (t0, n) in enumerate(SPANS):
                    gate = Mo.gt[0:n, j, bass.ds(it * GE, GE)]
                    i = tt(Mo.wpick[0:n, j, :].rearrange("p (e s) -> p e s", e=GE), Mo.pick[0:n, j, :].rearrange("p (e s) -> p e s", e=GE),
                           spread(gate, 2, SLOTS), M_)
                    if j < 2:
                        c(i)
                i.then_inc(sem["weighted_picks"], 1)
                if more:
                    dve.wait_ge(sem["weighted_picks"], 1)
                    picks(it * GE + GE)
                if prev:
                    slot_sums()
                for pair, n_up in enumerate((2, 4)):
                    dve.wait_ge(sem["gate_act"], pair + 1)
                    dve.wait_ge(sem["pair_mm"], n_up)
                    tt(Mo.hid[:, pair, :], Mo.silu[:, pair, :], PS[:, 2 * pair + 1, :], M_).then_inc(sem["hidden"], 1)

            def dense_group(it):
                Mo = moe
                for u in range(GE):
                    if u:
                        dve.wait_ge(sem["gate_mm"], u)
                    ts(Mo.gm[0:32, :], Mo.gT[0:32, :], ident[0:32, bass.ds(it * GE + u, 1)], None, M_).then_inc(sem["gate_row"], 1)
                    dve.wait_ge(sem["gate_copied"], u + 1)
                    for ff in range(4):
                        e = Mo.e[:, ff % 2, :]
                        dve.wait_ge(sem["gate_act"], 4 * u + ff + 1)
                        c(tt(e, e, PS[:, 2 + ff % 2, 0:T], M_))
                        tt(Mo.a[:, 4 * u + ff, :], e, Mo.gb, M_).then_inc(sem["hidden"], 1)
                        dve.wait_ge(sem["hidden"], 4 * u + ff + 1)
                for u in range(GE):
                    for d in range(8):
                        dve.wait_ge(sem["down_mm"], 8 * u + d + 1)
                        tt(Mo.y[:, d, :], Mo.y[:, d, :], PS[:, 4 + d % 4, 0:T], A_).then_inc(sem["down_added"], 1)

            def add_moe():
                y = moe.y
                c(tt(y[:, :, 0:SEQ], y[:, :, 0:SEQ], modT[:, 40:48, 0:1].to_broadcast([128, 8, SEQ]), M_))
                ys = y[:, :, SEQ:T].rearrange("p k (b i) -> p k b i", b=DB)
                c(tt(ys, ys, spread(modT[:, 40:48, 1:9], 3, 8), M_))
                c(tt(xT, xT, y, A_))

            def final():
                dve.wait_ge(sem["rms_mm"], 1)
                rsqrt(rr[:, :], PS[:, 1, 0:T], DM)
                c(tt(mT, xT, spread(rr[:, :], 1, KT8), M_))
                tt(mT, mT, spread(gfin[:, :], 2, T), M_).then_inc(sem["h_done"], 1)
                dve.wait_ge(sem["h_done"], 1)

            pre()
            barrier(dve)
            with dve.Fori(0, DEPTH) as l:
                stage_a()
                barrier(dve)
                stage_b()
                barrier(dve)
                stage_gla(l)
                barrier(dve)
                stage_ssd()
                barrier(dve)
                with dve.Fori(0, DB) as b:
                    seq_step(b)
                    barrier(dve)
                stage_out()
                barrier(dve)
                many = dve.value_load(crowded[0:1, 0:1], min_val=0, max_val=1)
                with dve.If(many > 0):
                    barrier(dve)
                    with dve.Fori(0, NE // 4) as it:
                        dense_group(it)
                        barrier(dve)
                with dve.Else():
                    picks(0)
                    barrier(dve)
                    group(0, False, True)
                    barrier(dve)
                    with dve.Fori(1, NE // GE - 1) as it:
                        group(it, True, True)
                        barrier(dve)
                    group(NE // GE - 1, True, False)
                    barrier(dve)
                    slot_sums()
                    dve.wait_ge(sem["down_added"], 8)
                add_moe()
                barrier(dve)
            final()
            barrier(dve)

        @block.gpsimd
        def _(pool):
            own[pool] = [sem["pool_step"], 0]
            def dma(out, in_, sem):
                pool.dma_start(out, in_).then_inc(sem, 16)

            def pre():
                dma(cst[:, :], consts, loads)
                rows = v3(big, 0, 3, 1024)
                dma(rows[:, 0:2, :], x_rows[0:256].rearrange("(t p) c -> p t c", p=128), loads)
                dma(rows[0:64, 2, :], x_rows[256:T], loads)
                dma(big[0:9, 4096:5120], c_rows, loads)
                dma(big[0:8, 5120:5248], g_final.rearrange("(k p) -> k p", p=128), loads)
                for u in range(NG):
                    src = pages.rearrange("b (g u) -> u (b g)", u=4)[u:u + 1, :]
                    pool.dma_start(idxi[32 * u:32 * u + 32, :], src.to_broadcast([32, NG * DB]), allow_slow_non_contiguous=True).then_inc(loads, 16)
                pool.wait_ge(loads, LOADS_PRE)

            def stage_a(l):
                dma(vrow[0:NVEC, :], vecs[l], loads)
                dma(bc[:, :], bcs[bass.ds(l, 1), :].to_broadcast([128, 52]), loads)
                dma(wtail, w_tail[l].rearrange("(k p) n -> p k n", p=128), loads)
                dma(wr, w_router[l].rearrange("(k p) n -> p k n", p=128), loads)
                dma(wa2[0:16, :], w_a2[l], loads)
                dma(big[0:24, SCR + 2560:SCR + 3072], st_conv[l].rearrange("b k c -> (b k) c"), loads)
                pool.wait_ge(loads, l * LOADS + LOADS_PRE + LOADS_A)

            def stage_b(l):
                pool.wait_ge(sem["tail27_ev"], 1)
                dma(cv_p[l, 0], cvo[0:3, :], outputs)
                dma(cv_s[l].rearrange("b k c -> (b k) c"), cvo[3:27, :], outputs)
                for n, (buf, op, os) in enumerate(((kA, wk_p, wk_s), (vA, wv_p, wv_s), (None, None, None), (kC, sk_p, sk_s), (vC, sv_p, sv_s))):
                    if buf is None:
                        continue
                    pool.wait_ge(sem["tok_ev"], n + 1)
                    dma(op[l].rearrange("(t p) c -> p t c", p=128), buf[:, 0:2, :], outputs)
                    dma(os[l], buf[0:64, 2, :], outputs)
                pool.wait_ge(outputs, l * OUTS + OUTS_B)

            def stage_gla(l):
                G = gla
                dma(G.raw, st_gla[l].rearrange("b h k v -> (h k) b v"), loads)
                pool.wait_ge(sem["gla_final_states"], 1)
                for h in range(4):
                    dma(gla_p[l, 0, h], G.stp[32 * h:32 * h + 32, 3, 64 * h:64 * h + 64], outputs)
                    dma(gla_s[l, :, h].rearrange("b k v -> k b v"), G.st0[32 * h:32 * h + 32, :, 64 * h:64 * h + 64], outputs)
                pool.wait_ge(outputs, l * OUTS + OUTS_B + OUTS_G)

            def stage_ssd(l):
                D = ssd
                for g in range(2):
                    dma(D.raw[:, :, 64 * g:64 * g + 64], st_ssm[l, :, 2 * g:2 * g + 2].rearrange("b h p n -> (h p) b n"), loads)
                pool.wait_ge(sem["ssm_out_copied"], 1)
                ob = D.outb.rearrange("p (j n) -> p j n", j=9)
                for g in range(2):
                    dma(ssm_p[l, 0, 2 * g:2 * g + 2].rearrange("h p n -> (h p) n"), ob[:, 0, 64 * g:64 * g + 64], outputs)
                    dma(ssm_s[l, :, 2 * g:2 * g + 2].rearrange("b h p n -> (h p) b n"), ob[:, 1:9, 64 * g:64 * g + 64], outputs)
                pool.wait_ge(outputs, l * OUTS + OUTS)

            def gather(cache, to, at, sem):
                for g in range(NG):
                    pool.indirect_dma_start(out=to[:, g, :, :].rearrange("p a b -> p (a b)"), out_offset=None, in_=cache,
                                            in_offset=bass.IndirectOffsetOnAxis(ap=idxb[:, at + g:at + g + 1], axis=0)).then_inc(sem, 16)

            def first_keys():
                nc.gpsimd.tensor_copy(idxb[:, NG:2 * NG], idxu[:, 0:NG]).then_inc(sem["first_indices"], 1)
                pool.wait_ge(sem["first_indices"], 1)
                gather(sb_k, seq.kc, NG, gathered_k)

            def seq_values(b):
                step(pool, nc.gpsimd.tensor_copy(idxb[:, 0:NG], idxu[:, bass.ds(b * NG, NG)]))
                gather(sb_v, seq.vc, 0, gathered_v)

            def next_keys(b):
                pool.wait_ge(sem["c_keys_turned"], 2 * NG)
                step(pool, nc.gpsimd.tensor_copy(idxb[:, NG:2 * NG], idxu[:, bass.ds(b * NG + NG, NG)]))
                gather(sb_k, seq.kc, NG, gathered_k)

            def final():
                pool.wait_ge(sem["rows_copied"], 1)
                rows = v3(big, 0, 3, 1024)
                dma(y_p.rearrange("(t p) c -> p t c", p=128), rows[:, 0:2, :], outputs)
                dma(y_s, rows[0:64, 2, :], outputs)
                pool.wait_ge(outputs, DEPTH * OUTS + 32)

            pre()
            barrier_lead(pool)
            with pool.Fori(0, DEPTH) as l:
                for stage in (stage_a, stage_b, stage_gla, stage_ssd):
                    stage(l)
                    barrier_lead(pool)
                first_keys()
                with pool.Fori(0, DB - 1) as b:
                    seq_values(b)
                    next_keys(b)
                    barrier_lead(pool)
                seq_values(DB - 1)
                barrier_lead(pool)
                barrier_lead(pool)
                barrier_lead(pool)
                with pool.Fori(0, NE // 4):
                    barrier_lead(pool)
                barrier_lead(pool)
            final()
            barrier_lead(pool)


def kernel(x_prompt, x_sample, cache_win_k, cache_win_v, cache_sb_k, cache_sb_v, state_gla, state_ssm, state_conv,
           page_table, c_prompt, c_sample, w_ada, b_ada, g_norm1, g_norm2, w_in, w_gla_a2, b_gla_a, g_gla, b_sb,
           w_conv, b_conv, dt_bias, a_log, d_skip, g_ssm, w_out, w_router_grp, b_router_grp, w_router_exp,
           b_router_exp, w_exp_gate, w_exp_up, w_exp_down, g_final):
    import concourse.bacc as bacc
    from concourse.bass_utils import run_bass_kernel_spmd

    a = {k: np.asarray(v) for k, v in locals().items() if k not in ("bacc", "run_bass_kernel_spmd")}
    L = DEPTH
    cols = np.split(a["w_in"], np.cumsum([256, 256, 256, 128, 128, 256, 16, 256, 256, 256, 256, 256, 512])[:13].tolist(), axis=-1)
    aq, ak, av, bq, bk, bv, lr, gate, cq, ck, cv, z, xbc, dt = cols
    vec = np.concatenate([a["b_ada"], a["g_norm1"], a["g_norm2"], a["w_conv"].reshape(L, -1), a["b_conv"], a["g_ssm"],
                          a["b_gla_a"], a["g_gla"], a["g_gla"]], axis=-1).reshape(L, NVEC, 128)
    ins = {
        "x_rows": np.concatenate([a["x_prompt"].reshape(-1, DM), a["x_sample"].reshape(-1, DM)]),
        "c_rows": np.concatenate([a["c_prompt"], a["c_sample"]]),
        "win_k": a["cache_win_k"].reshape(L, DB, PAST, 256), "win_v": a["cache_win_v"].reshape(L, DB, PAST, 256),
        "sb_k": a["cache_sb_k"].reshape(L * N_POOL * PAGE // NU, NU * 256), "sb_v": a["cache_sb_v"].reshape(L * N_POOL * PAGE // NU, NU * 256),
        "st_gla": a["state_gla"], "st_ssm": a["state_ssm"], "st_conv": a["state_conv"], "pages": a["page_table"],
        "w_ada": a["w_ada"], "vecs": vec,
        "w_in": np.concatenate([xbc, gate, z, aq, ak, av, bq, bk, bv, cq, ck, cv], axis=-1),
        "w_tail": np.concatenate([lr, dt], axis=-1), "w_a2": a["w_gla_a2"],
        "bcs": np.concatenate([a["b_sb"], a["dt_bias"], a["a_log"], a["d_skip"], a["b_router_grp"], a["b_router_exp"]], axis=-1),
        "w_out": a["w_out"],
        "w_router": np.concatenate([a["w_router_grp"], a["w_router_exp"]], axis=-1),
        "w_gate": a["w_exp_gate"], "w_up": a["w_exp_up"], "w_down": a["w_exp_down"], "g_final": a["g_final"],
        "consts": np.concatenate(list(CONST.values()), axis=1),
    }
    outs = [("y_p", (SEQ, DM)), ("y_s", (NS, DM)), ("wk_p", (L, SEQ, 256)), ("wv_p", (L, SEQ, 256)), ("wk_s", (L, NS, 256)),
            ("wv_s", (L, NS, 256)), ("sk_p", (L, SEQ, 256)), ("sv_p", (L, SEQ, 256)), ("sk_s", (L, NS, 256)),
            ("sv_s", (L, NS, 256)), ("gla_p", (L, 1, NH, 32, 64)), ("gla_s", (L, DB, NH, 32, 64)),
            ("ssm_p", (L, 1, NH, 64, 64)), ("ssm_s", (L, DB, NH, 64, 64)), ("cv_p", (L, 1, 3, CONV_CH)), ("cv_s", (L, DB, 3, CONV_CH))]
    nc = bacc.Bacc("TRN2", target_bir_lowering=False, num_devices=1)
    args, arrays = [], {}
    for name, x in ins.items():
        arrays["in_" + name] = np.ascontiguousarray(x)
        args.append(nc.dram_tensor("in_" + name, x.shape, mybir.dt.from_np(x.dtype), kind="ExternalInput").ap())
    for name, shape in outs:
        args.append(nc.dram_tensor("out_" + name, shape, F32, kind="ExternalOutput").ap())
    trunk(nc, *args)
    r = run_bass_kernel_spmd(nc, [arrays], core_ids=[0]).results[0]
    g = {n: r["out_" + n] for n, _ in outs}
    heads = (NH, HD)
    return (g["y_p"].reshape(1, SEQ, DM), g["y_s"].reshape(DB, DS, DM),
            g["wk_p"].reshape(L, 1, SEQ, *heads), g["wv_p"].reshape(L, 1, SEQ, *heads),
            g["wk_s"].reshape(L, DB, DS, *heads), g["wv_s"].reshape(L, DB, DS, *heads),
            g["sk_p"].reshape(L, 1, SEQ // PAGE, PAGE, *heads), g["sv_p"].reshape(L, 1, SEQ // PAGE, PAGE, *heads),
            g["sk_s"].reshape(L, DB, DS, *heads), g["sv_s"].reshape(L, DB, DS, *heads),
            g["gla_p"], g["gla_s"], g["ssm_p"], g["ssm_s"], g["cv_p"], g["cv_s"])
```
